# Optimizing a Trainium2 kernel written in Bass

```python
import math
import jax, jax.numpy as jnp
from jax import lax
import numpy as np

D_MODEL = 1024
BATCH = 1
SEQ = 1024
DEPTH = 1

RET_HEADS = 8
RET_QK = 64
RET_V = 64
RET_WIDTH = RET_HEADS * RET_V
DIFF_HEADS = 4
DIFF_QK = 64
DIFF_V = 2 * DIFF_QK
DIFF_WIDTH = DIFF_HEADS * DIFF_V
MIX_WIDTH = RET_WIDTH + DIFF_WIDTH
W_RQ = RET_HEADS * RET_QK
W_RK = RET_HEADS * RET_QK
W_RV = RET_WIDTH
W_RG = RET_WIDTH
W_DQ = DIFF_HEADS * 2 * DIFF_QK
W_DK = DIFF_HEADS * 2 * DIFF_QK
W_DV = DIFF_WIDTH
IN_WIDTH = W_RQ + W_RK + W_RV + W_RG + W_DQ + W_DK + W_DV
IN_SPLITS = (W_RQ, W_RQ + W_RK, W_RQ + W_RK + W_RV, W_RQ + W_RK + W_RV + W_RG,
             W_RQ + W_RK + W_RV + W_RG + W_DQ, W_RQ + W_RK + W_RV + W_RG + W_DQ + W_DK)
CHUNK = 128
Q_BLOCK = 128
ROPE_BASE = 10000.0
SUBLN_EPS = 1e-5
LN_EPS = 1e-5
N_EXPERTS = 16
N_GROUPS = 4
EXPERTS_PER_GROUP = N_EXPERTS // N_GROUPS
TOP_K = 2
D_EXPERT = 512
ALPHA = (2 * DEPTH) ** 0.25
BETA = (8 * DEPTH) ** -0.25
N_MOD = 6

kernel_name = 'hybrid_retention_diffattn_moe_deepnorm_adaln'

def _layer_norm(x, eps=LN_EPS):
    xf = x.astype(jnp.float32)
    mu = jnp.mean(xf, axis=-1, keepdims=True)
    var = jnp.mean(jnp.square(xf - mu), axis=-1, keepdims=True)
    return ((xf - mu) * lax.rsqrt(var + eps)).astype(x.dtype)

def _layer_norm_affine(x, g, b):
    return _layer_norm(x) * g + b

def _rms_norm(x, g, eps):
    xf = x.astype(jnp.float32)
    y = xf * lax.rsqrt(jnp.mean(jnp.square(xf), axis=-1, keepdims=True) + eps)
    return (y * g.astype(jnp.float32)).astype(x.dtype)

def _rotary(x, pos):
    d = x.shape[-1]
    inv = 1.0 / (ROPE_BASE ** (jnp.arange(0, d, 2, dtype=jnp.float32) / d))
    ang = pos.astype(jnp.float32)[:, None] * inv[None, :]
    cos = jnp.cos(ang)[None, :, None, :]
    sin = jnp.sin(ang)[None, :, None, :]
    xf = x.astype(jnp.float32)
    x1, x2 = xf[..., : d // 2], xf[..., d // 2:]
    return jnp.concatenate([x1 * cos - x2 * sin, x1 * sin + x2 * cos], axis=-1).astype(x.dtype)

def _retention(q, k, v):
    B, S, H, dk = q.shape
    dv = v.shape[-1]
    n = S // CHUNK
    log_g = jnp.log(1.0 - 2.0 ** (-5.0 - jnp.arange(H, dtype=jnp.float32)))
    idx = jnp.arange(CHUNK, dtype=jnp.float32)
    rel = idx[:, None] - idx[None, :]
    decay = jnp.where(rel >= 0, jnp.exp(log_g[:, None, None] * jnp.maximum(rel, 0.0)), 0.0)
    qc = q.reshape(B, n, CHUNK, H, dk) * (dk ** -0.5)
    kc = k.reshape(B, n, CHUNK, H, dk)
    vc = v.reshape(B, n, CHUNK, H, dv)
    scores = jnp.einsum('bnihd,bnjhd->bnhij', qc, kc) * decay[None, None]
    inner = jnp.einsum('bnhij,bnjhe->bnihe', scores, vc)
    k_decay = jnp.exp(log_g[None, :] * (CHUNK - 1 - idx)[:, None])
    chunk_kv = jnp.einsum('bnjhd,jh,bnjhe->nbhde', kc, k_decay, vc).astype(jnp.float32)
    g_chunk = jnp.exp(log_g * CHUNK)[None, :, None, None]

    def step(state, kv):
        return state * g_chunk + kv, state

    _, prev = lax.scan(step, jnp.zeros_like(chunk_kv[0]), chunk_kv)
    q_decay = jnp.exp(log_g[None, :] * (idx + 1.0)[:, None])
    cross = jnp.einsum('bnihd,nbhde,ih->bnihe', qc, prev, q_decay)
    return (inner + cross).reshape(B, S, H, dv).astype(v.dtype)

def _diff_attention(q, k, v, lam, subln_g, lambda_init):
    B, S, H, _, d = q.shape
    nb = S // Q_BLOCK
    qb = (q * (d ** -0.5)).reshape(B, nb, Q_BLOCK, H, 2, d).transpose(1, 0, 2, 3, 4, 5)
    kpos = jnp.arange(S)
    starts = jnp.arange(nb) * Q_BLOCK

    def block(args):
        qi, start = args
        s = jnp.einsum('bqhcd,bkhcd->bhcqk', qi, k).astype(jnp.float32)
        qpos = start + jnp.arange(Q_BLOCK)
        s = jnp.where((kpos[None, :] <= qpos[:, None])[None, None, None], s, -jnp.inf)
        p = jax.nn.softmax(s, axis=-1)
        a = p[:, :, 0] - lam * p[:, :, 1]
        return jnp.einsum('bhqk,bkhe->bqhe', a.astype(v.dtype), v)

    out = lax.map(block, (qb, starts))
    out = out.transpose(1, 0, 2, 3, 4).reshape(B, S, H, 2 * d)
    return _rms_norm(out, subln_g, SUBLN_EPS) * (1.0 - lambda_init)

def _moe(h, router_w, router_b, w_gate, w_up, w_down):
    B, S, D = h.shape
    t = h.reshape(B * S, D)
    logits = jnp.matmul(t, router_w).astype(jnp.float32) + router_b.astype(jnp.float32)
    probs = jax.nn.softmax(logits, axis=-1)
    grouped = probs.reshape(-1, N_GROUPS, EXPERTS_PER_GROUP)
    top_in_group, _ = lax.top_k(grouped, TOP_K)
    _, g_idx = lax.top_k(jnp.sum(top_in_group, axis=-1), 1)
    sel = jnp.einsum('tg,tge->te', jax.nn.one_hot(g_idx[:, 0], N_GROUPS, dtype=jnp.float32), grouped)
    top_p, top_i = lax.top_k(sel, TOP_K)
    gates = top_p / jnp.sum(top_p, axis=-1, keepdims=True)
    expert_idx = g_idx * EXPERTS_PER_GROUP + top_i
    combine = jnp.einsum('tk,tke->te', gates, jax.nn.one_hot(expert_idx, N_EXPERTS, dtype=jnp.float32))
    combine = combine.astype(t.dtype)
    out = jnp.zeros_like(t)
    for e in range(N_EXPERTS):
        he = jax.nn.silu(jnp.matmul(t, w_gate[e])) * jnp.matmul(t, w_up[e])
        out = out + combine[:, e:e + 1] * jnp.matmul(he, w_down[e])
    return out.reshape(B, S, D)

def setup_inputs(seed: int = 0) -> dict:
    key = jax.random.key(seed)
    ks = jax.random.split(key, 20)
    f32 = jnp.float32
    D = D_MODEL
    x = jax.random.normal(ks[0], (BATCH, SEQ, D), f32)
    c = jax.random.normal(ks[1], (BATCH, D), f32)
    w_ada = jax.random.normal(ks[2], (DEPTH, D, N_MOD * D), f32) * (0.2 * D ** -0.5)
    gate_offset = jnp.repeat(jnp.array([0.0, 0.0, 1.0, 0.0, 0.0, 1.0], f32), D)
    b_ada = 0.01 * jax.random.normal(ks[3], (DEPTH, N_MOD * D), f32) + gate_offset[None, :]
    col_scale = jnp.concatenate([
        jnp.ones((W_RQ + W_RK,), f32), jnp.full((W_RV,), BETA, f32), jnp.ones((W_RG + W_DQ + W_DK,), f32),
        jnp.full((W_DV,), BETA, f32)])
    w_in = jax.random.normal(ks[4], (DEPTH, D, IN_WIDTH), f32) * (D ** -0.5) * col_scale[None, None, :]
    w_out = jax.random.normal(ks[5], (DEPTH, MIX_WIDTH, D), f32) * (MIX_WIDTH ** -0.5) * BETA
    lambda_q1 = 0.1 * jax.random.normal(ks[6], (DEPTH, DIFF_QK), f32)
    lambda_k1 = 0.1 * jax.random.normal(ks[7], (DEPTH, DIFF_QK), f32)
    lambda_q2 = 0.1 * jax.random.normal(ks[8], (DEPTH, DIFF_QK), f32)
    lambda_k2 = 0.1 * jax.random.normal(ks[9], (DEPTH, DIFF_QK), f32)
    diff_subln = 1.0 + 0.02 * jax.random.normal(ks[10], (DEPTH, DIFF_V), f32)
    ln_mix_g = 1.0 + 0.02 * jax.random.normal(ks[11], (DEPTH, D), f32)
    ln_mix_b = 0.02 * jax.random.normal(ks[12], (DEPTH, D), f32)
    ln_ffn_g = 1.0 + 0.02 * jax.random.normal(ks[13], (DEPTH, D), f32)
    ln_ffn_b = 0.02 * jax.random.normal(ks[14], (DEPTH, D), f32)
    router_w = jax.random.normal(ks[15], (D, N_EXPERTS), f32) * (D ** -0.5)
    router_b = 0.01 * jax.random.normal(ks[16], (N_EXPERTS,), f32)
    w_gate = jax.random.normal(ks[17], (DEPTH, N_EXPERTS, D, D_EXPERT), f32) * (D ** -0.5) * BETA
    w_up = jax.random.normal(ks[18], (DEPTH, N_EXPERTS, D, D_EXPERT), f32) * (D ** -0.5) * BETA
    w_down = jax.random.normal(ks[19], (DEPTH, N_EXPERTS, D_EXPERT, D), f32) * (D_EXPERT ** -0.5) * BETA
    return {'x': x, 'c': c, 'w_ada': w_ada, 'b_ada': b_ada, 'w_in': w_in, 'w_out': w_out,
            'lambda_q1': lambda_q1, 'lambda_k1': lambda_k1, 'lambda_q2': lambda_q2, 'lambda_k2': lambda_k2,
            'diff_subln': diff_subln, 'ln_mix_g': ln_mix_g, 'ln_mix_b': ln_mix_b,
            'ln_ffn_g': ln_ffn_g, 'ln_ffn_b': ln_ffn_b, 'router_w': router_w, 'router_b': router_b,
            'w_gate': w_gate, 'w_up': w_up, 'w_down': w_down}

def reference(x, c, w_ada, b_ada, w_in, w_out, lambda_q1, lambda_k1, lambda_q2, lambda_k2,
              diff_subln, ln_mix_g, ln_mix_b, ln_ffn_g, ln_ffn_b, router_w, router_b,
              w_gate, w_up, w_down):
    B, S, D = x.shape
    pos = jnp.arange(S)
    cond = jax.nn.silu(c)
    for l in range(DEPTH):
        mod = jnp.matmul(cond, w_ada[l]) + b_ada[l]
        sh1, sc1, g1, sh2, sc2, g2 = jnp.split(mod, N_MOD, axis=-1)
        h = _layer_norm(x) * (1.0 + sc1[:, None, :]) + sh1[:, None, :]
        proj = jnp.matmul(h, w_in[l])
        rq, rk, rv, rg, dq, dk, dv = jnp.split(proj, IN_SPLITS, axis=-1)
        rq = _rotary(rq.reshape(B, S, RET_HEADS, RET_QK), pos)
        rk = _rotary(rk.reshape(B, S, RET_HEADS, RET_QK), pos)
        ret = _retention(rq, rk, rv.reshape(B, S, RET_HEADS, RET_V))
        ret = _layer_norm(ret).reshape(B, S, RET_WIDTH) * jax.nn.silu(rg)
        lambda_init = 0.8 - 0.6 * math.exp(-0.3 * l)
        lam = (jnp.exp(jnp.sum(lambda_q1[l].astype(jnp.float32) * lambda_k1[l].astype(jnp.float32)))
               - jnp.exp(jnp.sum(lambda_q2[l].astype(jnp.float32) * lambda_k2[l].astype(jnp.float32)))
               + lambda_init)
        dif = _diff_attention(dq.reshape(B, S, DIFF_HEADS, 2, DIFF_QK),
                              dk.reshape(B, S, DIFF_HEADS, 2, DIFF_QK),
                              dv.reshape(B, S, DIFF_HEADS, DIFF_V),
                              lam, diff_subln[l], lambda_init).reshape(B, S, DIFF_WIDTH)
        mixed = jnp.matmul(jnp.concatenate([ret, dif], axis=-1), w_out[l])
        x = _layer_norm_affine(ALPHA * x + g1[:, None, :] * mixed, ln_mix_g[l], ln_mix_b[l])
        h = _layer_norm(x) * (1.0 + sc2[:, None, :]) + sh2[:, None, :]
        y = _moe(h, router_w, router_b, w_gate[l], w_up[l], w_down[l])
        x = _layer_norm_affine(ALPHA * x + g2[:, None, :] * y, ln_ffn_g[l], ln_ffn_b[l])
    return x


_drawn_inputs = setup_inputs


def setup_inputs(seed=0):
    import zlib

    import numpy as np

    out = dict(_drawn_inputs(seed))
    spreads = {}
    factors = {'lambda_q1': 186.392,
     'lambda_k1': 3.196,
     'lambda_k2': 200.0,
     'diff_subln': 12.289,
     'ln_ffn_g': 20.308,
     'ln_ffn_b': 21.486,
     'router_b': 18.727,
     'ln_mix_b': 2.698}
    for name, (base, spread) in spreads.items():
        noise = np.random.default_rng([zlib.crc32(name.encode()), seed]).standard_normal(out[name].shape)
        drawn = base * np.exp(spread * noise) if base else spread * noise
        out[name] = __import__('jax').numpy.asarray(drawn.astype(out[name].dtype))
    for name, factor in factors.items():
        out[name] = (out[name] * factor).astype(out[name].dtype)
    return out
```

```python
import math
from contextlib import ExitStack

import concourse.bass as bass
from concourse import mybir

P = 128
D = 1024
S = 1024
NT = S // P
KC = D // P
H = 512
RET_H, DH = 8, 64
PAIRS = RET_H // 2
DIFF_H = 4
NE, NG, EPG = 16, 4, 4
DE = 512
FK = DE // P
MAX_TILES = (2 * S + NE * (P - 1)) // P
IDX_TILES = MAX_TILES + 1
assert IDX_TILES == 1 << 5 and P == 1 << 7
ALPHA = 2.0 ** 0.25
YBUF = 4
EPS = 1e-5
NEG = -1e30
BIG = 8192.0
LAMBDA_INIT = 0.8 - 0.6 * math.exp(0.0)

CONST_PARTS = [("ident", P), ("causal", P), ("neg_mask", P), ("before", P), ("cos", NT * 32), ("sin", NT * 32),
               ("v_decay", RET_H), ("q_decay", RET_H), ("chunk_decay", PAIRS), ("lower", EPG * EPG), ("steps", NT - 1)]
CONST_AT = {}
_at = 0
for _n, _w in CONST_PARTS:
    CONST_AT[_n] = (_at, _at + _w)
    _at += _w
CONST_W = _at

RING = 3
RQ, RK, RV, RG, DQ, DK, DV = range(7)
BLOCKS = [("ada", 0), ("ada", 1), ("ada", 2), ("ada", 3), ("in", RQ), ("in", RK), ("ada", 6), ("in", RV), ("ada", 7),
          ("in", RG), ("ada", 8), ("in", DV), ("ada", 9), ("in", DQ), ("ada", 4), ("in", DK), ("ada", 5), ("ada", 10),
          ("ada", 11), ("out", 0), ("out", 1)]
ADA_ORDER = [b for k, b in BLOCKS if k == "ada"]


PROJ_ORDER = [b for k, b in BLOCKS if k == "in"]


def slot_use(kind, b):
    n = BLOCKS.index((kind, b))
    return n % RING, n // RING + 1


def build(nc, x, c, w_ada, b_ada, w_in, w_out, lq1, lk1, lq2, lk2, subln, mix_g, mix_b, ffn_g, ffn_b, router_w,
          router_b, w_gate, w_up, w_down, consts, token_ids, out):
    f32, i32 = mybir.dt.float32, mybir.dt.int32
    ALU, ACT, AX = mybir.AluOpType, mybir.ActivationFunctionType, mybir.AxisListType

    z_rows = nc.dram_tensor("z_rows", (S, D), f32)
    slot_ids = nc.dram_tensor("slot_ids", (IDX_TILES * P, 1), i32)
    y_rows = nc.dram_tensor("y_rows", (MAX_TILES * P, D), f32)

    w_ada_v = w_ada[0].rearrange("(p k) n -> p k n", k=KC)
    w_in_v = w_in[0].rearrange("(k p) n -> p k n", p=P)
    w_out_v = w_out[0].rearrange("(k p) n -> p k n", p=P)
    x_v = x[0].rearrange("(t p) d -> p t d", p=P)
    out_v = out[0].rearrange("(t p) d -> p t d", p=P)

    with ExitStack() as ctx:
        def sb(name, shape, dt=f32):
            return ctx.enter_context(nc.sbuf_tensor(name, shape, dt))

        def sem(name):
            return ctx.enter_context(nc.semaphore(name))

        ring = [sb(f"ring{i}", [P, KC, H]) for i in range(RING)]
        A = sb("region_a", [P, 8192])
        B = sb("region_b", [P, 8192])
        C = sb("region_c", [P, 8192])
        M = sb("region_m", [P, 8192])
        V = sb("region_v", [P, 4096])
        cst = sb("cst", [P, CONST_W])
        ones = sb("ones", [P, P])
        g2b = sb("g2b", [P, D])
        b12 = sb("b12", [12, H])
        modcol = sb("modcol", [P, 4, KC])
        rw = sb("rw", [P, KC, NE])
        small = sb("small", [P, 224])
        ts_i = sb("ts_i", [1, NE + 1], i32)

        def const(name):
            a, b = CONST_AT[name]
            return cst[:, a:b]

        ident = const("ident")
        cos_t = const("cos").rearrange("p (t a) -> p t a", t=NT)
        sin_t = const("sin").rearrange("p (t a) -> p t a", t=NT)

        hT = A[:].rearrange("p (k s) -> p k s", k=KC)
        probs = A[:, 0:4096].rearrange("p (b c n) -> p b c n", b=2, c=2)
        aT = A[:, 4096:6144].rearrange("p (b n) -> p b n", b=2)
        x1 = A[:].rearrange("p (t d) -> p t d", t=NT)
        xn = B[:].rearrange("p (t d) -> p t d", t=NT)
        rqT = B[:, 0:4096].rearrange("p (c s) -> p c s", c=PAIRS)
        rkT = B[:, 4096:8192].rearrange("p (c s) -> p c s", c=PAIRS)
        dkT = rkT
        rk = C[:, 0:4096].rearrange("p (t n) -> p t n", t=NT)
        vs = C[:, 4096:8192].rearrange("p (t n) -> p t n", t=NT)
        g1b = C[:, 0:1024]
        dqT = [rqT, C[:, 1024:5120].rearrange("p (c s) -> p c s", c=DIFF_H)]
        xr = C[:, 1024:3072].rearrange("p (b d) -> p b d", b=2)
        u = C[:, 3072:5120].rearrange("p (b d) -> p b d", b=2)
        z = C[:, 5120:7168].rearrange("p (b d) -> p b d", b=2)
        mixT = [a.rearrange("p (k n) -> p k n", k=KC) for a in (C[:, 7168:8192], V[:, 3072:4096])]
        xg = C[:, 0:1024]
        hgT = C[:, 1024:2048].rearrange("p (k n) -> p k n", k=KC)
        sg = C[:, 2048:2560]
        he = C[:, 2560:3072]
        heT = C[:, 3072:3584].rearrange("p (k n) -> p k n", k=FK)
        yb = C[:, 3584:4608]
        idx_all = C[:, 4608:4608 + IDX_TILES].bitcast(i32)
        idx_cur = C[:, 4672:4673].bitcast(i32)
        tok_i = C[:, 4680:4680 + NT].bitcast(i32)
        rt = C[:, 4736:8192]
        ygath = B[:].rearrange("p (b j d) -> p b j d", b=YBUF, j=2)
        fin = M[:, 4096:8192].rearrange("p (b d) -> p b d", b=YBUF)
        ret_out = M[:, 0:4096].rearrange("p (t n) -> p t n", t=NT)
        dif_out = M[:, 4096:8192].rearrange("p (t n) -> p t n", t=NT)
        t1 = M[:, 4096:4608]
        t2 = M[:, 4608:5120]
        qrot = M[:, 5120:6144].rearrange("p (b n) -> p b n", b=2)
        pm = M[:, 6144:7168].rearrange("p (r c n) -> p r c n", r=2, c=PAIRS)
        state = M[:, 7168:7424].rearrange("p (c e) -> p c e", c=PAIRS)
        state_new = M[:, 7424:7680].rearrange("p (c e) -> p c e", c=PAIRS)
        lamv = M[:, 7680:7936].rearrange("p (v n) -> p v n", v=4)
        dv = V[:].rearrange("p (t n) -> p t n", t=NT)
        ln_g, ln_b = V[:, 0:1024], V[:, 1024:2048]
        h2T = V[:, 2048:3072].rearrange("p (k n) -> p k n", k=KC)

        def cols(a, n):
            return small[:, a:a + n]

        eps_c = cols(0, 1)
        cond = cols(1, KC)
        craw = cols(9, KC)
        nlam = cols(17, 1)
        lam4 = cols(18, 4)
        stat = cols(22, 24).rearrange("p (b n) -> p b n", b=2)
        aggr = cols(46, 4).rearrange("p (b n) -> p b n", b=2)
        l_rstd, l_std, l_nb = cols(50, 2), cols(52, 2), cols(146, 2)
        z_stat = cols(150, 24).rearrange("p (b n) -> p b n", b=2)
        z_aggr = cols(174, 4).rearrange("p (b n) -> p b n", b=2)
        z_rstd, z_std, z_nb = cols(178, 2), cols(180, 2), cols(182, 2)
        hsum, hvar, hstd = cols(54, 8), cols(62, 8), cols(70, 8)
        negmax = cols(78, 4).rearrange("p (b n) -> p b n", b=2)
        zsum = cols(82, 4).rearrange("p (b n) -> p b n", b=2)
        zinv = cols(86, 4).rearrange("p (b n) -> p b n", b=2)
        r1 = cols(90, 8).rearrange("p (b n) -> p b n", b=2)
        ssq = cols(98, 32)
        gates = cols(130, 2 * NT).rearrange("p (j t) -> p j t", j=2)
        router_bc = sb("router_bc", [P, NE])
        subg = sb("subg", [P, P])
        slot_i = sb("slot_i", [P, 2, NT], i32)
        id_at = sb("id_at", [P, 2, NT], i32)
        id_low = small[:, 190:190 + 2 * NT].bitcast(i32).rearrange("p (j t) -> p j t", j=2)

        psum = ctx.enter_context(nc.psum_tensor("psum", [P, 8, H], f32))

        def bank(i):
            return psum[:, i, :]

        def bank2(i):
            return psum[:, i:i + 2, :].rearrange("p b n -> p (b n)")

        sqt = C[:, 7168:7680]
        r_exp, r_prob = rt[:, 0:128], rt[:, 128:256]
        r_gt, r_eq = rt[:, 256:768], rt[:, 768:1280]
        r_rank, r_mask, r_tmp, r_tot = rt[:, 1280:1408], rt[:, 1408:1536], rt[:, 1536:1664], rt[:, 1664:1792]
        r_off = rt[:, 1792:1792 + (NT + 1) * NE]
        r_group, r_grank = rt[:, 1952:1984], rt[:, 1984:2016]
        r_row, r_lo, r_hi = rt[:, 2016:2024], rt[:, 2024:2032], rt[:, 2032:2040]
        r_tiles, r_start = rt[:, 2048:2064], rt[:, 2064:2081]

        slot_loaded = [sem(f"slot_loaded{i}") for i in range(RING)]
        consts_in, small_in, cond_ready, ones_ready = (
            sem("consts_in"), sem("small_in"), sem("cond_ready"), sem("ones_ready"))
        ada_summed, mod_done, mod_stored, var_ready = (
            sem("ada_summed"), sem("mod_done"), sem("mod_stored"), sem("var_ready"))
        std_ready, xn_ready, turned, hT_act = (
            sem("std_ready"), sem("xn_ready"), sem("turned"), sem("hT_act"))
        hT_dve, proj_done, rot_ready, rotT_done = (
            sem("hT_dve"), sem("proj_done"), sem("rot_ready"), sem("rotT_done"))
        rotT_stored, rs_done, rp_ready, ro_done = (
            sem("rotT_stored"), sem("rs_done"), sem("rp_ready"), sem("ro_done"))
        ro_free, kv_done, state_ready, rvar_ready = (
            sem("ro_free"), sem("kv_done"), sem("state_ready"), sem("rvar_ready"))
        rstd_ready, lam_sums, lam_exp, max_ready = (
            sem("rstd_ready"), sem("lam_sums"), sem("lam_exp"), sem("max_ready"))
        a_ready, aT_done, aT_stored, av_done = (
            sem("a_ready"), sem("aT_done"), sem("aT_stored"), sem("av_done"))
        ssq_ready, rms_std, ln_in, mix_ready = (
            sem("ssq_ready"), sem("rms_std"), sem("ln_in"), sem("mix_ready"))
        mixT_done, mixT_stored, o_done, o_free = (
            sem("mixT_done"), sem("mixT_stored"), sem("o_done"), sem("o_free"))
        ovar, ostd, orstd, un_ready = (
            sem("ovar"), sem("ostd"), sem("orstd"), sem("un_ready"))
        x1_ready, zvar, zstd, zrstd = (
            sem("x1_ready"), sem("zvar"), sem("zstd"), sem("zrstd"))
        z_ready, zT_done, h2_act, h2_dve = (
            sem("z_ready"), sem("zT_done"), sem("h2_act"), sem("h2_dve"))
        logits_done, lmax_ready, lexp_done, mask_ready = (
            sem("logits_done"), sem("lmax_ready"), sem("lexp_done"), sem("mask_ready"))
        count_done, ids_zeroed, slots_ready, ids_out = (
            sem("count_done"), sem("ids_zeroed"), sem("slots_ready"), sem("ids_out"))
        ids_in, idx_ready, tok_in, idx_zero = (
            sem("ids_in"), sem("idx_ready"), sem("tok_in"), sem("idx_zero"))
        starts_ready, gathered, xgT_done, hg_stored = (
            sem("starts_ready"), sem("gathered"), sem("xgT_done"), sem("hg_stored"))
        gate_done, up_done, silu_done, he_ready = (
            sem("gate_done"), sem("up_done"), sem("silu_done"), sem("he_ready"))
        heT_done, heT_stored, y_done, y_stored = (
            sem("heT_done"), sem("heT_stored"), sem("y_done"), sem("y_stored"))
        y_out, yg_free, fvar, fstd = (
            sem("y_out"), sem("yg_free"), sem("fvar"), sem("fstd"))
        frstd, fn_ready, ffn_in, dve_step = (
            sem("frstd"), sem("fn_ready"), sem("ffn_in"), sem("dve_step"))
        pool_step = (
            sem("pool_step"))
        av_free = sem("av_free")
        y_zeroed = sem("y_zeroed")
        passed = sem("passed")
        dq_zeroed = sem("dq_zeroed")
        x_in = [sem(f"x_in{i}") for i in range(NT)]
        proj_free = [sem(f"proj_free{i}") for i in range(2)]
        s_done = [sem(f"s_done{i}") for i in range(2)]
        exp_done = [sem(f"exp_done{i}") for i in range(2)]
        xr_in = [sem(f"xr_in{i}") for i in range(2)]
        z_out = [sem(f"z_out{i}") for i in range(2)]
        w_ready = [[sem(f"w_ready{q}{j}") for j in range(3)] for q in range(2)]
        y_in = [[sem(f"y_in{b}{j}") for j in range(2)] for b in range(YBUF)]
        out_done = [sem(f"out_done{i}") for i in range(YBUF)]
        xn_inv = sem("xn_inv")
        x1_scaled, y1_scaled, gained, biased = sem("x1_scaled"), sem("y1_scaled"), sem("gained"), sem("biased")

        block = ctx.enter_context(nc.Block())

        exp_w = [[ring[0][:], B[:, 0:4096].rearrange("p (k n) -> p k n", k=KC),
                  B[:, 4096:8192].rearrange("p (k n) -> p k n", k=FK)],
                 [ring[1][:], ring[2][:], M[:, 0:4096].rearrange("p (k n) -> p k n", k=FK)]]

        def bc(ap, shape, at):
            for d in at:
                ap = ap.unsqueeze(d)
            return ap.broadcast_to(shape)

        def wait_nonzero(engine, semaphore, count):
            if count > 0:
                engine.wait_ge(semaphore, count)

        def keys(qb):
            return (qb + 1) * P

        def mod_bank(b):
            return bank(2 if b in (0, 1, 2, 3, 6, 7, 8, 9, 4) else 7)

        def used_up(kind, b):
            if kind == "ada":
                return mod_done, ADA_ORDER.index(b) + 1
            if kind == "in":
                return proj_done, NT * (PROJ_ORDER.index(b) + 1)
            return o_done, NT

        @block.sync
        def _(sp):
            for n, (kind, b) in enumerate(BLOCKS):
                s, _ = slot_use(kind, b)
                if n >= RING:
                    sp.wait_ge(*used_up(*BLOCKS[n - RING]))
                src = {"ada": w_ada_v, "in": w_in_v, "out": w_out_v}[kind][:, :, b * H:(b + 1) * H]
                sp.dma_start(ring[s][:], src).then_inc(slot_loaded[s], 16)

            def load_expert(e, q):
                gate = w_gate[0][bass.ds(e, 1)].rearrange("o (k p) n -> p (o k) n", p=P)
                up = w_up[0][bass.ds(e, 1)].rearrange("o (k p) n -> p (o k) n", p=P)
                down = w_down[0][bass.ds(e, 1)].rearrange("o (k p) n -> p (o k) n", p=P)
                for j, src in enumerate((gate, up, down)):
                    sp.dma_start(exp_w[q][j], src).then_inc(w_ready[q][j], 16)

            sp.wait_ge(mod_done, len(ADA_ORDER))
            sp.wait_ge(s_done[1], NT * DIFF_H)
            load_expert(0, 0)
            sp.wait_ge(o_done, NT)
            load_expert(1, 1)
            sp.wait_ge(starts_ready, 1)
            with sp.Fori(1, NE // 2) as i:
                for q in range(2):
                    end = sp.value_load(ts_i[0:1, bass.ds(i * 2 + (q - 1), 1)], min_val=1, max_val=MAX_TILES)
                    sp.wait_ge(y_done, end + 1)
                    load_expert(i * 2 + q, q)
            for t in range(NT):
                sp.wait_ge(biased, t + 1)
                sp.dma_start(out_v[:, t], fin[:, t % YBUF]).then_inc(out_done[t % YBUF], 16)
            for b in range(YBUF):
                sp.wait_ge(out_done[b], 16 * NT // YBUF)

        @block.gpsimd
        def _(pool):
            pool.dma_start(craw, c.rearrange("o (p k) -> (o p) k", k=KC)).then_inc(small_in, 16)
            pool.dma_start(cst[:], consts).then_inc(consts_in, 16)
            pool.dma_start(b12[:], b_ada[0].rearrange("(b n) -> b n", n=H)).then_inc(small_in, 16)
            for i, v in enumerate((lq1, lk1, lq2, lk2)):
                pool.dma_start(lamv[:, i, :], v[0].partition_broadcast(P)).then_inc(small_in, 16)
            pool.dma_start(subg[:], subln[0].partition_broadcast(P)).then_inc(small_in, 16)
            pool.dma_start(rw[:], router_w.rearrange("(k p) e -> p k e", p=P)).then_inc(small_in, 16)
            pool.dma_start(router_bc[:], router_b.partition_broadcast(P)).then_inc(small_in, 16)

            pool.memset(g2b[:], 0.0).then_inc(pool_step, 1)
            pool.wait_ge(pool_step, 1)
            for g in range(NE, MAX_TILES):
                pool.dma_start(y_rows.ap()[g * P:(g + 1) * P, :], g2b[:]).then_inc(y_zeroed, 16)
            pool.wait_ge(rs_done, NT)
            pool.wait_ge(ro_done, NT)
            pool.memset(dqT[0][DH:P], 0.0).then_inc(dq_zeroed, 1)
            pool.memset(dqT[1][0:DH], 0.0).then_inc(dq_zeroed, 1)
            pool.wait_ge(av_done, NT * DIFF_H)
            pool.dma_start(ln_g, mix_g[0].partition_broadcast(P)).then_inc(ln_in, 16)
            pool.dma_start(ln_b, mix_b[0].partition_broadcast(P)).then_inc(ln_in, 16)
            pool.wait_ge(ln_in, 32)
            for t in range(NT):
                pool.wait_ge(un_ready, t + 1)
                pool.tensor_tensor(x1[:, t], u[:, t % 2], ln_g, ALU.mult).then_inc(pool_step, 1)
                pool.wait_ge(pool_step, t + 2)
                pool.tensor_tensor(x1[:, t], x1[:, t], ln_b, ALU.add).then_inc(x1_ready, 1)

            pool.wait_ge(x1_ready, NT)
            pool.memset(idx_all, 0).then_inc(idx_zero, 1)
            pool.wait_ge(idx_zero, 1)
            pool.dma_start(slot_ids.ap().rearrange("(p g) o -> p (g o)", p=P), idx_all).then_inc(ids_zeroed, 16)
            pool.dma_start(tok_i, token_ids).then_inc(tok_in, 16)
            pool.wait_ge(ids_zeroed, 16)
            pool.wait_ge(tok_in, 16)
            pool.wait_ge(slots_ready, 1)
            for t in range(NT):
                for j in range(2):
                    pool.indirect_dma_start(slot_ids.ap(), bass.IndirectOffsetOnAxis(ap=id_at[:, j, t:t + 1], axis=0),
                                            tok_i[:, t:t + 1], None).then_inc(ids_out, 16)
            pool.wait_ge(ids_out, 16 * 2 * NT)
            pool.dma_start(idx_all, slot_ids.ap().rearrange("(p g) o -> p (g o)", p=P)).then_inc(ids_in, 16)
            pool.wait_ge(ids_in, 16)
            pool.wait_ge(starts_ready, 1)
            total = pool.value_load(ts_i[0:1, NE:NE + 1], min_val=NE, max_val=MAX_TILES)
            with pool.Fori(0, total + 1) as g:
                pool.wait_ge(xgT_done, g + 1)
                pool.tensor_copy(idx_cur, idx_all[:, bass.ds(g, 1)]).then_inc(idx_ready, 1)
                pool.wait_ge(idx_ready, g + 1)
                pool.sem_inc(passed, 1)
                pool.indirect_dma_start(xg, None, z_rows.ap(),
                                        bass.IndirectOffsetOnAxis(ap=idx_cur, axis=0)).then_inc(gathered, 16)
                pool.wait_ge(gathered, g * 16 + 16)

            pool.dma_start(ln_g, ffn_g[0].partition_broadcast(P)).then_inc(ffn_in, 16)
            pool.dma_start(ln_b, ffn_b[0].partition_broadcast(P)).then_inc(ffn_in, 16)
            pool.wait_ge(y_out, total * 16 + 16)
            pool.sem_inc(passed, 1)

            def gain(t):
                pool.wait_ge(fn_ready, t + 1)
                pool.tensor_tensor(fin[:, t % YBUF], fin[:, t % YBUF], ln_g, ALU.mult).then_inc(gained, 1)

            for t in range(NT):
                if t >= YBUF:
                    pool.wait_ge(yg_free, t - YBUF + 1)
                for j in range(2):
                    pool.indirect_dma_start(ygath[:, t % YBUF, j], None, y_rows.ap(),
                                            bass.IndirectOffsetOnAxis(ap=slot_i[:, j, t:t + 1], axis=0)
                                            ).then_inc(y_in[t % YBUF][j], 16)
                if t == 0:
                    pool.wait_ge(ffn_in, 32)
                if t >= 3:
                    gain(t - 3)
            for t in range(NT - 3, NT):
                gain(t)

        @block.scalar
        def _(act):
            for t in range(NT):
                act.dma_start(xn[:, t], x_v[:, t]).then_inc(x_in[t], 16)
            act.wait_ge(small_in, 144)
            nc.scalar.activation(cond, craw, ACT.Silu).then_inc(cond_ready, 1)
            act.wait_ge(lam_sums, 1)
            nc.scalar.activation(lam4[:, 2:4], lam4[:, 0:2], ACT.Exp).then_inc(lam_exp, 1)
            for t in range(NT):
                b = t % 2
                act.wait_ge(var_ready, t + 1)
                nc.scalar.activation(l_std[:, b:b + 1], aggr[:, b, 1:2], ACT.Sqrt, bias=eps_c).then_inc(std_ready, 1)
                act.wait_ge(xn_inv, t + 1)
                nc.scalar.activation(xn[:, t], xn[:, t], ACT.Identity, scale=l_rstd[:, b:b + 1], bias=l_nb[:, b:b + 1]
                                     ).then_inc(xn_ready, 1)
            act.wait_ge(mod_stored, 4)
            for t in range(NT):
                act.wait_ge(turned, 2 * t + 1)
                for k in range(4):
                    last = nc.scalar.activation(hT[:, k, t * P:(t + 1) * P], bank((2 * t) % 4)[:, k * P:(k + 1) * P],
                                                ACT.Identity, scale=modcol[:, 1, k:k + 1], bias=modcol[:, 0, k:k + 1])
                last.then_inc(hT_act, 1)
            for i in range(2 * NT):
                t = i % NT
                act.wait_ge(rotT_done, i + 1)
                nc.scalar.activation((rqT, rkT)[i // NT][:, :, t * P:(t + 1) * P],
                                     bank(3 + i % 2).rearrange("p (c n) -> p c n", c=PAIRS), ACT.Copy
                                     ).then_inc(rotT_stored, 1)

            def from_projection(g, dst, func=ACT.Copy, scale=1.0):
                act.wait_ge(proj_done, g + 1)
                nc.scalar.activation(dst, bank(g % 2), func, scale=scale).then_inc(proj_free[g % 2], 1)

            for t in range(NT):
                from_projection(3 * NT + t, ret_out[:, t], ACT.Silu)
            for n in range(NT):
                from_projection(4 * NT + n, dv[:, n])
                act.wait_ge(rvar_ready, n + 1)
                nc.scalar.activation(hstd, hvar, ACT.Sqrt, bias=eps_c, scale=1.0 / DH).then_inc(rstd_ready, 1)
            for j in range(NT):
                g = 5 * NT + j
                act.wait_ge(proj_done, g + 1)
                for q in range(2):
                    rows = slice(q * DH, (q + 1) * DH)
                    last = nc.scalar.activation(dqT[q][rows, j // 2, (j % 2) * H:(j % 2 + 1) * H], bank(g % 2)[rows, :],
                                                ACT.Copy, scale=DH ** -0.5)
                last.then_inc(proj_free[g % 2], 1)
            for j in range(NT):
                from_projection(6 * NT + j, dkT[:, j // 2, (j % 2) * H:(j % 2 + 1) * H])

            def exps(i):
                for q in range(2):
                    act.wait_ge(max_ready, 2 * i + q + 1)
                    if i >= 2:
                        act.wait_ge(aT_done, i - 1)
                    nc.scalar.activation(probs[:, i % 2, q, 0:keys(i // DIFF_H)], bank2(2 * q)[:, 0:keys(i // DIFF_H)],
                                         ACT.Exp, bias=negmax[:, i % 2, q:q + 1], accum_out=zsum[:, i % 2, q:q + 1]
                                         ).then_inc(exp_done[q], 1)

            def store_turned(i):
                act.wait_ge(aT_done, i + 1)
                if i >= 2:
                    act.wait_ge(av_done, i - 1)
                nc.scalar.activation(aT[:, i % 2, 0:keys(i // DIFF_H)], bank2(4)[:, 0:keys(i // DIFF_H)], ACT.Copy
                                     ).then_inc(aT_stored, 1)

            for i in range(NT * DIFF_H):
                if i >= 2:
                    store_turned(i - 2)
                exps(i)
            store_turned(NT * DIFF_H - 2)
            store_turned(NT * DIFF_H - 1)
            act.wait_ge(ssq_ready, NT)
            nc.scalar.activation(ssq, ssq, ACT.Sqrt, bias=eps_c, scale=1.0 / P).then_inc(rms_std, 1)

            def store_mixT(t):
                act.wait_ge(mixT_done, t + 1)
                if t >= 2:
                    act.wait_ge(o_done, t - 1)
                nc.scalar.activation(mixT[t % 2], bank2(0).rearrange("p (k n) -> p k n", k=KC), ACT.Copy
                                     ).then_inc(mixT_stored, 1)

            def mixed(t):
                b = t % 2
                if t == 0:
                    for n in range(2):
                        act.dma_start(xr[:, n], x_v[:, n]).then_inc(xr_in[n], 16)
                elif t + 1 < NT:
                    wait_nonzero(act, ovar, t)
                    act.dma_start(xr[:, (t + 1) % 2], x_v[:, t + 1]).then_inc(xr_in[(t + 1) % 2], 16)
                act.wait_ge(ovar, t + 1)
                nc.scalar.activation(l_std[:, b:b + 1], aggr[:, b, 1:2], ACT.Sqrt, bias=eps_c).then_inc(ostd, 1)
                act.wait_ge(orstd, t + 1)
                nc.scalar.activation(u[:, b], u[:, b], ACT.Identity, scale=l_rstd[:, b:b + 1], bias=l_nb[:, b:b + 1]
                                     ).then_inc(un_ready, 1)

            def renormed(t):
                b = t % 2
                act.wait_ge(zvar, t + 1)
                nc.scalar.activation(z_std[:, b:b + 1], z_aggr[:, b, 1:2], ACT.Sqrt, bias=eps_c).then_inc(zstd, 1)
                act.wait_ge(zrstd, t + 1)
                if t >= 2:
                    act.wait_ge(z_out[b], 16 * (t // 2))
                    act.wait_ge(zT_done, t - 1)
                nc.scalar.activation(z[:, b], x1[:, t], ACT.Identity, scale=z_rstd[:, b:b + 1], bias=z_nb[:, b:b + 1]
                                     ).then_inc(z_ready, 1)
                act.wait_ge(z_ready, t + 1)
                nc.scalar.activation(x1[:, t], x1[:, t], ACT.Copy, scale=ALPHA).then_inc(x1_scaled, 1)
                act.dma_start(z_rows.ap()[t * P:(t + 1) * P, :], z[:, b]).then_inc(z_out[b], 16)

            def modulated(t):
                act.wait_ge(zT_done, t + 1)
                wait_nonzero(act, logits_done, t)
                for k in range(4):
                    last = nc.scalar.activation(h2T[:, k], bank(4)[:, k * P:(k + 1) * P], ACT.Identity,
                                                scale=modcol[:, 3, k:k + 1], bias=modcol[:, 2, k:k + 1])
                last.then_inc(h2_act, 1)

            store_mixT(0)
            for t in range(NT + 2):
                if t + 1 < NT:
                    store_mixT(t + 1)
                if t >= 2:
                    modulated(t - 2)
                if t < NT:
                    mixed(t)
                if 1 <= t <= NT:
                    renormed(t - 1)
            act.wait_ge(lmax_ready, 1)
            nc.scalar.activation(r_exp, r_exp, ACT.Exp).then_inc(lexp_done, 1)

            act.wait_ge(starts_ready, 1)
            total = act.value_load(ts_i[0:1, NE:NE + 1], min_val=NE, max_val=MAX_TILES)

            def modulate_gathered():
                for k in range(KC):
                    last = nc.scalar.activation(hgT[:, k], bank2(2)[:, k * P:(k + 1) * P], ACT.Identity,
                                                scale=modcol[:, 3, k:k + 1], bias=modcol[:, 2, k:k + 1])
                last.then_inc(hg_stored, 1)

            act.sem_inc(silu_done, 1)
            act.sem_inc(y_out, 16)
            act.wait_ge(xgT_done, 2)
            modulate_gathered()
            with act.Fori(0, total) as g:
                act.wait_ge(gate_done, g + 1)
                act.wait_ge(he_ready, g + 1)
                nc.scalar.activation(sg, bank(0), ACT.Silu).then_inc(silu_done, 1)
                act.wait_ge(xgT_done, g + 3)
                modulate_gathered()
                act.wait_ge(y_stored, g + 2)
                act.dma_start(y_rows.ap()[bass.ds(g * P, P), :], yb).then_inc(y_out, 16)

            def weigh(t):
                y1 = ygath[:, t % YBUF, 1]
                act.wait_ge(y_in[t % YBUF][1], 16 * (t // YBUF + 1))
                nc.scalar.activation(y1, y1, ACT.Copy, scale=gates[:, 1, t:t + 1]).then_inc(y1_scaled, 1)

            weigh(0)
            for t in range(NT):
                b = t % 2
                if t + 1 < NT:
                    weigh(t + 1)
                act.wait_ge(fvar, t + 1)
                nc.scalar.activation(l_std[:, b:b + 1], aggr[:, b, 1:2], ACT.Sqrt, bias=eps_c).then_inc(fstd, 1)
                act.wait_ge(frstd, t + 1)
                if t >= YBUF:
                    act.wait_ge(out_done[t % YBUF], 16 * (t // YBUF))
                nc.scalar.activation(fin[:, t % YBUF], x1[:, t], ACT.Identity, scale=l_rstd[:, b:b + 1],
                                     bias=l_nb[:, b:b + 1]).then_inc(fn_ready, 1)

        @block.vector
        def _(dve):
            steps = [0]

            def link(ins):
                steps[0] += 1
                ins.then_inc(dve_step, 1)
                dve.wait_ge(dve_step, steps[0])

            def mark(ins):
                steps[0] += 1
                ins.then_inc(dve_step, 1)

            def wait_marks():
                dve.wait_ge(dve_step, steps[0])

            def statistics(src, st, ag, ready):
                mark(nc.vector.bn_stats(st[:, 0:6], src[:, 0:H]))
                mark(nc.vector.bn_stats(st[:, 6:12], src[:, H:D]))
                wait_marks()
                nc.vector.bn_aggr(ag, st.rearrange("p (s n) -> p s n", s=2)).then_inc(ready, 1)

            def invert(sd, ag, rs, nb, ready):
                link(nc.vector.reciprocal(rs, sd))
                nc.vector.tensor_scalar(nb, ag[:, 0:1], rs, -1.0, ALU.mult, ALU.mult).then_inc(ready, 1)

            mark(nc.vector.memset(eps_c, EPS))
            mark(nc.vector.memset(state, 0.0))
            nc.vector.memset(ones[:], 1.0).then_inc(ones_ready, 1)
            wait_marks()
            dve.wait_ge(small_in, 144)
            for i in range(2):
                link(nc.vector.tensor_tensor(lamv[:, 2 * i, :], lamv[:, 2 * i, :], lamv[:, 2 * i + 1, :], ALU.mult))
                ins = nc.vector.tensor_reduce(lam4[:, i:i + 1], lamv[:, 2 * i, :], AX.X, ALU.add)
                if i == 0:
                    mark(ins)
            ins.then_inc(lam_sums, 1)
            mark(nc.vector.tensor_scalar(subg[:], subg[:], 1.0 - LAMBDA_INIT, None, ALU.mult))
            dve.wait_ge(lam_exp, 1)
            link(nc.vector.tensor_tensor(nlam, lam4[:, 3:4], lam4[:, 2:3], ALU.subtract))
            mark(nc.vector.tensor_scalar(nlam, nlam, -LAMBDA_INIT, None, ALU.add))
            dve.wait_ge(cond_ready, 1)

            def ada_sum(b):
                s, uses = slot_use("ada", b)
                w = ring[s]
                dve.wait_ge(slot_loaded[s], 16 * uses)
                link(nc.vector.tensor_scalar(w[:, 0, :], w[:, 0, :], cond[:, 0:1], None, ALU.mult))
                for k in range(1, KC):
                    ins = nc.vector.scalar_tensor_tensor(out=w[:, 0, :], in0=w[:, k, :], scalar=cond[:, k:k + 1],
                                                         in1=w[:, 0, :], op0=ALU.mult, op1=ALU.add)
                    if k < KC - 1:
                        link(ins)
                ins.then_inc(ada_summed, 1)

            def mod_store(b):
                dve.wait_ge(mod_done, ADA_ORDER.index(b) + 1)
                vec, half = b // 2, b % 2
                if vec in (2, 5):
                    dst = (g1b if vec == 2 else g2b[:, :])[:, half * H:(half + 1) * H]
                    nc.vector.tensor_copy(dst, mod_bank(b)).then_inc(mod_stored, 1)
                else:
                    at, one = {0: (0, 0.0), 1: (1, 1.0), 3: (2, 0.0), 4: (3, 1.0)}[vec]
                    nc.vector.tensor_scalar(modcol[:, at, half * 4:half * 4 + 4], mod_bank(b)[:, 0:4], one, None,
                                            ALU.add).then_inc(mod_stored, 1)

            for m in range(4):
                ada_sum(m)
                for t in (2 * m, 2 * m + 1):
                    dve.wait_ge(x_in[t], 16)
                    statistics(xn[:, t], stat[:, t % 2], aggr[:, t % 2], var_ready)
                for t in (2 * m, 2 * m + 1):
                    dve.wait_ge(std_ready, t + 1)
                    if t >= 2:
                        dve.wait_ge(xn_ready, t - 1)
                    invert(l_std[:, t % 2:t % 2 + 1], aggr[:, t % 2], l_rstd[:, t % 2:t % 2 + 1], l_nb[:, t % 2:t % 2 + 1],
                           xn_inv)
                mod_store(m)
            dve.wait_ge(mod_stored, 4)
            for t in range(NT):
                dve.wait_ge(turned, 2 * t + 2)
                for k in range(4, KC):
                    last = nc.vector.tensor_scalar(hT[:, k, t * P:(t + 1) * P],
                                                   bank((2 * t + 1) % 4)[:, (k - 4) * P:(k - 3) * P],
                                                   modcol[:, 1, k:k + 1], modcol[:, 0, k:k + 1], ALU.mult, ALU.add)
                last.then_inc(hT_dve, 1)

            dve.wait_ge(consts_in, 16)
            for i in range(2 * NT):
                t = i % NT
                dve.wait_ge(proj_done, i + 1)
                v = bank(i % 2).rearrange("p (h a d) -> p h a d", h=RET_H, a=2)
                ta = t1.rearrange("p (h a d) -> p h a d", h=RET_H, a=2)
                tb = t2.rearrange("p (h a d) -> p h a d", h=RET_H, a=2)
                sin_b = bc(sin_t[:, t], [P, RET_H, 32], (1,))
                wait_marks()
                wait_nonzero(dve, rot_ready, i)
                mark(nc.vector.tensor_tensor(ta, v, bc(cos_t[:, t], [P, RET_H, 2, 32], (1, 1)), ALU.mult))
                mark(nc.vector.tensor_tensor(tb[:, :, 0], v[:, :, 1], sin_b, ALU.mult))
                nc.vector.tensor_tensor(tb[:, :, 1], v[:, :, 0], sin_b, ALU.mult).then_inc(proj_free[i % 2], 1)
                wait_marks()
                dve.wait_ge(proj_free[i % 2], i // 2 + 1)
                if 2 <= i < NT:
                    dve.wait_ge(rotT_done, i - 1)
                dst = (qrot[:, t % 2] if i < NT else rk[:, t]).rearrange("p (h a d) -> p h a d", h=RET_H, a=2)
                mark(nc.vector.tensor_tensor(dst[:, :, 0], ta[:, :, 0], tb[:, :, 0], ALU.subtract))
                nc.vector.tensor_tensor(dst[:, :, 1], ta[:, :, 1], tb[:, :, 1], ALU.add).then_inc(rot_ready, 1)
            ada_sum(6)
            for t in range(NT):
                g = 2 * NT + t
                dve.wait_ge(proj_done, g + 1)
                nc.vector.tensor_tensor(vs[:, t].rearrange("p (h d) -> p h d", h=RET_H),
                                        bank(g % 2).rearrange("p (h d) -> p h d", h=RET_H),
                                        bc(const("v_decay"), [P, RET_H, DH], (2,)), ALU.mult
                                        ).then_inc(proj_free[g % 2], 1)
                if t == 4:
                    mod_store(6)
            ada_sum(7)
            mod_store(7)
            ada_sum(8)

            q_dec = const("q_decay").rearrange("p (c r) -> p c r", r=2)
            dve.wait_ge(rot_ready, 2 * NT)
            for n in range(NT):
                dve.wait_ge(rs_done, n + 1)
                wait_nonzero(dve, ro_done, n)
                mark(nc.vector.tensor_tensor(pm[:, 0], bank(3).rearrange("p (c n) -> p c n", c=PAIRS),
                                             bc(const("causal"), [P, PAIRS, P], (1,)), ALU.mult))
                nc.vector.tensor_tensor(pm[:, 1], bank(4).rearrange("p (c n) -> p c n", c=PAIRS),
                                        bc(const("causal"), [P, PAIRS, P], (1,)), ALU.mult).then_inc(rp_ready, 1)
                if n == 4:
                    mod_store(8)
                dve.wait_ge(ro_done, n + 1)
                o = t1.rearrange("p (c r d) -> p c r d", c=PAIRS, r=2)
                oh = t1.rearrange("p (h d) -> p h d", h=RET_H)
                xc = t2.rearrange("p (h d) -> p h d", h=RET_H)
                sq = qrot[:, 0].rearrange("p (h d) -> p h d", h=RET_H)
                wait_marks()
                for r in range(2):
                    ins = nc.vector.tensor_tensor(o[:, :, r], bank(5 + r)[:, 0:PAIRS * DH].rearrange("p (c d) -> p c d", c=PAIRS),
                                                  bc(q_dec[:, :, r], [P, PAIRS, DH], (2,)), ALU.mult)
                    if r == 0:
                        mark(ins)
                ins.then_inc(ro_free, 1)
                if n < NT - 1:
                    dve.wait_ge(kv_done, n + 1)
                    kv = bank(7).rearrange("p (c n) -> p c n", c=PAIRS)
                    mark(nc.vector.tensor_tensor(state_new[0:DH], kv[0:DH, :, 0:DH], state[0:DH], ALU.add))
                    mark(nc.vector.tensor_tensor(state_new[DH:P], kv[DH:P, :, DH:P], state[DH:P], ALU.add))
                    wait_marks()
                    nc.vector.tensor_tensor(state, state_new, bc(const("chunk_decay"), [P, PAIRS, DH], (2,)), ALU.mult
                                            ).then_inc(state_ready, 1)
                    dve.wait_ge(state_ready, n + 1)
                wait_marks()
                dve.wait_ge(ro_free, n + 1)
                link(nc.vector.tensor_reduce(hsum, oh, AX.X, ALU.add))
                link(nc.vector.tensor_scalar(hsum, hsum, 1.0 / DH, None, ALU.mult))
                link(nc.vector.tensor_tensor(xc, oh, bc(hsum, [P, RET_H, DH], (2,)), ALU.subtract))
                link(nc.vector.tensor_tensor(sq, xc, xc, ALU.mult))
                nc.vector.tensor_reduce(hvar, sq, AX.X, ALU.add).then_inc(rvar_ready, 1)
                dve.wait_ge(rstd_ready, n + 1)
                link(nc.vector.reciprocal(hstd, hstd))
                link(nc.vector.tensor_tensor(xc, xc, bc(hstd, [P, RET_H, DH], (2,)), ALU.mult))
                if n == 0:
                    dve.wait_ge(proj_free[0], 4 * NT // 2)
                    dve.wait_ge(proj_free[1], 4 * NT // 2)
                mark(nc.vector.tensor_tensor(ret_out[:, n], t2, ret_out[:, n], ALU.mult))
            for b in (9, 4, 5, 10):
                ada_sum(b)
                if b == 10:
                    dve.wait_ge(y_zeroed, 16 * (MAX_TILES - NE))
                mod_store(b)

            def maxima(i):
                for q in range(2):
                    dve.wait_ge(s_done[q], i + 1)
                    nc.vector.tensor_reduce(negmax[:, i % 2, q:q + 1], bank2(2 * q)[:, 0:keys(i // DIFF_H)], AX.X, ALU.max,
                                            negate=True).then_inc(max_ready, 1)

            def combine(i):
                b, qb, h = i % 2, i // DIFF_H, i % DIFF_H
                dve.wait_ge(exp_done[0], i + 1)
                dve.wait_ge(exp_done[1], i + 1)
                link(nc.vector.reciprocal(zinv[:, b], zsum[:, b]))
                mark(nc.vector.tensor_copy(r1[:, qb % 2, h:h + 1], zinv[:, b, 0:1]))
                link(nc.vector.scalar_tensor_tensor(out=zinv[:, b, 1:2], in0=zinv[:, b, 1:2], scalar=zsum[:, b, 0:1],
                                                    in1=nlam, op0=ALU.mult, op1=ALU.mult))
                nc.vector.scalar_tensor_tensor(out=probs[:, b, 0, 0:keys(qb)], in0=probs[:, b, 1, 0:keys(qb)],
                                               scalar=zinv[:, b, 1:2], in1=probs[:, b, 0, 0:keys(qb)],
                                               op0=ALU.mult, op1=ALU.add).then_inc(a_ready, 1)

            def heads_out(qb):
                dve.wait_ge(av_done, DIFF_H * (qb + 1))
                o = dif_out[:, qb].rearrange("p (h e) -> p h e", h=DIFF_H)
                nc.vector.tensor_tensor(o, bank(6).rearrange("p (h e) -> p h e", h=DIFF_H),
                                        bc(r1[:, qb % 2], [P, DIFF_H, P], (2,)), ALU.mult).then_inc(av_free, 1)
                dve.wait_ge(av_free, qb + 1)
                link(nc.vector.tensor_tensor(sqt.rearrange("p (h e) -> p h e", h=DIFF_H), o, o, ALU.mult))
                nc.vector.tensor_reduce(ssq[:, qb * DIFF_H:(qb + 1) * DIFF_H], sqt.rearrange("p (h e) -> p h e", h=DIFF_H),
                                        AX.X, ALU.add).then_inc(ssq_ready, 1)

            maxima(0)
            for i in range(NT * DIFF_H):
                if i % DIFF_H == 1 and i > 1:
                    heads_out(i // DIFF_H - 1)
                combine(i)
                if i + 1 < NT * DIFF_H:
                    maxima(i + 1)
                if i == 5:
                    ada_sum(11)
                if i == 7:
                    mod_store(11)
            heads_out(NT - 1)
            dve.wait_ge(rms_std, 1)
            link(nc.vector.reciprocal(ssq, ssq))

            def mix(t):
                o = dif_out[:, t].rearrange("p (h e) -> p h e", h=DIFF_H)
                link(nc.vector.tensor_tensor(o, o, bc(ssq[:, t * DIFF_H:(t + 1) * DIFF_H], [P, DIFF_H, P], (2,)), ALU.mult))
                nc.vector.tensor_tensor(o, o, bc(subg[:], [P, DIFF_H, P], (1,)), ALU.mult).then_inc(mix_ready, 1)

            def mixed(t):
                b = t % 2
                dve.wait_ge(o_done, t + 1)
                nc.vector.tensor_tensor(u[:, b], bank2(2), g1b, ALU.mult).then_inc(o_free, 1)
                dve.wait_ge(o_free, t + 1)
                dve.wait_ge(xr_in[b], 16 * (t // 2 + 1))
                link(nc.vector.scalar_tensor_tensor(out=u[:, b], in0=xr[:, b], scalar=ALPHA, in1=u[:, b],
                                                    op0=ALU.mult, op1=ALU.add))
                statistics(u[:, b], stat[:, b], aggr[:, b], ovar)
                dve.wait_ge(ostd, t + 1)
                invert(l_std[:, b:b + 1], aggr[:, b], l_rstd[:, b:b + 1], l_nb[:, b:b + 1], orstd)

            def renormed(t):
                b = t % 2
                dve.wait_ge(x1_ready, t + 1)
                statistics(x1[:, t], z_stat[:, b], z_aggr[:, b], zvar)
                dve.wait_ge(zstd, t + 1)
                invert(z_std[:, b:b + 1], z_aggr[:, b], z_rstd[:, b:b + 1], z_nb[:, b:b + 1], zrstd)

            def modulated(t):
                dve.wait_ge(zT_done, t + 1)
                wait_nonzero(dve, logits_done, t)
                for k in range(4, KC):
                    last = nc.vector.tensor_scalar(h2T[:, k], bank(5)[:, (k - 4) * P:(k - 3) * P],
                                                   modcol[:, 3, k:k + 1], modcol[:, 2, k:k + 1], ALU.mult, ALU.add)
                last.then_inc(h2_dve, 1)

            mix(0)
            mix(1)
            for t in range(NT + 2):
                if t + 2 < NT:
                    mix(t + 2)
                if t >= 2:
                    modulated(t - 2)
                if t < NT:
                    mixed(t)
                if 1 <= t <= NT:
                    renormed(t - 1)

            dve.wait_ge(logits_done, NT)
            dve.wait_ge(z_out[0], 16 * NT // 2)
            dve.wait_ge(z_out[1], 16 * NT // 2)
            te = lambda a: a.rearrange("p (t e) -> p t e", e=NE)
            link(nc.vector.tensor_tensor(te(r_exp), te(bank(7)[:, 0:NT * NE]), bc(router_bc[:], [P, NT, NE], (1,)), ALU.add))
            link(nc.vector.tensor_reduce(r_row, te(r_exp), AX.X, ALU.max))
            nc.vector.tensor_tensor(te(r_exp), te(r_exp), bc(r_row, [P, NT, NE], (2,)), ALU.subtract).then_inc(lmax_ready, 1)
            dve.wait_ge(lexp_done, 1)
            link(nc.vector.tensor_reduce(r_row, te(r_exp), AX.X, ALU.add))
            link(nc.vector.reciprocal(r_row, r_row))
            link(nc.vector.tensor_tensor(te(r_prob), te(r_exp), bc(r_row, [P, NT, NE], (2,)), ALU.mult))

            lower = const("lower").rearrange("p (e j) -> p e j", e=EPG)

            def ranks(values, n, gt, ge, rank):
                v = values.rearrange("p (g e) -> p g e", e=EPG)
                g4 = gt.rearrange("p (g e j) -> p g e j", e=EPG, j=EPG)
                q4 = ge.rearrange("p (g e j) -> p g e j", e=EPG, j=EPG)
                vj, ve = bc(v, [P, n, EPG, EPG], (2,)), bc(v, [P, n, EPG, EPG], (3,))
                mark(nc.vector.tensor_tensor(g4, vj, ve, ALU.is_gt))
                link(nc.vector.tensor_tensor(q4, vj, ve, ALU.is_equal))
                link(nc.vector.tensor_tensor(q4, q4, bc(lower, [P, n, EPG, EPG], (1,)), ALU.mult))
                link(nc.vector.tensor_tensor(g4, g4, q4, ALU.add))
                link(nc.vector.tensor_reduce(rank, g4, AX.X, ALU.add))

            ranks(r_prob, NT * NG, r_gt, r_eq, r_rank)
            link(nc.vector.tensor_scalar(r_mask, r_rank, 1.5, None, ALU.is_lt))
            link(nc.vector.tensor_tensor(r_tmp, r_prob, r_mask, ALU.mult))
            link(nc.vector.tensor_reduce(r_group, r_tmp.rearrange("p (g e) -> p g e", e=EPG), AX.X, ALU.add))
            ranks(r_group, NT, r_gt[:, 0:NT * 16], r_eq[:, 0:NT * 16], r_grank)
            link(nc.vector.tensor_scalar(r_grank, r_grank, 0.5, None, ALU.is_lt))
            gm = r_mask.rearrange("p (g e) -> p g e", e=EPG)
            nc.vector.tensor_tensor(gm, gm, bc(r_grank, [P, NT * NG, EPG], (2,)), ALU.mult).then_inc(mask_ready, 1)
            dve.wait_ge(mask_ready, 1)
            link(nc.vector.tensor_tensor(r_prob, r_prob, r_mask, ALU.mult))
            link(nc.vector.tensor_reduce(r_row, te(r_prob), AX.X, ALU.add))
            link(nc.vector.reciprocal(r_row, r_row))
            link(nc.vector.tensor_tensor(te(r_prob), te(r_prob), bc(r_row, [P, NT, NE], (2,)), ALU.mult))
            dve.wait_ge(count_done, 1)
            mark(nc.vector.memset(r_off[:, 0:NE], 0.0))
            link(nc.vector.tensor_copy(r_tot, bank(1)[:, 0:NT * NE]))
            for t in range(1, NT + 1):
                link(nc.vector.tensor_tensor(r_off[:, t * NE:(t + 1) * NE], r_off[:, (t - 1) * NE:t * NE],
                                             r_tot[:, (t - 1) * NE:t * NE], ALU.add))
            r7 = r_gt[:, 0:NE * (NT - 1)].rearrange("p (e m) -> p e m", m=NT - 1)
            link(nc.vector.tensor_tensor(r7, bc(r_off[:, NT * NE:], [P, NE, NT - 1], (2,)),
                                         bc(const("steps"), [P, NE, NT - 1], (1,)), ALU.is_gt))
            link(nc.vector.tensor_reduce(r_tiles, r7, AX.X, ALU.add))
            link(nc.vector.tensor_scalar(r_tiles, r_tiles, 1.0, None, ALU.add))
            mark(nc.vector.memset(r_start[:, 0:1], 0.0))
            link(nc.vector.tensor_tensor_scan(r_start[:, 1:NE + 1], ones[:, 0:NE], r_tiles, 0.0, ALU.mult, ALU.add))
            nc.vector.tensor_copy(ts_i[:], r_start[0:1, :]).then_inc(starts_ready, 1)
            link(nc.vector.tensor_scalar(r_tiles, r_start[:, 0:NE], float(P), None, ALU.mult))
            link(nc.vector.tensor_tensor(r_tmp, bank(0)[:, 0:NT * NE], r_off[:, 0:NT * NE], ALU.add))
            link(nc.vector.tensor_tensor(te(r_tmp), te(r_tmp), bc(r_tiles, [P, NT, NE], (1,)), ALU.add))
            link(nc.vector.tensor_tensor(r_tmp, r_tmp, r_mask, ALU.mult))
            link(nc.vector.tensor_reduce(r_hi, te(r_tmp), AX.X, ALU.max))
            link(nc.vector.tensor_tensor(te(r_tot), te(r_tmp), bc(r_hi, [P, NT, NE], (2,)), ALU.is_equal))
            link(nc.vector.tensor_tensor(te(r_gt[:, 0:NT * NE]), te(r_tot), te(r_prob), ALU.mult))
            link(nc.vector.tensor_reduce(gates[:, 1], te(r_gt[:, 0:NT * NE]), AX.X, ALU.add))
            link(nc.vector.tensor_tensor(r_tot, r_mask, r_tot, ALU.subtract))
            link(nc.vector.tensor_tensor(te(r_gt[:, 0:NT * NE]), te(r_tot), te(r_prob), ALU.mult))
            link(nc.vector.tensor_reduce(gates[:, 0], te(r_gt[:, 0:NT * NE]), AX.X, ALU.add))
            link(nc.vector.tensor_tensor(r_tot, r_tot, r_tmp, ALU.mult))
            link(nc.vector.tensor_reduce(r_lo, te(r_tot), AX.X, ALU.add))
            link(nc.vector.tensor_copy(slot_i[:, 0], r_lo))
            link(nc.vector.tensor_copy(slot_i[:, 1], r_hi))
            link(nc.vector.tensor_single_scalar(id_at[:], slot_i[:], 7, ALU.logical_shift_right))
            link(nc.vector.tensor_scalar(id_low, slot_i[:], P - 1, 5, ALU.bitwise_and, ALU.logical_shift_left))
            nc.vector.tensor_tensor(id_at[:], id_at[:], id_low, ALU.bitwise_or).then_inc(slots_ready, 1)

            dve.wait_ge(starts_ready, 1)
            total = dve.value_load(ts_i[0:1, NE:NE + 1], min_val=NE, max_val=MAX_TILES)
            for buffer_free in (he_ready, heT_stored, y_stored):
                dve.sem_inc(buffer_free, 1)
            with dve.Fori(0, total) as g:
                dve.wait_ge(silu_done, g + 2)
                dve.wait_ge(up_done, g + 1)
                dve.wait_ge(heT_done, g + 1)
                nc.vector.tensor_tensor(he, sg, bank(1), ALU.mult).then_inc(he_ready, 1)
                dve.wait_ge(heT_done, g + 2)
                dve.wait_ge(y_done, g + 1)
                nc.vector.tensor_copy(heT, bank(4).rearrange("p (k n) -> p k n", k=FK)).then_inc(heT_stored, 1)
                dve.wait_ge(y_done, g + 2)
                dve.wait_ge(y_out, g * 16 + 16)
                nc.vector.tensor_tensor(yb, bank2(5), g2b[:], ALU.mult).then_inc(y_stored, 1)

            def last_norm(t):
                b = t % 2
                dve.wait_ge(fstd, t + 1)
                invert(l_std[:, b:b + 1], aggr[:, b], l_rstd[:, b:b + 1], l_nb[:, b:b + 1], frstd)

            def bias(t):
                dve.wait_ge(gained, t + 1)
                nc.vector.tensor_tensor(fin[:, t % YBUF], fin[:, t % YBUF], ln_b, ALU.add).then_inc(biased, 1)

            dve.wait_ge(x1_scaled, NT)
            for t in range(NT):
                b, yb_t = t % 2, t % YBUF
                dve.wait_ge(y_in[yb_t][0], 16 * (t // YBUF + 1))
                dve.wait_ge(y1_scaled, t + 1)
                link(nc.vector.scalar_tensor_tensor(out=ygath[:, yb_t, 1], in0=ygath[:, yb_t, 0],
                                                    scalar=gates[:, 0, t:t + 1], in1=ygath[:, yb_t, 1],
                                                    op0=ALU.mult, op1=ALU.add))
                nc.vector.tensor_tensor(x1[:, t], x1[:, t], ygath[:, yb_t, 1], ALU.add).then_inc(yg_free, 1)
                dve.wait_ge(yg_free, t + 1)
                statistics(x1[:, t], stat[:, b], aggr[:, b], fvar)
                last_norm(t)
                if t >= 2:
                    bias(t - 2)
            bias(NT - 2)
            bias(NT - 1)

        @block.tensor
        def _(pe):
            mm, tr = nc.tensor.matmul, nc.tensor.transpose

            def modulation(b):
                m = ADA_ORDER.index(b)
                vec = b // 2
                pe.wait_ge(ada_summed, m + 1)
                if m >= 1:
                    pe.wait_ge(mod_stored, m)
                w, out_b = ring[slot_use("ada", b)[0]], mod_bank(b)
                if vec in (2, 5):
                    mm(out_b, ones[:], w[:, 0, :], start=True, stop=False)
                    last = mm(out_b, ident[0:12, b:b + 1].broadcast_to([12, P]), b12[:, :], start=False, stop=True)
                else:
                    for q in range(4):
                        mm(out_b[:, q:q + 1], w[:, 0, q * P:(q + 1) * P], ones[:, 0:1], start=True, stop=False)
                        last = mm(out_b[:, q:q + 1], b12[:, q * P:(q + 1) * P], ident[0:12, b:b + 1],
                                  start=False, stop=True)
                last.then_inc(mod_done, 1)

            pe.wait_ge(ones_ready, 1)
            pe.wait_ge(consts_in, 16)
            pe.wait_ge(small_in, 144)
            pe.wait_ge(cond_ready, 1)
            for b in range(4):
                modulation(b)
            pe.wait_ge(mod_stored, 4)
            for t in range(NT):
                pe.wait_ge(xn_ready, t + 1)
                if t >= 2:
                    pe.wait_ge(hT_act, t - 1)
                    pe.wait_ge(hT_dve, t - 1)
                for k in range(KC):
                    last = tr(bank((2 * t + k // 4) % 4)[:, (k % 4) * P:(k % 4 + 1) * P], xn[:, t, k * P:(k + 1) * P], ident)
                    if k % 4 == 3:
                        last.then_inc(turned, 1)
            pe.wait_ge(hT_act, NT)
            pe.wait_ge(hT_dve, NT)

            def project(b, j):
                g = NT * PROJ_ORDER.index(b) + j
                s, uses = slot_use("in", b)
                if j == 0:
                    pe.wait_ge(slot_loaded[s], 16 * uses)
                if g >= 2:
                    pe.wait_ge(proj_free[g % 2], g // 2)
                for k in range(KC):
                    if b in (DQ, DK):
                        last = mm(bank(g % 2), ring[s][:, k, (j // 2) * P:(j // 2 + 1) * P],
                                  hT[:, k, (j % 2) * H:(j % 2 + 1) * H], start=(k == 0), stop=(k == KC - 1))
                    else:
                        last = mm(bank(g % 2), hT[:, k, j * P:(j + 1) * P], ring[s][:, k, :],
                                  start=(k == 0), stop=(k == KC - 1))
                last.then_inc(proj_done, 1)

            def turn_rotated(i):
                pe.wait_ge(rot_ready, i + 1)
                if i >= 2:
                    pe.wait_ge(rotT_stored, i - 1)
                src = qrot[:, i % 2] if i < NT else rk[:, i - NT]
                for p in range(PAIRS):
                    last = tr(bank(3 + i % 2)[:, p * P:(p + 1) * P], src[:, p * P:(p + 1) * P], ident)
                last.then_inc(rotT_done, 1)

            for i in range(2 * NT):
                project((RQ, RK)[i // NT], i % NT)
                if i >= 1:
                    turn_rotated(i - 1)
            for t in range(NT):
                project(RV, t)
                if t == 0:
                    turn_rotated(2 * NT - 1)
                if t == 3:
                    modulation(6)
            for t in range(NT):
                project(RG, t)
                if t == 3:
                    modulation(7)
            pe.wait_ge(rotT_stored, 2 * NT)
            for n in range(NT):
                wait_nonzero(pe, rp_ready, n)
                here = slice(n * P, (n + 1) * P)
                for p in range(PAIRS):
                    for r in range(2):
                        rows = slice(r * DH, (r + 1) * DH)
                        last = mm(bank(3 + r)[:, p * P:(p + 1) * P], rkT[rows, p, here], rqT[rows, p, here],
                                  start=True, stop=True)
                last.then_inc(rs_done, 1)
                project(DV, n)
                if n == 3:
                    modulation(8)
                pe.wait_ge(rp_ready, n + 1)
                wait_nonzero(pe, ro_free, n)
                if n >= 1:
                    wait_nonzero(pe, state_ready, n)
                for p in range(PAIRS):
                    for r in range(2):
                        h = 2 * p + r
                        rows = slice(r * DH, (r + 1) * DH)
                        o = bank(5 + r)[:, p * DH:(p + 1) * DH]
                        last = mm(o, pm[:, r, p], vs[:, n, h * DH:(h + 1) * DH], start=True, stop=(n == 0))
                        if n > 0:
                            last = mm(o, rqT[rows, p, here], state[rows, p], start=False, stop=True)
                last.then_inc(ro_done, 1)
                if n < NT - 1:
                    for p in range(PAIRS):
                        last = mm(bank(7)[:, p * P:(p + 1) * P], rk[:, n, p * P:(p + 1) * P], vs[:, n, p * P:(p + 1) * P],
                                  start=True, stop=True)
                    last.then_inc(kv_done, 1)
            for j in range(NT):
                project(DQ, j)
                if j == 3:
                    modulation(9)
            for j in range(NT):
                project(DK, j)
                if j == 3:
                    modulation(4)
            modulation(5)
            modulation(10)
            pe.wait_ge(proj_free[0], 7 * NT // 2)
            pe.wait_ge(proj_free[1], 7 * NT // 2)

            pe.wait_ge(dq_zeroed, 2)

            def scores(i, q):
                qb, h = i // DIFF_H, i % DIFF_H
                wait_nonzero(pe, exp_done[q], i)
                for a in range(0, keys(qb), H):
                    n = min(H, keys(qb) - a)
                    diagonal = a + n == keys(qb)
                    mm(bank(2 * q + a // H)[:, 0:n], dqT[q][:, h, qb * P:(qb + 1) * P], dkT[:, h, a:a + n],
                       start=True, stop=not diagonal)
                mm(bank(2 * q + a // H)[:, n - P:n], ident, const("neg_mask"), start=False, stop=True
                   ).then_inc(s_done[q], 1)

            def turn_probs(i):
                qb = i // DIFF_H
                pe.wait_ge(a_ready, i + 1)
                wait_nonzero(pe, aT_stored, i)
                for kb in range(qb + 1):
                    last = tr(bank2(4)[:, kb * P:(kb + 1) * P], probs[:, i % 2, 0, kb * P:(kb + 1) * P], ident)
                last.then_inc(aT_done, 1)

            def times_v(i):
                qb, h = i // DIFF_H, i % DIFF_H
                pe.wait_ge(aT_stored, i + 1)
                if h == 0:
                    wait_nonzero(pe, av_free, qb)
                for kb in range(qb + 1):
                    last = mm(bank(6)[:, h * P:(h + 1) * P], aT[:, i % 2, kb * P:(kb + 1) * P],
                              dv[:, kb, h * P:(h + 1) * P], start=(kb == 0), stop=(kb == qb))
                last.then_inc(av_done, 1)

            for i in range(NT * DIFF_H + 2):
                if i >= 2:
                    turn_probs(i - 2)
                if i < NT * DIFF_H:
                    scores(i, 0)
                if i >= 2:
                    times_v(i - 2)
                if i < NT * DIFF_H:
                    scores(i, 1)
                if i == 7:
                    modulation(11)

            def turn_mixed(t):
                pe.wait_ge(mix_ready, t + 1)
                wait_nonzero(pe, mixT_stored, t)
                for k in range(KC):
                    src = ret_out if k < 4 else dif_out
                    last = tr(bank(k // 4)[:, (k % 4) * P:(k % 4 + 1) * P], src[:, t, (k % 4) * P:(k % 4 + 1) * P], ident)
                last.then_inc(mixT_done, 1)

            def project_out(t, half):
                s, uses = slot_use("out", half)
                if t == 0:
                    pe.wait_ge(slot_loaded[s], 16 * uses)
                if half == 0:
                    pe.wait_ge(mixT_stored, t + 1)
                    wait_nonzero(pe, o_free, t)
                for k in range(KC):
                    last = mm(bank(2 + half), mixT[t % 2][:, k], ring[s][:, k, :], start=(k == 0), stop=(k == KC - 1))
                if half == 1:
                    last.then_inc(o_done, 1)

            def turn_z(t):
                pe.wait_ge(z_ready, t + 1)
                wait_nonzero(pe, h2_act, t)
                wait_nonzero(pe, h2_dve, t)
                for k in range(KC):
                    last = tr(bank(4 + k // 4)[:, (k % 4) * P:(k % 4 + 1) * P], z[:, t % 2, k * P:(k + 1) * P], ident)
                last.then_inc(zT_done, 1)

            def logits(t):
                pe.wait_ge(h2_act, t + 1)
                pe.wait_ge(h2_dve, t + 1)
                for k in range(KC):
                    last = mm(bank(7)[:, t * NE:(t + 1) * NE], h2T[:, k], rw[:, k], start=(k == 0), stop=(k == KC - 1))
                last.then_inc(logits_done, 1)

            pe.wait_ge(exp_done[0], NT * DIFF_H)
            pe.wait_ge(exp_done[1], NT * DIFF_H)
            pe.wait_ge(mod_stored, len(ADA_ORDER))
            turn_mixed(0)
            for t in range(NT + 2):
                if t < NT:
                    project_out(t, 0)
                if t + 1 < NT:
                    turn_mixed(t + 1)
                if t >= 2:
                    turn_z(t - 2)
                if t < NT:
                    project_out(t, 1)
                if t >= 2:
                    logits(t - 2)
            pe.wait_ge(mask_ready, 1)
            mm(bank(0)[:, 0:NT * NE], const("before"), r_mask, start=True, stop=True)
            mm(bank(1)[:, 0:NT * NE], ones[:], r_mask, start=True, stop=True).then_inc(count_done, 1)

            def turn_gathered(done):
                pe.wait_ge(gathered, done * 16 + 16)
                pe.wait_ge(hg_stored, done)
                for k in range(KC):
                    last = tr(bank2(2)[:, k * P:(k + 1) * P], xg[:, k * P:(k + 1) * P], ident)
                last.then_inc(xgT_done, 1)

            pe.wait_ge(slots_ready, 1)
            pe.wait_ge(o_free, NT)
            pe.wait_ge(av_free, NT)
            for buffer_free in (xgT_done, heT_done, y_done):
                pe.sem_inc(buffer_free, 1)
            turn_gathered(0)
            with pe.Fori(0, NE // 2) as i:
                for q in range(2):
                    first = pe.value_load(ts_i[0:1, bass.ds(i * 2 + q, 1)], min_val=0, max_val=MAX_TILES)
                    end = pe.value_load(ts_i[0:1, bass.ds(i * 2 + (q + 1), 1)], min_val=1, max_val=MAX_TILES)
                    for j in range(3):
                        pe.wait_ge(w_ready[q][j], i * 16 + 16)
                    pe.sem_inc(passed, 1)
                    w_g, w_u, w_d = exp_w[q]
                    with pe.Fori(first, end) as g:
                        pe.wait_ge(hg_stored, g + 1)
                        pe.wait_ge(silu_done, g + 1)
                        for k in range(KC):
                            last = mm(bank(0), hgT[:, k], w_g[:, k, :], start=(k == 0), stop=(k == KC - 1))
                        last.then_inc(gate_done, 1)
                        pe.wait_ge(he_ready, g + 1)
                        for k in range(KC):
                            last = mm(bank(1), hgT[:, k], w_u[:, k, :], start=(k == 0), stop=(k == KC - 1))
                        last.then_inc(up_done, 1)
                        turn_gathered(g + 1)
                        pe.wait_ge(he_ready, g + 2)
                        pe.wait_ge(heT_stored, g + 1)
                        for k in range(FK):
                            last = tr(bank(4)[:, k * P:(k + 1) * P], he[:, k * P:(k + 1) * P], ident)
                        last.then_inc(heT_done, 1)
                        pe.wait_ge(heT_stored, g + 2)
                        pe.wait_ge(y_stored, g + 1)
                        for half in range(2):
                            for k in range(FK):
                                last = mm(bank(5 + half), heT[:, k], w_d[:, k, half * H:(half + 1) * H],
                                          start=(k == 0), stop=(k == FK - 1))
                        last.then_inc(y_done, 1)


def table_of_constants():
    import numpy as np

    p = np.arange(P)
    inv = (np.float32(1.0) / np.float32(10000.0) ** (np.arange(0, DH, 2, dtype=np.float32) / np.float32(DH))).astype(np.float32)
    angle = (np.arange(S, dtype=np.float32)[:, None] * inv[None, :]).astype(np.float32).astype(np.float64)
    gamma = 1.0 - 2.0 ** (-5.0 - np.arange(RET_H))
    by_tile = lambda a: a.reshape(NT, P, 32).transpose(1, 0, 2).reshape(P, NT * 32)
    pair_head = 2 * np.arange(PAIRS)[None, :] + (p // DH)[:, None]
    parts = {
        "ident": np.eye(P),
        "causal": p[:, None] <= p[None, :],
        "neg_mask": np.where(p[None, :] <= p[:, None], 0.0, NEG),
        "before": p[:, None] < p[None, :],
        "cos": by_tile(np.cos(angle)),
        "sin": by_tile(np.sin(angle)),
        "v_decay": gamma[None, :] ** -(p[:, None] + 1.0),
        "q_decay": gamma[None, :] ** (p[:, None] + 1.0) * DH ** -0.5,
        "chunk_decay": gamma[pair_head] ** float(P),
        "lower": np.tile((np.arange(EPG)[None, :] < np.arange(EPG)[:, None]).reshape(1, -1), (P, 1)),
        "steps": np.tile(P * np.arange(1, NT)[None, :], (P, 1)),
    }
    return np.ascontiguousarray(np.concatenate([np.asarray(parts[n], np.float32) for n, _ in CONST_PARTS], axis=1))


_INS = ["x", "c", "w_ada", "b_ada", "w_in", "w_out", "lambda_q1", "lambda_k1", "lambda_q2", "lambda_k2", "diff_subln",
        "ln_mix_g", "ln_mix_b", "ln_ffn_g", "ln_ffn_b", "router_w", "router_b", "w_gate", "w_up", "w_down"]


def kernel(**inputs):
    import numpy as np
    import concourse.bacc as bacc
    from concourse.bass_utils import run_bass_kernel_spmd

    nc = bacc.Bacc("TRN2", target_bir_lowering=False, num_devices=1)
    arrays, args = {}, []
    tables = {"consts": table_of_constants(),
              "token_ids": np.ascontiguousarray(np.arange(S, dtype=np.int32).reshape(NT, P).T)}
    for name in _INS + ["consts", "token_ids"]:
        a = np.ascontiguousarray(inputs[name] if name in inputs else tables[name])
        arrays[f"in_{name}"] = a
        args.append(nc.dram_tensor(f"in_{name}", a.shape, mybir.dt.from_np(a.dtype), kind="ExternalInput").ap())
    out = nc.dram_tensor("out", (1, S, D), mybir.dt.float32, kind="ExternalOutput").ap()
    build(nc, *args, out)
    r = run_bass_kernel_spmd(nc, [arrays], core_ids=[0])
    return r.results[0]["out"]
```

```python
import math
from contextlib import ExitStack

import concourse.bass as bass
from concourse import mybir

P = 128
D = 1024
S = 1024
NT = S // P
KC = D // P
H = 512
RET_H, DH = 8, 64
PAIRS = RET_H // 2
DIFF_H = 4
NE, NG, EPG = 16, 4, 4
DE = 512
FK = DE // P
MAX_TILES = (2 * S + NE * (P - 1)) // P
IDX_TILES = MAX_TILES + 1
assert IDX_TILES == 1 << 5 and P == 1 << 7
ALPHA = 2.0 ** 0.25
YBUF = 4
EPS = 1e-5
NEG = -1e30
BIG = 8192.0
QUARTERS = 4
LAMBDA_INIT = 0.8 - 0.6 * math.exp(0.0)

CONST_PARTS = [("ident", P), ("causal", P), ("neg_mask", P), ("before", P), ("cos", NT * 32), ("sin", NT * 32),
               ("v_decay", RET_H), ("q_decay", RET_H), ("chunk_decay", PAIRS), ("lower", EPG * EPG), ("steps", NT - 1)]
CONST_AT = {}
_at = 0
for _n, _w in CONST_PARTS:
    CONST_AT[_n] = (_at, _at + _w)
    _at += _w
CONST_W = _at

RING = 3
RQ, RK, RV, RG, DQ, DK, DV = range(7)
BLOCKS = [("ada", 0), ("ada", 1), ("ada", 2), ("ada", 3), ("in", RQ), ("in", RK), ("ada", 6), ("in", RV), ("ada", 7),
          ("in", RG), ("ada", 8), ("in", DV), ("ada", 9), ("in", DQ), ("ada", 4), ("in", DK), ("ada", 5), ("ada", 10),
          ("ada", 11), ("out", 0), ("out", 1)]
ADA_ORDER = [b for k, b in BLOCKS if k == "ada"]


PROJ_ORDER = [b for k, b in BLOCKS if k == "in"]


def slot_use(kind, b):
    n = BLOCKS.index((kind, b))
    return n % RING, n // RING + 1


def build(nc, x, c, w_ada, b_ada, w_in, w_out, lq1, lk1, lq2, lk2, subln, mix_g, mix_b, ffn_g, ffn_b, router_w,
          router_b, w_gate, w_up, w_down, consts, token_ids, out):
    f32, f32r, i32 = mybir.dt.float32, mybir.dt.float32r, mybir.dt.int32
    ALU, ACT, AX = mybir.AluOpType, mybir.ActivationFunctionType, mybir.AxisListType

    z_rows = nc.dram_tensor("z_rows", (S, D), f32)
    slot_ids = nc.dram_tensor("slot_ids", (IDX_TILES * P, 1), i32)
    x1_rows = nc.dram_tensor("x1_rows", (S, D), f32)
    y_rows = nc.dram_tensor("y_rows", (MAX_TILES * P, D), f32)

    w_ada_v = w_ada[0].rearrange("(p k) n -> p k n", k=KC)
    w_in_v = w_in[0].rearrange("(k p) n -> p k n", p=P)
    w_out_v = w_out[0].rearrange("(k p) n -> p k n", p=P)
    x_v = x[0].rearrange("(t p) d -> p t d", p=P)
    out_v = out[0].rearrange("(t p) d -> p t d", p=P)

    with ExitStack() as ctx:
        def sb(name, shape, dt=f32):
            return ctx.enter_context(nc.sbuf_tensor(name, shape, dt))

        def sem(name):
            return ctx.enter_context(nc.semaphore(name))

        start_of = {}

        def region(name, shape):
            t = sb(name, shape)
            start_of[name] = nc.sbuf_base - 4 * math.prod(shape[1:])
            return t

        ring = [region(f"ring{i}", [P, KC, H]) for i in range(RING)]
        A = region("region_a", [P, 8192])
        B = region("region_b", [P, 8192])
        C = region("region_c", [P, 8192])
        M = region("region_m", [P, 8192])
        V = region("region_v", [P, 4096])

        def f32r_in(name, where, at, n):
            return nc.alloc_sbuf_tensor_at(name, [P, n], f32r, offset=start_of[where] + 4 * at)

        gate_w = [[f32r_in(f"gate{q}_{n}", w, at, 4096) for n, at in (("hi", a0), ("lo", a1))]
                  for q, (w, a0, a1) in enumerate((("region_b", 0, 4096), ("ring1", 0, 4096)))]
        up_w = [f32r_in(f"up_{n}", "region_m", at, 4096) for n, at in (("hi", 0), ("lo", 4096))]
        down_w = [f32r_in(f"down_{n}", "region_a", at, 4096) for n, at in (("hi", 0), ("lo", 4096))]
        hg_parts = [f32r_in(f"hg_{n}", "region_c", at, D) for n, at in (("hi", 2048), ("lo", 3072))]
        heT_parts = [f32r_in(f"heT_{n}", "region_c", at, DE) for n, at in (("hi", 5120), ("lo", 5632))]
        raw = [ring[0][:].rearrange("p k n -> p (k n)"), V[:]]
        cst = sb("cst", [P, CONST_W])
        ones = sb("ones", [P, P])
        g2b = sb("g2b", [P, D])
        b12 = sb("b12", [12, H])
        modcol = sb("modcol", [P, 4, KC])
        rw = sb("rw", [P, KC, NE])
        small = sb("small", [P, 224])
        ts_i = sb("ts_i", [1, NE + 1], i32)

        def const(name):
            a, b = CONST_AT[name]
            return cst[:, a:b]

        ident = const("ident")
        cos_t = const("cos").rearrange("p (t a) -> p t a", t=NT)
        sin_t = const("sin").rearrange("p (t a) -> p t a", t=NT)

        hT = A[:].rearrange("p (k s) -> p k s", k=KC)
        probs = A[:, 0:4096].rearrange("p (b c n) -> p b c n", b=2, c=2)
        aT = A[:, 4096:6144].rearrange("p (b n) -> p b n", b=2)
        x1 = A[:].rearrange("p (t d) -> p t d", t=NT)
        xn = B[:].rearrange("p (t d) -> p t d", t=NT)
        rqT = B[:, 0:4096].rearrange("p (c s) -> p c s", c=PAIRS)
        rkT = B[:, 4096:8192].rearrange("p (c s) -> p c s", c=PAIRS)
        dkT = rkT
        rk = C[:, 0:4096].rearrange("p (t n) -> p t n", t=NT)
        vs = C[:, 4096:8192].rearrange("p (t n) -> p t n", t=NT)
        g1b = C[:, 0:1024]
        dqT = [rqT, C[:, 1024:5120].rearrange("p (c s) -> p c s", c=DIFF_H)]
        xr = C[:, 1024:3072].rearrange("p (b d) -> p b d", b=2)
        u = C[:, 3072:5120].rearrange("p (b d) -> p b d", b=2)
        z = C[:, 5120:7168].rearrange("p (b d) -> p b d", b=2)
        mixT = [a.rearrange("p (k n) -> p k n", k=KC) for a in (C[:, 7168:8192], V[:, 3072:4096])]
        xg = C[:, 0:1024]
        hgf = C[:, 1024:2048]
        sg = C[:, 4096:4608]
        he = C[:, 4608:5120]
        yb = C[:, 6144:7168]
        idx_all = C[:, 7168:7168 + IDX_TILES].bitcast(i32)
        idx_cur = C[:, 7232:7233].bitcast(i32)
        tok_i = C[:, 7240:7240 + NT].bitcast(i32)
        rt = C[:, 4736:7168]
        x1_end = B[:].rearrange("p (t d) -> p t d", t=NT)
        ygath = M[:].rearrange("p (b j d) -> p b j d", b=YBUF, j=2)
        fin = A[:, 0:4096].rearrange("p (b d) -> p b d", b=YBUF)
        ret_out = M[:, 0:4096].rearrange("p (t n) -> p t n", t=NT)
        dif_out = M[:, 4096:8192].rearrange("p (t n) -> p t n", t=NT)
        t1 = M[:, 4096:4608]
        t2 = M[:, 4608:5120]
        qrot = M[:, 5120:6144].rearrange("p (b n) -> p b n", b=2)
        pm = M[:, 6144:7168].rearrange("p (r c n) -> p r c n", r=2, c=PAIRS)
        state = M[:, 7168:7424].rearrange("p (c e) -> p c e", c=PAIRS)
        state_new = M[:, 7424:7680].rearrange("p (c e) -> p c e", c=PAIRS)
        lamv = M[:, 7680:7936].rearrange("p (v n) -> p v n", v=4)
        dv = V[:].rearrange("p (t n) -> p t n", t=NT)
        ln_g, ln_b = V[:, 0:1024], V[:, 1024:2048]
        h2T = V[:, 2048:3072].rearrange("p (k n) -> p k n", k=KC)

        def cols(a, n):
            return small[:, a:a + n]

        eps_c = cols(0, 1)
        cond = cols(1, KC)
        craw = cols(9, KC)
        nlam = cols(17, 1)
        lam4 = cols(18, 4)
        stat = cols(22, 24).rearrange("p (b n) -> p b n", b=2)
        aggr = cols(46, 4).rearrange("p (b n) -> p b n", b=2)
        l_rstd, l_std, l_nb = cols(50, 2), cols(52, 2), cols(146, 2)
        z_stat = cols(150, 24).rearrange("p (b n) -> p b n", b=2)
        z_aggr = cols(174, 4).rearrange("p (b n) -> p b n", b=2)
        z_rstd, z_std, z_nb = cols(178, 2), cols(180, 2), cols(182, 2)
        hsum, hvar, hstd = cols(54, 8), cols(62, 8), cols(70, 8)
        negmax = cols(78, 4).rearrange("p (b n) -> p b n", b=2)
        zsum = cols(82, 4).rearrange("p (b n) -> p b n", b=2)
        zinv = cols(86, 4).rearrange("p (b n) -> p b n", b=2)
        r1 = cols(90, 8).rearrange("p (b n) -> p b n", b=2)
        ssq = cols(98, 32)
        r_spare = cols(206, 1)
        gates = cols(130, 2 * NT).rearrange("p (j t) -> p j t", j=2)
        router_bc = sb("router_bc", [P, NE])
        subg = sb("subg", [P, P])
        slot_i = sb("slot_i", [P, 2, NT], i32)
        id_at = sb("id_at", [P, 2, NT], i32)
        id_low = small[:, 190:190 + 2 * NT].bitcast(i32).rearrange("p (j t) -> p j t", j=2)

        psum = ctx.enter_context(nc.psum_tensor("psum", [P, 8, H], f32))

        def bank(i):
            return psum[:, i, :]

        def bank2(i):
            return psum[:, i:i + 2, :].rearrange("p b n -> p (b n)")

        sqt = C[:, 7168:7680]
        r_exp, r_prob = rt[:, 0:128], rt[:, 128:256]
        r_gt, r_eq = rt[:, 256:768], rt[:, 768:1280]
        r_rank, r_mask, r_tmp, r_tot = rt[:, 1280:1408], rt[:, 1408:1536], rt[:, 1536:1664], rt[:, 1664:1792]
        r_off = rt[:, 1792:1792 + (NT + 1) * NE]
        r_group, r_grank = rt[:, 1952:1984], rt[:, 1984:2016]
        r_row, r_lo, r_hi = rt[:, 2016:2024], rt[:, 2024:2032], rt[:, 2032:2040]
        r_tiles, r_start = rt[:, 2048:2064], rt[:, 2064:2081]

        slot_loaded = [sem(f"slot_loaded{i}") for i in range(RING)]
        consts_in, small_in, cond_ready, ones_ready = (
            sem("consts_in"), sem("small_in"), sem("cond_ready"), sem("ones_ready"))
        ada_summed, mod_done, mod_stored, var_ready = (
            sem("ada_summed"), sem("mod_done"), sem("mod_stored"), sem("var_ready"))
        std_ready, xn_ready, turned, hT_act = (
            sem("std_ready"), sem("xn_ready"), sem("turned"), sem("hT_act"))
        hT_dve, proj_done, rot_ready, rotT_done = (
            sem("hT_dve"), sem("proj_done"), sem("rot_ready"), sem("rotT_done"))
        rotT_stored, rs_done, rp_ready, ro_done = (
            sem("rotT_stored"), sem("rs_done"), sem("rp_ready"), sem("ro_done"))
        ro_free, kv_done, state_ready, rvar_ready = (
            sem("ro_free"), sem("kv_done"), sem("state_ready"), sem("rvar_ready"))
        rstd_ready, lam_sums, lam_exp, max_ready = (
            sem("rstd_ready"), sem("lam_sums"), sem("lam_exp"), sem("max_ready"))
        a_ready, aT_done, aT_stored, av_done = (
            sem("a_ready"), sem("aT_done"), sem("aT_stored"), sem("av_done"))
        ssq_ready, rms_std, ln_in, mix_ready = (
            sem("ssq_ready"), sem("rms_std"), sem("ln_in"), sem("mix_ready"))
        mixT_done, mixT_stored, o_done, o_free = (
            sem("mixT_done"), sem("mixT_stored"), sem("o_done"), sem("o_free"))
        ovar, ostd, orstd, un_ready = (
            sem("ovar"), sem("ostd"), sem("orstd"), sem("un_ready"))
        x1_ready, zvar, zstd, zrstd = (
            sem("x1_ready"), sem("zvar"), sem("zstd"), sem("zrstd"))
        z_ready, zT_done, h2_act, h2_dve = (
            sem("z_ready"), sem("zT_done"), sem("h2_act"), sem("h2_dve"))
        logits_done, lmax_ready, lexp_done, mask_ready = (
            sem("logits_done"), sem("lmax_ready"), sem("lexp_done"), sem("mask_ready"))
        count_done, ids_zeroed, slots_ready, ids_out = (
            sem("count_done"), sem("ids_zeroed"), sem("slots_ready"), sem("ids_out"))
        ids_in, idx_ready, tok_in, idx_zero = (
            sem("ids_in"), sem("idx_ready"), sem("tok_in"), sem("idx_zero"))
        starts_ready, gathered, xgT_done, hg_stored = (
            sem("starts_ready"), sem("gathered"), sem("xgT_done"), sem("hg_stored"))
        gate_done, up_done, silu_done, he_ready = (
            sem("gate_done"), sem("up_done"), sem("silu_done"), sem("he_ready"))
        heT_done, heT_stored, y_done, y_stored = (
            sem("heT_done"), sem("heT_stored"), sem("y_done"), sem("y_stored"))
        y_out, yg_free, fvar, fstd = (
            sem("y_out"), sem("yg_free"), sem("fvar"), sem("fstd"))
        frstd, fn_ready, ffn_in, dve_step = (
            sem("frstd"), sem("fn_ready"), sem("ffn_in"), sem("dve_step"))
        pool_step = (
            sem("pool_step"))
        av_free = sem("av_free")
        y_zeroed = sem("y_zeroed")
        passed = sem("passed")
        dq_zeroed = sem("dq_zeroed")
        x_in = [sem(f"x_in{i}") for i in range(NT)]
        proj_free = [sem(f"proj_free{i}") for i in range(2)]
        s_done = [sem(f"s_done{i}") for i in range(2)]
        exp_done = [sem(f"exp_done{i}") for i in range(2)]
        xr_in = [sem(f"xr_in{i}") for i in range(2)]
        z_out = [sem(f"z_out{i}") for i in range(2)]
        raw_in = [[sem(f"raw_in{i}_{k}") for k in range(QUARTERS)] for i in range(2)]
        hi_ready, lo_ready = sem("hi_ready"), sem("lo_ready")
        hg_act, hg_dve, hg_hi_ready, heT_hi_ready = sem("hg_act"), sem("hg_dve"), sem("hg_hi_ready"), sem("heT_hi_ready")
        x1_out, x1_in = sem("x1_out"), sem("x1_in")
        y_in = [[sem(f"y_in{b}{j}") for j in range(2)] for b in range(YBUF)]
        out_done = [sem(f"out_done{i}") for i in range(YBUF)]
        xn_inv = sem("xn_inv")
        x1_scaled, y1_scaled, gained, biased = sem("x1_scaled"), sem("y1_scaled"), sem("gained"), sem("biased")

        block = ctx.enter_context(nc.Block())

        he_half = (slice(0, DE // 2), slice(DE // 2, DE))

        def quarter(k):
            return slice(k * 1024, (k + 1) * 1024)

        def block_no(i, q, j):
            return i * 6 + (3 * q + j)

        def split_count(i, q, j, quarters):
            return block_no(i, q, j) * QUARTERS + quarters

        def raw_count(i, q, j):
            n = 3 * q + j
            return n % 2, i * 48 + 16 * (n // 2 + 1)

        def bc(ap, shape, at):
            for d in at:
                ap = ap.unsqueeze(d)
            return ap.broadcast_to(shape)

        def wait_nonzero(engine, semaphore, count):
            if count > 0:
                engine.wait_ge(semaphore, count)

        def keys(qb):
            return (qb + 1) * P

        def mod_bank(b):
            return bank(2 if b in (0, 1, 2, 3, 6, 7, 8, 9, 4) else 7)

        def used_up(kind, b):
            if kind == "ada":
                return mod_done, ADA_ORDER.index(b) + 1
            if kind == "in":
                return proj_done, NT * (PROJ_ORDER.index(b) + 1)
            return o_done, NT

        @block.sync
        def _(sp):
            for n, (kind, b) in enumerate(BLOCKS):
                s, _ = slot_use(kind, b)
                if n >= RING:
                    sp.wait_ge(*used_up(*BLOCKS[n - RING]))
                src = {"ada": w_ada_v, "in": w_in_v, "out": w_out_v}[kind][:, :, b * H:(b + 1) * H]
                sp.dma_start(ring[s][:], src).then_inc(slot_loaded[s], 16)

            def load_raw(e, j, parity, after=None):
                src = (w_gate, w_up, w_down)[j][0][bass.ds(e, 1)].rearrange("o (k p) n -> p (o k) n", p=P)
                chunks = (FK if j == 2 else KC) // QUARTERS
                for k in range(QUARTERS):
                    if after:
                        sp.wait_ge(lo_ready, after(k))
                    dst = raw[parity][:, quarter(k)].rearrange("p (k n) -> p k n", k=chunks)
                    sp.dma_start(dst, src[:, k * chunks:(k + 1) * chunks]).then_inc(raw_in[parity][k], 16)

            sp.wait_ge(mod_done, len(ADA_ORDER))
            load_raw(0, 0, 0)
            sp.wait_ge(x1_out, 16 * NT)
            sp.wait_ge(x1_ready, NT)
            sp.wait_ge(o_done, NT)
            sp.wait_ge(logits_done, NT)
            load_raw(0, 1, 1)
            load_raw(0, 2, 0, after=lambda k: k + 1)

            def load_next(i, q):
                for j in range(3):
                    load_raw((i * 2 + (q + 1)).with_bounds(min_val=1, max_val=NE - 1), j, (3 * (q + 1) + j) % 2,
                             after=lambda k: split_count(i, q, 1 + j, k + 1))

            def store_y(g):
                sp.wait_ge(y_stored, g + 2)
                sp.dma_start(y_rows.ap()[bass.ds(g * P, P), :], yb).then_inc(y_out, 16)

            sp.wait_ge(starts_ready, 1)
            sp.sem_inc(y_out, 16)
            with sp.Fori(0, NE // 2) as i:
                for q in range(2):
                    first = sp.value_load(ts_i[0:1, bass.ds(i * 2 + q, 1)], min_val=0, max_val=MAX_TILES - 1)
                    end = sp.value_load(ts_i[0:1, bass.ds(i * 2 + (q + 1), 1)], min_val=1, max_val=MAX_TILES)
                    if q == 0:
                        load_next(i, q)
                    else:
                        with sp.If(i < NE // 2 - 1):
                            load_next(i, q)
                        with sp.If(i > NE // 2 - 2):
                            sp.wait_ge(y_done, first + 1)
                            sp.dma_start(x1_end, x1_rows.ap().rearrange("(t p) d -> p t d", p=P)).then_inc(x1_in, 16)
                    store_y(first)
                    with sp.If(first + 1 < end):
                        with sp.Fori(first + 1, end) as g:
                            store_y(g)
            for t in range(NT):
                sp.wait_ge(biased, t + 1)
                sp.dma_start(out_v[:, t], fin[:, t % YBUF]).then_inc(out_done[t % YBUF], 16)
            for b in range(YBUF):
                sp.wait_ge(out_done[b], 16 * NT // YBUF)

        @block.gpsimd
        def _(pool):
            pool.dma_start(craw, c.rearrange("o (p k) -> (o p) k", k=KC)).then_inc(small_in, 16)
            pool.dma_start(cst[:], consts).then_inc(consts_in, 16)
            pool.dma_start(b12[:], b_ada[0].rearrange("(b n) -> b n", n=H)).then_inc(small_in, 16)
            for i, v in enumerate((lq1, lk1, lq2, lk2)):
                pool.dma_start(lamv[:, i, :], v[0].partition_broadcast(P)).then_inc(small_in, 16)
            pool.dma_start(subg[:], subln[0].partition_broadcast(P)).then_inc(small_in, 16)
            pool.dma_start(rw[:], router_w.rearrange("(k p) e -> p k e", p=P)).then_inc(small_in, 16)
            pool.dma_start(router_bc[:], router_b.partition_broadcast(P)).then_inc(small_in, 16)

            pool.memset(g2b[:], 0.0).then_inc(pool_step, 1)
            pool.wait_ge(pool_step, 1)
            for g in range(NE, MAX_TILES):
                pool.dma_start(y_rows.ap()[g * P:(g + 1) * P, :], g2b[:]).then_inc(y_zeroed, 16)
            pool.wait_ge(rs_done, NT)
            pool.wait_ge(ro_done, NT)
            pool.memset(dqT[0][DH:P], 0.0).then_inc(dq_zeroed, 1)
            pool.memset(dqT[1][0:DH], 0.0).then_inc(dq_zeroed, 1)
            pool.wait_ge(av_done, NT * DIFF_H)
            pool.dma_start(ln_g, mix_g[0].partition_broadcast(P)).then_inc(ln_in, 16)
            pool.dma_start(ln_b, mix_b[0].partition_broadcast(P)).then_inc(ln_in, 16)
            pool.wait_ge(ln_in, 32)
            for t in range(NT):
                pool.wait_ge(un_ready, t + 1)
                pool.tensor_tensor(x1[:, t], u[:, t % 2], ln_g, ALU.mult).then_inc(pool_step, 1)
                pool.wait_ge(pool_step, t + 2)
                pool.tensor_tensor(x1[:, t], x1[:, t], ln_b, ALU.add).then_inc(x1_ready, 1)

            pool.wait_ge(x1_ready, NT)
            pool.memset(idx_all, 0).then_inc(idx_zero, 1)
            pool.wait_ge(idx_zero, 1)
            pool.dma_start(slot_ids.ap().rearrange("(p g) o -> p (g o)", p=P), idx_all).then_inc(ids_zeroed, 16)
            pool.dma_start(tok_i, token_ids).then_inc(tok_in, 16)
            pool.wait_ge(ids_zeroed, 16)
            pool.wait_ge(tok_in, 16)
            pool.wait_ge(slots_ready, 1)
            for t in range(NT):
                for j in range(2):
                    pool.indirect_dma_start(slot_ids.ap(), bass.IndirectOffsetOnAxis(ap=id_at[:, j, t:t + 1], axis=0),
                                            tok_i[:, t:t + 1], None).then_inc(ids_out, 16)
            pool.wait_ge(ids_out, 16 * 2 * NT)
            pool.dma_start(idx_all, slot_ids.ap().rearrange("(p g) o -> p (g o)", p=P)).then_inc(ids_in, 16)
            pool.wait_ge(ids_in, 16)
            pool.wait_ge(starts_ready, 1)
            total = pool.value_load(ts_i[0:1, NE:NE + 1], min_val=NE, max_val=MAX_TILES)
            def gather(g):
                pool.wait_ge(xgT_done, g + 1)
                pool.tensor_copy(idx_cur, idx_all[:, bass.ds(g, 1)]).then_inc(idx_ready, 1)
                pool.wait_ge(idx_ready, g + 1)
                pool.sem_inc(passed, 1)
                pool.indirect_dma_start(xg, None, z_rows.ap(),
                                        bass.IndirectOffsetOnAxis(ap=idx_cur, axis=0)).then_inc(gathered, 16)
                pool.wait_ge(gathered, g * 16 + 16)

            with pool.Fori(0, total + 1) as g:
                gather(g)

            pool.wait_ge(lo_ready, 3 * NE * QUARTERS)
            pool.dma_start(ln_g, ffn_g[0].partition_broadcast(P)).then_inc(ffn_in, 16)
            pool.dma_start(ln_b, ffn_b[0].partition_broadcast(P)).then_inc(ffn_in, 16)
            pool.wait_ge(y_out, total * 16 + 16)
            pool.sem_inc(passed, 1)

            def gain(t):
                pool.wait_ge(fn_ready, t + 1)
                pool.tensor_tensor(fin[:, t % YBUF], fin[:, t % YBUF], ln_g, ALU.mult).then_inc(gained, 1)

            for t in range(NT):
                if t >= YBUF:
                    pool.wait_ge(yg_free, t - YBUF + 1)
                for j in range(2):
                    pool.indirect_dma_start(ygath[:, t % YBUF, j], None, y_rows.ap(),
                                            bass.IndirectOffsetOnAxis(ap=slot_i[:, j, t:t + 1], axis=0)
                                            ).then_inc(y_in[t % YBUF][j], 16)
                if t == 0:
                    pool.wait_ge(ffn_in, 32)
                if t >= 3:
                    gain(t - 3)
            for t in range(NT - 3, NT):
                gain(t)

        @block.scalar
        def _(act):
            for t in range(NT):
                act.dma_start(xn[:, t], x_v[:, t]).then_inc(x_in[t], 16)
            act.wait_ge(small_in, 144)
            nc.scalar.activation(cond, craw, ACT.Silu).then_inc(cond_ready, 1)
            act.wait_ge(lam_sums, 1)
            nc.scalar.activation(lam4[:, 2:4], lam4[:, 0:2], ACT.Exp).then_inc(lam_exp, 1)
            for t in range(NT):
                b = t % 2
                act.wait_ge(var_ready, t + 1)
                nc.scalar.activation(l_std[:, b:b + 1], aggr[:, b, 1:2], ACT.Sqrt, bias=eps_c).then_inc(std_ready, 1)
                act.wait_ge(xn_inv, t + 1)
                nc.scalar.activation(xn[:, t], xn[:, t], ACT.Identity, scale=l_rstd[:, b:b + 1], bias=l_nb[:, b:b + 1]
                                     ).then_inc(xn_ready, 1)
            act.wait_ge(mod_stored, 4)
            for t in range(NT):
                act.wait_ge(turned, 2 * t + 1)
                for k in range(4):
                    last = nc.scalar.activation(hT[:, k, t * P:(t + 1) * P], bank((2 * t) % 4)[:, k * P:(k + 1) * P],
                                                ACT.Identity, scale=modcol[:, 1, k:k + 1], bias=modcol[:, 0, k:k + 1])
                last.then_inc(hT_act, 1)
            for i in range(2 * NT):
                t = i % NT
                act.wait_ge(rotT_done, i + 1)
                nc.scalar.activation((rqT, rkT)[i // NT][:, :, t * P:(t + 1) * P],
                                     bank(3 + i % 2).rearrange("p (c n) -> p c n", c=PAIRS), ACT.Copy
                                     ).then_inc(rotT_stored, 1)

            def from_projection(g, dst, func=ACT.Copy, scale=1.0):
                act.wait_ge(proj_done, g + 1)
                nc.scalar.activation(dst, bank(g % 2), func, scale=scale).then_inc(proj_free[g % 2], 1)

            for t in range(NT):
                from_projection(3 * NT + t, ret_out[:, t], ACT.Silu)
            for n in range(NT):
                from_projection(4 * NT + n, dv[:, n])
                act.wait_ge(rvar_ready, n + 1)
                nc.scalar.activation(hstd, hvar, ACT.Sqrt, bias=eps_c, scale=1.0 / DH).then_inc(rstd_ready, 1)
            for j in range(NT):
                g = 5 * NT + j
                act.wait_ge(proj_done, g + 1)
                for q in range(2):
                    rows = slice(q * DH, (q + 1) * DH)
                    last = nc.scalar.activation(dqT[q][rows, j // 2, (j % 2) * H:(j % 2 + 1) * H], bank(g % 2)[rows, :],
                                                ACT.Copy, scale=DH ** -0.5)
                last.then_inc(proj_free[g % 2], 1)
            for j in range(NT):
                from_projection(6 * NT + j, dkT[:, j // 2, (j % 2) * H:(j % 2 + 1) * H])

            def exps(i):
                for q in range(2):
                    act.wait_ge(max_ready, 2 * i + q + 1)
                    if i >= 2:
                        act.wait_ge(aT_done, i - 1)
                    nc.scalar.activation(probs[:, i % 2, q, 0:keys(i // DIFF_H)], bank2(2 * q)[:, 0:keys(i // DIFF_H)],
                                         ACT.Exp, bias=negmax[:, i % 2, q:q + 1], accum_out=zsum[:, i % 2, q:q + 1]
                                         ).then_inc(exp_done[q], 1)

            def store_turned(i):
                act.wait_ge(aT_done, i + 1)
                if i >= 2:
                    act.wait_ge(av_done, i - 1)
                nc.scalar.activation(aT[:, i % 2, 0:keys(i // DIFF_H)], bank2(4)[:, 0:keys(i // DIFF_H)], ACT.Copy
                                     ).then_inc(aT_stored, 1)

            for i in range(NT * DIFF_H):
                if i >= 2:
                    store_turned(i - 2)
                exps(i)
            store_turned(NT * DIFF_H - 2)
            store_turned(NT * DIFF_H - 1)
            act.wait_ge(ssq_ready, NT)
            nc.scalar.activation(ssq, ssq, ACT.Sqrt, bias=eps_c, scale=1.0 / P).then_inc(rms_std, 1)

            def store_mixT(t):
                act.wait_ge(mixT_done, t + 1)
                if t >= 2:
                    act.wait_ge(o_done, t - 1)
                nc.scalar.activation(mixT[t % 2], bank2(0).rearrange("p (k n) -> p k n", k=KC), ACT.Copy
                                     ).then_inc(mixT_stored, 1)

            def mixed(t):
                b = t % 2
                if t == 0:
                    for n in range(2):
                        act.dma_start(xr[:, n], x_v[:, n]).then_inc(xr_in[n], 16)
                elif t + 1 < NT:
                    wait_nonzero(act, ovar, t)
                    act.dma_start(xr[:, (t + 1) % 2], x_v[:, t + 1]).then_inc(xr_in[(t + 1) % 2], 16)
                act.wait_ge(ovar, t + 1)
                nc.scalar.activation(l_std[:, b:b + 1], aggr[:, b, 1:2], ACT.Sqrt, bias=eps_c).then_inc(ostd, 1)
                act.wait_ge(orstd, t + 1)
                nc.scalar.activation(u[:, b], u[:, b], ACT.Identity, scale=l_rstd[:, b:b + 1], bias=l_nb[:, b:b + 1]
                                     ).then_inc(un_ready, 1)

            def renormed(t):
                b = t % 2
                act.wait_ge(zvar, t + 1)
                nc.scalar.activation(z_std[:, b:b + 1], z_aggr[:, b, 1:2], ACT.Sqrt, bias=eps_c).then_inc(zstd, 1)
                act.wait_ge(zrstd, t + 1)
                if t >= 2:
                    act.wait_ge(z_out[b], 16 * (t // 2))
                    act.wait_ge(zT_done, t - 1)
                nc.scalar.activation(z[:, b], x1[:, t], ACT.Identity, scale=z_rstd[:, b:b + 1], bias=z_nb[:, b:b + 1]
                                     ).then_inc(z_ready, 1)
                act.wait_ge(z_ready, t + 1)
                nc.scalar.activation(x1[:, t], x1[:, t], ACT.Copy, scale=ALPHA).then_inc(x1_scaled, 1)
                act.dma_start(z_rows.ap()[t * P:(t + 1) * P, :], z[:, b]).then_inc(z_out[b], 16)
                act.wait_ge(x1_scaled, t + 1)
                act.dma_start(x1_rows.ap()[t * P:(t + 1) * P, :], x1[:, t]).then_inc(x1_out, 16)

            def modulated(t):
                act.wait_ge(zT_done, t + 1)
                wait_nonzero(act, logits_done, t)
                for k in range(4):
                    last = nc.scalar.activation(h2T[:, k], bank(4)[:, k * P:(k + 1) * P], ACT.Identity,
                                                scale=modcol[:, 3, k:k + 1], bias=modcol[:, 2, k:k + 1])
                last.then_inc(h2_act, 1)

            def split_hi(dst, parity, loaded, quarters=range(QUARTERS)):
                for k in quarters:
                    act.wait_ge(raw_in[parity][k], loaded)
                    nc.scalar.activation(dst[:, quarter(k)], raw[parity][:, quarter(k)], ACT.Copy).then_inc(hi_ready, 1)

            store_mixT(0)
            for t in range(NT + 2):
                if 2 <= t < 2 + QUARTERS:
                    split_hi(gate_w[0][0], 0, 16, [t - 2])
                if t + 1 < NT:
                    store_mixT(t + 1)
                if t >= 2:
                    modulated(t - 2)
                if t < NT:
                    mixed(t)
                if 1 <= t <= NT:
                    renormed(t - 1)
            act.wait_ge(lmax_ready, 1)
            nc.scalar.activation(r_exp, r_exp, ACT.Exp).then_inc(lexp_done, 1)

            def modulate_gathered(g):
                for k in range(4):
                    last = nc.scalar.activation(hgf[:, k * P:(k + 1) * P], bank(2)[:, k * P:(k + 1) * P],
                                                ACT.Identity, scale=modcol[:, 3, k:k + 1], bias=modcol[:, 2, k:k + 1])
                last.then_inc(hg_act, 1)
                act.wait_ge(hg_act, g + 1)
                act.wait_ge(hg_dve, g + 1)
                nc.scalar.activation(hg_parts[0][:], hgf, ACT.Copy).then_inc(hg_hi_ready, 1)

            def expert_tile(g, first=None, i=None, q=None):
                if first is not None:
                    nc.scalar.activation(r_spare, eps_c, ACT.Silu)
                    act.wait_ge(up_done, first + 1)
                    split_hi(up_w[0], *raw_count(i, q, 1))
                act.wait_ge(gate_done, g + 1)
                act.wait_ge(he_ready, g * 2 + 2)
                nc.scalar.activation(sg, bank(0), ACT.Silu).then_inc(silu_done, 1)
                if first is not None:
                    act.wait_ge(y_done, first + 1)
                    split_hi(down_w[0], *raw_count(i, q, 2))
                act.wait_ge(y_done, g + 1)
                for r in range(2):
                    act.wait_ge(heT_done, g * 2 + (3 + r))
                    nc.scalar.activation(heT_parts[0][:, he_half[r]], bank((4, 7)[r])[:, 0:DE // 2], ACT.Copy
                                         ).then_inc(heT_hi_ready, 1)
                act.wait_ge(xgT_done, g + 3)
                act.wait_ge(hg_stored, g + 1)
                modulate_gathered(g + 1)
                if first is not None:
                    def split_next_gate():
                        split_hi(gate_w[1 - q][0], *raw_count(i, q, 3))
                    if q == 0:
                        split_next_gate()
                    else:
                        with act.If(i < NE // 2 - 1):
                            split_next_gate()
            act.wait_ge(starts_ready, 1)
            act.sem_inc(silu_done, 1)
            act.wait_ge(x1_out, 16 * NT)
            act.wait_ge(xgT_done, 2)
            modulate_gathered(0)
            with act.Fori(0, NE // 2) as i:
                for q in range(2):
                    first = act.value_load(ts_i[0:1, bass.ds(i * 2 + q, 1)], min_val=0, max_val=MAX_TILES - 1)
                    end = act.value_load(ts_i[0:1, bass.ds(i * 2 + (q + 1), 1)], min_val=1, max_val=MAX_TILES)
                    expert_tile(first, first, i, q)
                    with act.If(first + 1 < end):
                        with act.Fori(first + 1, end) as g:
                            expert_tile(g)

            def weigh(t):
                y1 = ygath[:, t % YBUF, 1]
                act.wait_ge(y_in[t % YBUF][1], 16 * (t // YBUF + 1))
                nc.scalar.activation(y1, y1, ACT.Copy, scale=gates[:, 1, t:t + 1]).then_inc(y1_scaled, 1)

            weigh(0)
            for t in range(NT):
                b = t % 2
                if t + 1 < NT:
                    weigh(t + 1)
                act.wait_ge(fvar, t + 1)
                nc.scalar.activation(l_std[:, b:b + 1], aggr[:, b, 1:2], ACT.Sqrt, bias=eps_c).then_inc(fstd, 1)
                act.wait_ge(frstd, t + 1)
                if t >= YBUF:
                    act.wait_ge(out_done[t % YBUF], 16 * (t // YBUF))
                nc.scalar.activation(fin[:, t % YBUF], x1_end[:, t], ACT.Identity, scale=l_rstd[:, b:b + 1],
                                     bias=l_nb[:, b:b + 1]).then_inc(fn_ready, 1)

        @block.vector
        def _(dve):
            steps = [0]

            def link(ins):
                steps[0] += 1
                ins.then_inc(dve_step, 1)
                dve.wait_ge(dve_step, steps[0])

            def mark(ins):
                steps[0] += 1
                ins.then_inc(dve_step, 1)

            def wait_marks():
                dve.wait_ge(dve_step, steps[0])

            def statistics(src, st, ag, ready):
                mark(nc.vector.bn_stats(st[:, 0:6], src[:, 0:H]))
                mark(nc.vector.bn_stats(st[:, 6:12], src[:, H:D]))
                wait_marks()
                nc.vector.bn_aggr(ag, st.rearrange("p (s n) -> p s n", s=2)).then_inc(ready, 1)

            def invert(sd, ag, rs, nb, ready):
                link(nc.vector.reciprocal(rs, sd))
                nc.vector.tensor_scalar(nb, ag[:, 0:1], rs, -1.0, ALU.mult, ALU.mult).then_inc(ready, 1)

            mark(nc.vector.memset(eps_c, EPS))
            mark(nc.vector.memset(state, 0.0))
            nc.vector.memset(ones[:], 1.0).then_inc(ones_ready, 1)
            wait_marks()
            dve.wait_ge(small_in, 144)
            for i in range(2):
                link(nc.vector.tensor_tensor(lamv[:, 2 * i, :], lamv[:, 2 * i, :], lamv[:, 2 * i + 1, :], ALU.mult))
                ins = nc.vector.tensor_reduce(lam4[:, i:i + 1], lamv[:, 2 * i, :], AX.X, ALU.add)
                if i == 0:
                    mark(ins)
            ins.then_inc(lam_sums, 1)
            mark(nc.vector.tensor_scalar(subg[:], subg[:], 1.0 - LAMBDA_INIT, None, ALU.mult))
            dve.wait_ge(lam_exp, 1)
            link(nc.vector.tensor_tensor(nlam, lam4[:, 3:4], lam4[:, 2:3], ALU.subtract))
            mark(nc.vector.tensor_scalar(nlam, nlam, -LAMBDA_INIT, None, ALU.add))
            dve.wait_ge(cond_ready, 1)

            def ada_sum(b):
                s, uses = slot_use("ada", b)
                w = ring[s]
                dve.wait_ge(slot_loaded[s], 16 * uses)
                link(nc.vector.tensor_scalar(w[:, 0, :], w[:, 0, :], cond[:, 0:1], None, ALU.mult))
                for k in range(1, KC):
                    ins = nc.vector.scalar_tensor_tensor(out=w[:, 0, :], in0=w[:, k, :], scalar=cond[:, k:k + 1],
                                                         in1=w[:, 0, :], op0=ALU.mult, op1=ALU.add)
                    if k < KC - 1:
                        link(ins)
                ins.then_inc(ada_summed, 1)

            def mod_store(b):
                dve.wait_ge(mod_done, ADA_ORDER.index(b) + 1)
                vec, half = b // 2, b % 2
                if vec in (2, 5):
                    dst = (g1b if vec == 2 else g2b[:, :])[:, half * H:(half + 1) * H]
                    nc.vector.tensor_copy(dst, mod_bank(b)).then_inc(mod_stored, 1)
                else:
                    at, one = {0: (0, 0.0), 1: (1, 1.0), 3: (2, 0.0), 4: (3, 1.0)}[vec]
                    nc.vector.tensor_scalar(modcol[:, at, half * 4:half * 4 + 4], mod_bank(b)[:, 0:4], one, None,
                                            ALU.add).then_inc(mod_stored, 1)

            for m in range(4):
                ada_sum(m)
                for t in (2 * m, 2 * m + 1):
                    dve.wait_ge(x_in[t], 16)
                    statistics(xn[:, t], stat[:, t % 2], aggr[:, t % 2], var_ready)
                for t in (2 * m, 2 * m + 1):
                    dve.wait_ge(std_ready, t + 1)
                    if t >= 2:
                        dve.wait_ge(xn_ready, t - 1)
                    invert(l_std[:, t % 2:t % 2 + 1], aggr[:, t % 2], l_rstd[:, t % 2:t % 2 + 1], l_nb[:, t % 2:t % 2 + 1],
                           xn_inv)
                mod_store(m)
            dve.wait_ge(mod_stored, 4)
            for t in range(NT):
                dve.wait_ge(turned, 2 * t + 2)
                for k in range(4, KC):
                    last = nc.vector.tensor_scalar(hT[:, k, t * P:(t + 1) * P],
                                                   bank((2 * t + 1) % 4)[:, (k - 4) * P:(k - 3) * P],
                                                   modcol[:, 1, k:k + 1], modcol[:, 0, k:k + 1], ALU.mult, ALU.add)
                last.then_inc(hT_dve, 1)

            dve.wait_ge(consts_in, 16)
            for i in range(2 * NT):
                t = i % NT
                dve.wait_ge(proj_done, i + 1)
                v = bank(i % 2).rearrange("p (h a d) -> p h a d", h=RET_H, a=2)
                ta = t1.rearrange("p (h a d) -> p h a d", h=RET_H, a=2)
                tb = t2.rearrange("p (h a d) -> p h a d", h=RET_H, a=2)
                sin_b = bc(sin_t[:, t], [P, RET_H, 32], (1,))
                wait_marks()
                wait_nonzero(dve, rot_ready, i)
                mark(nc.vector.tensor_tensor(ta, v, bc(cos_t[:, t], [P, RET_H, 2, 32], (1, 1)), ALU.mult))
                mark(nc.vector.tensor_tensor(tb[:, :, 0], v[:, :, 1], sin_b, ALU.mult))
                nc.vector.tensor_tensor(tb[:, :, 1], v[:, :, 0], sin_b, ALU.mult).then_inc(proj_free[i % 2], 1)
                wait_marks()
                dve.wait_ge(proj_free[i % 2], i // 2 + 1)
                if 2 <= i < NT:
                    dve.wait_ge(rotT_done, i - 1)
                dst = (qrot[:, t % 2] if i < NT else rk[:, t]).rearrange("p (h a d) -> p h a d", h=RET_H, a=2)
                mark(nc.vector.tensor_tensor(dst[:, :, 0], ta[:, :, 0], tb[:, :, 0], ALU.subtract))
                nc.vector.tensor_tensor(dst[:, :, 1], ta[:, :, 1], tb[:, :, 1], ALU.add).then_inc(rot_ready, 1)
            ada_sum(6)
            for t in range(NT):
                g = 2 * NT + t
                dve.wait_ge(proj_done, g + 1)
                nc.vector.tensor_tensor(vs[:, t].rearrange("p (h d) -> p h d", h=RET_H),
                                        bank(g % 2).rearrange("p (h d) -> p h d", h=RET_H),
                                        bc(const("v_decay"), [P, RET_H, DH], (2,)), ALU.mult
                                        ).then_inc(proj_free[g % 2], 1)
                if t == 4:
                    mod_store(6)
            ada_sum(7)
            mod_store(7)
            ada_sum(8)

            q_dec = const("q_decay").rearrange("p (c r) -> p c r", r=2)
            dve.wait_ge(rot_ready, 2 * NT)
            for n in range(NT):
                dve.wait_ge(rs_done, n + 1)
                wait_nonzero(dve, ro_done, n)
                mark(nc.vector.tensor_tensor(pm[:, 0], bank(3).rearrange("p (c n) -> p c n", c=PAIRS),
                                             bc(const("causal"), [P, PAIRS, P], (1,)), ALU.mult))
                nc.vector.tensor_tensor(pm[:, 1], bank(4).rearrange("p (c n) -> p c n", c=PAIRS),
                                        bc(const("causal"), [P, PAIRS, P], (1,)), ALU.mult).then_inc(rp_ready, 1)
                if n == 4:
                    mod_store(8)
                dve.wait_ge(ro_done, n + 1)
                o = t1.rearrange("p (c r d) -> p c r d", c=PAIRS, r=2)
                oh = t1.rearrange("p (h d) -> p h d", h=RET_H)
                xc = t2.rearrange("p (h d) -> p h d", h=RET_H)
                sq = qrot[:, 0].rearrange("p (h d) -> p h d", h=RET_H)
                wait_marks()
                for r in range(2):
                    ins = nc.vector.tensor_tensor(o[:, :, r], bank(5 + r)[:, 0:PAIRS * DH].rearrange("p (c d) -> p c d", c=PAIRS),
                                                  bc(q_dec[:, :, r], [P, PAIRS, DH], (2,)), ALU.mult)
                    if r == 0:
                        mark(ins)
                ins.then_inc(ro_free, 1)
                if n < NT - 1:
                    dve.wait_ge(kv_done, n + 1)
                    kv = bank(7).rearrange("p (c n) -> p c n", c=PAIRS)
                    mark(nc.vector.tensor_tensor(state_new[0:DH], kv[0:DH, :, 0:DH], state[0:DH], ALU.add))
                    mark(nc.vector.tensor_tensor(state_new[DH:P], kv[DH:P, :, DH:P], state[DH:P], ALU.add))
                    wait_marks()
                    nc.vector.tensor_tensor(state, state_new, bc(const("chunk_decay"), [P, PAIRS, DH], (2,)), ALU.mult
                                            ).then_inc(state_ready, 1)
                    dve.wait_ge(state_ready, n + 1)
                wait_marks()
                dve.wait_ge(ro_free, n + 1)
                link(nc.vector.tensor_reduce(hsum, oh, AX.X, ALU.add))
                link(nc.vector.tensor_scalar(hsum, hsum, 1.0 / DH, None, ALU.mult))
                link(nc.vector.tensor_tensor(xc, oh, bc(hsum, [P, RET_H, DH], (2,)), ALU.subtract))
                link(nc.vector.tensor_tensor(sq, xc, xc, ALU.mult))
                nc.vector.tensor_reduce(hvar, sq, AX.X, ALU.add).then_inc(rvar_ready, 1)
                dve.wait_ge(rstd_ready, n + 1)
                link(nc.vector.reciprocal(hstd, hstd))
                link(nc.vector.tensor_tensor(xc, xc, bc(hstd, [P, RET_H, DH], (2,)), ALU.mult))
                if n == 0:
                    dve.wait_ge(proj_free[0], 4 * NT // 2)
                    dve.wait_ge(proj_free[1], 4 * NT // 2)
                mark(nc.vector.tensor_tensor(ret_out[:, n], t2, ret_out[:, n], ALU.mult))
            for b in (9, 4, 5, 10):
                ada_sum(b)
                if b == 10:
                    dve.wait_ge(y_zeroed, 16 * (MAX_TILES - NE))
                mod_store(b)

            def maxima(i):
                for q in range(2):
                    dve.wait_ge(s_done[q], i + 1)
                    nc.vector.tensor_reduce(negmax[:, i % 2, q:q + 1], bank2(2 * q)[:, 0:keys(i // DIFF_H)], AX.X, ALU.max,
                                            negate=True).then_inc(max_ready, 1)

            def combine(i):
                b, qb, h = i % 2, i // DIFF_H, i % DIFF_H
                dve.wait_ge(exp_done[0], i + 1)
                dve.wait_ge(exp_done[1], i + 1)
                link(nc.vector.reciprocal(zinv[:, b], zsum[:, b]))
                mark(nc.vector.tensor_copy(r1[:, qb % 2, h:h + 1], zinv[:, b, 0:1]))
                link(nc.vector.scalar_tensor_tensor(out=zinv[:, b, 1:2], in0=zinv[:, b, 1:2], scalar=zsum[:, b, 0:1],
                                                    in1=nlam, op0=ALU.mult, op1=ALU.mult))
                nc.vector.scalar_tensor_tensor(out=probs[:, b, 0, 0:keys(qb)], in0=probs[:, b, 1, 0:keys(qb)],
                                               scalar=zinv[:, b, 1:2], in1=probs[:, b, 0, 0:keys(qb)],
                                               op0=ALU.mult, op1=ALU.add).then_inc(a_ready, 1)

            def heads_out(qb):
                dve.wait_ge(av_done, DIFF_H * (qb + 1))
                o = dif_out[:, qb].rearrange("p (h e) -> p h e", h=DIFF_H)
                nc.vector.tensor_tensor(o, bank(6).rearrange("p (h e) -> p h e", h=DIFF_H),
                                        bc(r1[:, qb % 2], [P, DIFF_H, P], (2,)), ALU.mult).then_inc(av_free, 1)
                dve.wait_ge(av_free, qb + 1)
                link(nc.vector.tensor_tensor(sqt.rearrange("p (h e) -> p h e", h=DIFF_H), o, o, ALU.mult))
                nc.vector.tensor_reduce(ssq[:, qb * DIFF_H:(qb + 1) * DIFF_H], sqt.rearrange("p (h e) -> p h e", h=DIFF_H),
                                        AX.X, ALU.add).then_inc(ssq_ready, 1)

            maxima(0)
            for i in range(NT * DIFF_H):
                if i % DIFF_H == 1 and i > 1:
                    heads_out(i // DIFF_H - 1)
                combine(i)
                if i + 1 < NT * DIFF_H:
                    maxima(i + 1)
                if i == 5:
                    ada_sum(11)
                if i == 7:
                    mod_store(11)
            heads_out(NT - 1)
            dve.wait_ge(rms_std, 1)
            link(nc.vector.reciprocal(ssq, ssq))

            def mix(t):
                o = dif_out[:, t].rearrange("p (h e) -> p h e", h=DIFF_H)
                link(nc.vector.tensor_tensor(o, o, bc(ssq[:, t * DIFF_H:(t + 1) * DIFF_H], [P, DIFF_H, P], (2,)), ALU.mult))
                nc.vector.tensor_tensor(o, o, bc(subg[:], [P, DIFF_H, P], (1,)), ALU.mult).then_inc(mix_ready, 1)

            def mixed(t):
                b = t % 2
                dve.wait_ge(o_done, t + 1)
                nc.vector.tensor_tensor(u[:, b], bank2(2), g1b, ALU.mult).then_inc(o_free, 1)
                dve.wait_ge(o_free, t + 1)
                dve.wait_ge(xr_in[b], 16 * (t // 2 + 1))
                link(nc.vector.scalar_tensor_tensor(out=u[:, b], in0=xr[:, b], scalar=ALPHA, in1=u[:, b],
                                                    op0=ALU.mult, op1=ALU.add))
                statistics(u[:, b], stat[:, b], aggr[:, b], ovar)
                dve.wait_ge(ostd, t + 1)
                invert(l_std[:, b:b + 1], aggr[:, b], l_rstd[:, b:b + 1], l_nb[:, b:b + 1], orstd)

            def renormed(t):
                b = t % 2
                dve.wait_ge(x1_ready, t + 1)
                statistics(x1[:, t], z_stat[:, b], z_aggr[:, b], zvar)
                dve.wait_ge(zstd, t + 1)
                invert(z_std[:, b:b + 1], z_aggr[:, b], z_rstd[:, b:b + 1], z_nb[:, b:b + 1], zrstd)

            def modulated(t):
                dve.wait_ge(zT_done, t + 1)
                wait_nonzero(dve, logits_done, t)
                for k in range(4, KC):
                    last = nc.vector.tensor_scalar(h2T[:, k], bank(5)[:, (k - 4) * P:(k - 3) * P],
                                                   modcol[:, 3, k:k + 1], modcol[:, 2, k:k + 1], ALU.mult, ALU.add)
                last.then_inc(h2_dve, 1)

            def split_lo(parts, parity, count):
                for k in range(QUARTERS) if callable(count) else [count]:
                    dve.wait_ge(hi_ready, count(k) if callable(count) else k + 1)
                    nc.vector.tensor_tensor(parts[1][:, quarter(k)], raw[parity][:, quarter(k)],
                                            parts[0][:, quarter(k)].bitcast(f32), ALU.subtract).then_inc(lo_ready, 1)

            mix(0)
            mix(1)
            for t in range(NT + 2):
                if 2 <= t < 2 + QUARTERS:
                    split_lo(gate_w[0], 0, t - 2)
                if t + 2 < NT:
                    mix(t + 2)
                if t >= 2:
                    modulated(t - 2)
                if t < NT:
                    mixed(t)
                if 1 <= t <= NT:
                    renormed(t - 1)

            dve.wait_ge(logits_done, NT)
            dve.wait_ge(z_out[0], 16 * NT // 2)
            dve.wait_ge(z_out[1], 16 * NT // 2)
            te = lambda a: a.rearrange("p (t e) -> p t e", e=NE)
            link(nc.vector.tensor_tensor(te(r_exp), te(bank(7)[:, 0:NT * NE]), bc(router_bc[:], [P, NT, NE], (1,)), ALU.add))
            link(nc.vector.tensor_reduce(r_row, te(r_exp), AX.X, ALU.max))
            nc.vector.tensor_tensor(te(r_exp), te(r_exp), bc(r_row, [P, NT, NE], (2,)), ALU.subtract).then_inc(lmax_ready, 1)
            dve.wait_ge(lexp_done, 1)
            link(nc.vector.tensor_reduce(r_row, te(r_exp), AX.X, ALU.add))
            link(nc.vector.reciprocal(r_row, r_row))
            link(nc.vector.tensor_tensor(te(r_prob), te(r_exp), bc(r_row, [P, NT, NE], (2,)), ALU.mult))

            lower = const("lower").rearrange("p (e j) -> p e j", e=EPG)

            def ranks(values, n, gt, ge, rank):
                v = values.rearrange("p (g e) -> p g e", e=EPG)
                g4 = gt.rearrange("p (g e j) -> p g e j", e=EPG, j=EPG)
                q4 = ge.rearrange("p (g e j) -> p g e j", e=EPG, j=EPG)
                vj, ve = bc(v, [P, n, EPG, EPG], (2,)), bc(v, [P, n, EPG, EPG], (3,))
                mark(nc.vector.tensor_tensor(g4, vj, ve, ALU.is_gt))
                link(nc.vector.tensor_tensor(q4, vj, ve, ALU.is_equal))
                link(nc.vector.tensor_tensor(q4, q4, bc(lower, [P, n, EPG, EPG], (1,)), ALU.mult))
                link(nc.vector.tensor_tensor(g4, g4, q4, ALU.add))
                link(nc.vector.tensor_reduce(rank, g4, AX.X, ALU.add))

            ranks(r_prob, NT * NG, r_gt, r_eq, r_rank)
            link(nc.vector.tensor_scalar(r_mask, r_rank, 1.5, None, ALU.is_lt))
            link(nc.vector.tensor_tensor(r_tmp, r_prob, r_mask, ALU.mult))
            link(nc.vector.tensor_reduce(r_group, r_tmp.rearrange("p (g e) -> p g e", e=EPG), AX.X, ALU.add))
            ranks(r_group, NT, r_gt[:, 0:NT * 16], r_eq[:, 0:NT * 16], r_grank)
            link(nc.vector.tensor_scalar(r_grank, r_grank, 0.5, None, ALU.is_lt))
            gm = r_mask.rearrange("p (g e) -> p g e", e=EPG)
            nc.vector.tensor_tensor(gm, gm, bc(r_grank, [P, NT * NG, EPG], (2,)), ALU.mult).then_inc(mask_ready, 1)
            dve.wait_ge(mask_ready, 1)
            link(nc.vector.tensor_tensor(r_prob, r_prob, r_mask, ALU.mult))
            link(nc.vector.tensor_reduce(r_row, te(r_prob), AX.X, ALU.add))
            link(nc.vector.reciprocal(r_row, r_row))
            link(nc.vector.tensor_tensor(te(r_prob), te(r_prob), bc(r_row, [P, NT, NE], (2,)), ALU.mult))
            dve.wait_ge(count_done, 1)
            mark(nc.vector.memset(r_off[:, 0:NE], 0.0))
            link(nc.vector.tensor_copy(r_tot, bank(1)[:, 0:NT * NE]))
            for t in range(1, NT + 1):
                link(nc.vector.tensor_tensor(r_off[:, t * NE:(t + 1) * NE], r_off[:, (t - 1) * NE:t * NE],
                                             r_tot[:, (t - 1) * NE:t * NE], ALU.add))
            r7 = r_gt[:, 0:NE * (NT - 1)].rearrange("p (e m) -> p e m", m=NT - 1)
            link(nc.vector.tensor_tensor(r7, bc(r_off[:, NT * NE:], [P, NE, NT - 1], (2,)),
                                         bc(const("steps"), [P, NE, NT - 1], (1,)), ALU.is_gt))
            link(nc.vector.tensor_reduce(r_tiles, r7, AX.X, ALU.add))
            link(nc.vector.tensor_scalar(r_tiles, r_tiles, 1.0, None, ALU.add))
            mark(nc.vector.memset(r_start[:, 0:1], 0.0))
            link(nc.vector.tensor_tensor_scan(r_start[:, 1:NE + 1], ones[:, 0:NE], r_tiles, 0.0, ALU.mult, ALU.add))
            nc.vector.tensor_copy(ts_i[:], r_start[0:1, :]).then_inc(starts_ready, 1)
            link(nc.vector.tensor_scalar(r_tiles, r_start[:, 0:NE], float(P), None, ALU.mult))
            link(nc.vector.tensor_tensor(r_tmp, bank(0)[:, 0:NT * NE], r_off[:, 0:NT * NE], ALU.add))
            link(nc.vector.tensor_tensor(te(r_tmp), te(r_tmp), bc(r_tiles, [P, NT, NE], (1,)), ALU.add))
            link(nc.vector.tensor_tensor(r_tmp, r_tmp, r_mask, ALU.mult))
            link(nc.vector.tensor_reduce(r_hi, te(r_tmp), AX.X, ALU.max))
            link(nc.vector.tensor_tensor(te(r_tot), te(r_tmp), bc(r_hi, [P, NT, NE], (2,)), ALU.is_equal))
            link(nc.vector.tensor_tensor(te(r_gt[:, 0:NT * NE]), te(r_tot), te(r_prob), ALU.mult))
            link(nc.vector.tensor_reduce(gates[:, 1], te(r_gt[:, 0:NT * NE]), AX.X, ALU.add))
            link(nc.vector.tensor_tensor(r_tot, r_mask, r_tot, ALU.subtract))
            link(nc.vector.tensor_tensor(te(r_gt[:, 0:NT * NE]), te(r_tot), te(r_prob), ALU.mult))
            link(nc.vector.tensor_reduce(gates[:, 0], te(r_gt[:, 0:NT * NE]), AX.X, ALU.add))
            link(nc.vector.tensor_tensor(r_tot, r_tot, r_tmp, ALU.mult))
            link(nc.vector.tensor_reduce(r_lo, te(r_tot), AX.X, ALU.add))
            link(nc.vector.tensor_copy(slot_i[:, 0], r_lo))
            link(nc.vector.tensor_copy(slot_i[:, 1], r_hi))
            link(nc.vector.tensor_single_scalar(id_at[:], slot_i[:], 7, ALU.logical_shift_right))
            link(nc.vector.tensor_scalar(id_low, slot_i[:], P - 1, 5, ALU.bitwise_and, ALU.logical_shift_left))
            nc.vector.tensor_tensor(id_at[:], id_at[:], id_low, ALU.bitwise_or).then_inc(slots_ready, 1)

            def modulate_gathered(g):
                for k in range(4, KC):
                    last = nc.vector.tensor_scalar(hgf[:, k * P:(k + 1) * P], bank(3)[:, (k - 4) * P:(k - 3) * P],
                                                   modcol[:, 3, k:k + 1], modcol[:, 2, k:k + 1], ALU.mult, ALU.add)
                last.then_inc(hg_dve, 1)
                dve.wait_ge(hg_hi_ready, g + 1)
                nc.vector.tensor_tensor(hg_parts[1][:], hgf, hg_parts[0][:].bitcast(f32), ALU.subtract
                                        ).then_inc(hg_stored, 1)

            def expert_tile(g, first=None, i=None, q=None):
                if first is not None:
                    for j, parts in ((1, up_w), (2, down_w)):
                        split_lo(parts, raw_count(i, q, j)[0], lambda k: split_count(i, q, j, k + 1))
                dve.wait_ge(silu_done, g + 2)
                dve.wait_ge(up_done, g + 2)
                dve.wait_ge(heT_done, g * 2 + 2)
                for r in range(2):
                    nc.vector.tensor_tensor(he[:, he_half[r]], sg[:, he_half[r]], bank(1)[:, he_half[r]], ALU.mult
                                            ).then_inc(he_ready, 1)
                for r in range(2):
                    dve.wait_ge(heT_hi_ready, g * 2 + (1 + r))
                    nc.vector.tensor_tensor(heT_parts[1][:, he_half[r]], bank((4, 7)[r])[:, 0:DE // 2],
                                            heT_parts[0][:, he_half[r]].bitcast(f32), ALU.subtract
                                            ).then_inc(heT_stored, 1)
                dve.wait_ge(xgT_done, g + 3)
                dve.wait_ge(hg_stored, g + 1)
                modulate_gathered(g + 1)
                if first is not None:
                    def split_next_gate():
                        split_lo(gate_w[1 - q], raw_count(i, q, 3)[0], lambda k: split_count(i, q, 3, k + 1))
                    if q == 0:
                        split_next_gate()
                    else:
                        with dve.If(i < NE // 2 - 1):
                            split_next_gate()
                dve.wait_ge(y_done, g + 2)
                dve.wait_ge(y_out, g * 16 + 16)
                nc.vector.tensor_tensor(yb, bank2(5), g2b[:], ALU.mult).then_inc(y_stored, 1)

            dve.wait_ge(starts_ready, 1)
            for buffer_free, halves in ((he_ready, 2), (heT_stored, 2), (y_stored, 1)):
                dve.sem_inc(buffer_free, halves)
            dve.wait_ge(xgT_done, 2)
            modulate_gathered(0)
            with dve.Fori(0, NE // 2) as i:
                for q in range(2):
                    first = dve.value_load(ts_i[0:1, bass.ds(i * 2 + q, 1)], min_val=0, max_val=MAX_TILES - 1)
                    end = dve.value_load(ts_i[0:1, bass.ds(i * 2 + (q + 1), 1)], min_val=1, max_val=MAX_TILES)
                    expert_tile(first, first, i, q)
                    with dve.If(first + 1 < end):
                        with dve.Fori(first + 1, end) as g:
                            expert_tile(g)

            def last_norm(t):
                b = t % 2
                dve.wait_ge(fstd, t + 1)
                invert(l_std[:, b:b + 1], aggr[:, b], l_rstd[:, b:b + 1], l_nb[:, b:b + 1], frstd)

            def bias(t):
                dve.wait_ge(gained, t + 1)
                nc.vector.tensor_tensor(fin[:, t % YBUF], fin[:, t % YBUF], ln_b, ALU.add).then_inc(biased, 1)

            dve.wait_ge(x1_in, 16)
            for t in range(NT):
                b, yb_t = t % 2, t % YBUF
                dve.wait_ge(y_in[yb_t][0], 16 * (t // YBUF + 1))
                dve.wait_ge(y1_scaled, t + 1)
                link(nc.vector.scalar_tensor_tensor(out=ygath[:, yb_t, 1], in0=ygath[:, yb_t, 0],
                                                    scalar=gates[:, 0, t:t + 1], in1=ygath[:, yb_t, 1],
                                                    op0=ALU.mult, op1=ALU.add))
                nc.vector.tensor_tensor(x1_end[:, t], x1_end[:, t], ygath[:, yb_t, 1], ALU.add).then_inc(yg_free, 1)
                dve.wait_ge(yg_free, t + 1)
                statistics(x1_end[:, t], stat[:, b], aggr[:, b], fvar)
                last_norm(t)
                if t >= 2:
                    bias(t - 2)
            bias(NT - 2)
            bias(NT - 1)

        @block.tensor
        def _(pe):
            mm, tr = nc.tensor.matmul, nc.tensor.transpose

            def modulation(b):
                m = ADA_ORDER.index(b)
                vec = b // 2
                pe.wait_ge(ada_summed, m + 1)
                if m >= 1:
                    pe.wait_ge(mod_stored, m)
                w, out_b = ring[slot_use("ada", b)[0]], mod_bank(b)
                if vec in (2, 5):
                    mm(out_b, ones[:], w[:, 0, :], start=True, stop=False)
                    last = mm(out_b, ident[0:12, b:b + 1].broadcast_to([12, P]), b12[:, :], start=False, stop=True)
                else:
                    for q in range(4):
                        mm(out_b[:, q:q + 1], w[:, 0, q * P:(q + 1) * P], ones[:, 0:1], start=True, stop=False)
                        last = mm(out_b[:, q:q + 1], b12[:, q * P:(q + 1) * P], ident[0:12, b:b + 1],
                                  start=False, stop=True)
                last.then_inc(mod_done, 1)

            pe.wait_ge(ones_ready, 1)
            pe.wait_ge(consts_in, 16)
            pe.wait_ge(small_in, 144)
            pe.wait_ge(cond_ready, 1)
            for b in range(4):
                modulation(b)
            pe.wait_ge(mod_stored, 4)
            for t in range(NT):
                pe.wait_ge(xn_ready, t + 1)
                if t >= 2:
                    pe.wait_ge(hT_act, t - 1)
                    pe.wait_ge(hT_dve, t - 1)
                for k in range(KC):
                    last = tr(bank((2 * t + k // 4) % 4)[:, (k % 4) * P:(k % 4 + 1) * P], xn[:, t, k * P:(k + 1) * P], ident)
                    if k % 4 == 3:
                        last.then_inc(turned, 1)
            pe.wait_ge(hT_act, NT)
            pe.wait_ge(hT_dve, NT)

            def project(b, j):
                g = NT * PROJ_ORDER.index(b) + j
                s, uses = slot_use("in", b)
                if j == 0:
                    pe.wait_ge(slot_loaded[s], 16 * uses)
                if g >= 2:
                    pe.wait_ge(proj_free[g % 2], g // 2)
                for k in range(KC):
                    if b in (DQ, DK):
                        last = mm(bank(g % 2), ring[s][:, k, (j // 2) * P:(j // 2 + 1) * P],
                                  hT[:, k, (j % 2) * H:(j % 2 + 1) * H], start=(k == 0), stop=(k == KC - 1))
                    else:
                        last = mm(bank(g % 2), hT[:, k, j * P:(j + 1) * P], ring[s][:, k, :],
                                  start=(k == 0), stop=(k == KC - 1))
                last.then_inc(proj_done, 1)

            def turn_rotated(i):
                pe.wait_ge(rot_ready, i + 1)
                if i >= 2:
                    pe.wait_ge(rotT_stored, i - 1)
                src = qrot[:, i % 2] if i < NT else rk[:, i - NT]
                for p in range(PAIRS):
                    last = tr(bank(3 + i % 2)[:, p * P:(p + 1) * P], src[:, p * P:(p + 1) * P], ident)
                last.then_inc(rotT_done, 1)

            for i in range(2 * NT):
                project((RQ, RK)[i // NT], i % NT)
                if i >= 1:
                    turn_rotated(i - 1)
            for t in range(NT):
                project(RV, t)
                if t == 0:
                    turn_rotated(2 * NT - 1)
                if t == 3:
                    modulation(6)
            for t in range(NT):
                project(RG, t)
                if t == 3:
                    modulation(7)
            pe.wait_ge(rotT_stored, 2 * NT)
            for n in range(NT):
                wait_nonzero(pe, rp_ready, n)
                here = slice(n * P, (n + 1) * P)
                for p in range(PAIRS):
                    for r in range(2):
                        rows = slice(r * DH, (r + 1) * DH)
                        last = mm(bank(3 + r)[:, p * P:(p + 1) * P], rkT[rows, p, here], rqT[rows, p, here],
                                  start=True, stop=True)
                last.then_inc(rs_done, 1)
                project(DV, n)
                if n == 3:
                    modulation(8)
                pe.wait_ge(rp_ready, n + 1)
                wait_nonzero(pe, ro_free, n)
                if n >= 1:
                    wait_nonzero(pe, state_ready, n)
                for p in range(PAIRS):
                    for r in range(2):
                        h = 2 * p + r
                        rows = slice(r * DH, (r + 1) * DH)
                        o = bank(5 + r)[:, p * DH:(p + 1) * DH]
                        last = mm(o, pm[:, r, p], vs[:, n, h * DH:(h + 1) * DH], start=True, stop=(n == 0))
                        if n > 0:
                            last = mm(o, rqT[rows, p, here], state[rows, p], start=False, stop=True)
                last.then_inc(ro_done, 1)
                if n < NT - 1:
                    for p in range(PAIRS):
                        last = mm(bank(7)[:, p * P:(p + 1) * P], rk[:, n, p * P:(p + 1) * P], vs[:, n, p * P:(p + 1) * P],
                                  start=True, stop=True)
                    last.then_inc(kv_done, 1)
            for j in range(NT):
                project(DQ, j)
                if j == 3:
                    modulation(9)
            for j in range(NT):
                project(DK, j)
                if j == 3:
                    modulation(4)
            modulation(5)
            modulation(10)
            pe.wait_ge(proj_free[0], 7 * NT // 2)
            pe.wait_ge(proj_free[1], 7 * NT // 2)

            pe.wait_ge(dq_zeroed, 2)

            def scores(i, q):
                qb, h = i // DIFF_H, i % DIFF_H
                wait_nonzero(pe, exp_done[q], i)
                for a in range(0, keys(qb), H):
                    n = min(H, keys(qb) - a)
                    diagonal = a + n == keys(qb)
                    mm(bank(2 * q + a // H)[:, 0:n], dqT[q][:, h, qb * P:(qb + 1) * P], dkT[:, h, a:a + n],
                       start=True, stop=not diagonal)
                mm(bank(2 * q + a // H)[:, n - P:n], ident, const("neg_mask"), start=False, stop=True
                   ).then_inc(s_done[q], 1)

            def turn_probs(i):
                qb = i // DIFF_H
                pe.wait_ge(a_ready, i + 1)
                wait_nonzero(pe, aT_stored, i)
                for kb in range(qb + 1):
                    last = tr(bank2(4)[:, kb * P:(kb + 1) * P], probs[:, i % 2, 0, kb * P:(kb + 1) * P], ident)
                last.then_inc(aT_done, 1)

            def times_v(i):
                qb, h = i // DIFF_H, i % DIFF_H
                pe.wait_ge(aT_stored, i + 1)
                if h == 0:
                    wait_nonzero(pe, av_free, qb)
                for kb in range(qb + 1):
                    last = mm(bank(6)[:, h * P:(h + 1) * P], aT[:, i % 2, kb * P:(kb + 1) * P],
                              dv[:, kb, h * P:(h + 1) * P], start=(kb == 0), stop=(kb == qb))
                last.then_inc(av_done, 1)

            for i in range(NT * DIFF_H + 2):
                if i >= 2:
                    turn_probs(i - 2)
                if i < NT * DIFF_H:
                    scores(i, 0)
                if i >= 2:
                    times_v(i - 2)
                if i < NT * DIFF_H:
                    scores(i, 1)
                if i == 7:
                    modulation(11)

            def turn_mixed(t):
                pe.wait_ge(mix_ready, t + 1)
                wait_nonzero(pe, mixT_stored, t)
                for k in range(KC):
                    src = ret_out if k < 4 else dif_out
                    last = tr(bank(k // 4)[:, (k % 4) * P:(k % 4 + 1) * P], src[:, t, (k % 4) * P:(k % 4 + 1) * P], ident)
                last.then_inc(mixT_done, 1)

            def project_out(t, half):
                s, uses = slot_use("out", half)
                if t == 0:
                    pe.wait_ge(slot_loaded[s], 16 * uses)
                if half == 0:
                    pe.wait_ge(mixT_stored, t + 1)
                    wait_nonzero(pe, o_free, t)
                for k in range(KC):
                    last = mm(bank(2 + half), mixT[t % 2][:, k], ring[s][:, k, :], start=(k == 0), stop=(k == KC - 1))
                if half == 1:
                    last.then_inc(o_done, 1)

            def turn_z(t):
                pe.wait_ge(z_ready, t + 1)
                wait_nonzero(pe, h2_act, t)
                wait_nonzero(pe, h2_dve, t)
                for k in range(KC):
                    last = tr(bank(4 + k // 4)[:, (k % 4) * P:(k % 4 + 1) * P], z[:, t % 2, k * P:(k + 1) * P], ident)
                last.then_inc(zT_done, 1)

            def logits(t):
                pe.wait_ge(h2_act, t + 1)
                pe.wait_ge(h2_dve, t + 1)
                for k in range(KC):
                    last = mm(bank(7)[:, t * NE:(t + 1) * NE], h2T[:, k], rw[:, k], start=(k == 0), stop=(k == KC - 1))
                last.then_inc(logits_done, 1)

            pe.wait_ge(exp_done[0], NT * DIFF_H)
            pe.wait_ge(exp_done[1], NT * DIFF_H)
            pe.wait_ge(mod_stored, len(ADA_ORDER))
            turn_mixed(0)
            for t in range(NT + 2):
                if t < NT:
                    project_out(t, 0)
                if t + 1 < NT:
                    turn_mixed(t + 1)
                if t >= 2:
                    turn_z(t - 2)
                if t < NT:
                    project_out(t, 1)
                if t >= 2:
                    logits(t - 2)
            pe.wait_ge(mask_ready, 1)
            mm(bank(0)[:, 0:NT * NE], const("before"), r_mask, start=True, stop=True)
            mm(bank(1)[:, 0:NT * NE], ones[:], r_mask, start=True, stop=True).then_inc(count_done, 1)

            def turn_gathered():
                for k in range(KC):
                    last = tr(bank2(2)[:, k * P:(k + 1) * P], xg[:, k * P:(k + 1) * P], ident)
                last.then_inc(xgT_done, 1)

            def rows_times(out_bank, right, before_step):
                for k in range(KC):
                    before_step(k)
                    here, cols_k = slice(k * P, (k + 1) * P), slice(k * H, (k + 1) * H)
                    mm(out_bank, hg_parts[0][:, here], right[0][:, cols_k], start=(k == 0), stop=False)
                    mm(out_bank, hg_parts[0][:, here], right[1][:, cols_k], start=False, stop=False)
                    last = mm(out_bank, hg_parts[1][:, here], right[0][:, cols_k], start=False, stop=(k == KC - 1))
                return last

            def expert_tile(g, q, first=None, i=None):
                def weights_split(j):
                    def wait(k):
                        if first is not None and k % 2 == 0:
                            pe.wait_ge(lo_ready, split_count(i, q, j, k // 2 + 1))
                    return wait

                pe.wait_ge(hg_stored, g + 1)
                pe.wait_ge(silu_done, g + 1)
                rows_times(bank(0), gate_w[q], weights_split(0)).then_inc(gate_done, 1)
                pe.wait_ge(he_ready, g * 2 + 2)
                rows_times(bank(1), up_w, weights_split(1)).then_inc(up_done, 1)
                pe.wait_ge(gathered, g * 16 + 32)
                turn_gathered()
                for r in range(2):
                    pe.wait_ge(he_ready, g * 2 + (3 + r))
                    pe.wait_ge(heT_stored, g * 2 + (1 + r))
                    for k in range(2):
                        last = tr(bank((4, 7)[r])[:, k * P:(k + 1) * P], he[:, (2 * r + k) * P:(2 * r + k + 1) * P], ident)
                    last.then_inc(heT_done, 1)
                if first is not None:
                    pe.wait_ge(lo_ready, split_count(i, q, 2, QUARTERS))
                pe.wait_ge(y_stored, g + 1)
                for r in range(2):
                    for left, rights in ((0, (0, 1)), (1, (0,))):
                        if left == 0:
                            pe.wait_ge(heT_hi_ready, g * 2 + (1 + r))
                        else:
                            pe.wait_ge(heT_stored, g * 2 + (3 + r))
                        for k in (2 * r, 2 * r + 1):
                            for half in range(2):
                                for right in rights:
                                    last = mm(bank(5 + half), heT_parts[left][:, k * P:(k + 1) * P],
                                              down_w[right][:, k * D + half * H:k * D + (half + 1) * H],
                                              start=(k == 0 and left == right == 0), stop=(k == FK - 1 and left == 1))
                last.then_inc(y_done, 1)

            pe.wait_ge(slots_ready, 1)
            pe.wait_ge(o_free, NT)
            pe.wait_ge(av_free, NT)
            for buffer_free in (xgT_done, up_done, y_done):
                pe.sem_inc(buffer_free, 1)
            pe.sem_inc(heT_done, 2)
            pe.wait_ge(gathered, 16)
            turn_gathered()
            with pe.Fori(0, NE // 2) as i:
                for q in range(2):
                    first = pe.value_load(ts_i[0:1, bass.ds(i * 2 + q, 1)], min_val=0, max_val=MAX_TILES - 1)
                    end = pe.value_load(ts_i[0:1, bass.ds(i * 2 + (q + 1), 1)], min_val=1, max_val=MAX_TILES)
                    expert_tile(first, q, first, i)
                    with pe.If(first + 1 < end):
                        with pe.Fori(first + 1, end) as g:
                            expert_tile(g, q)


def table_of_constants():
    import numpy as np

    p = np.arange(P)
    inv = (np.float32(1.0) / np.float32(10000.0) ** (np.arange(0, DH, 2, dtype=np.float32) / np.float32(DH))).astype(np.float32)
    angle = (np.arange(S, dtype=np.float32)[:, None] * inv[None, :]).astype(np.float32).astype(np.float64)
    gamma = 1.0 - 2.0 ** (-5.0 - np.arange(RET_H))
    by_tile = lambda a: a.reshape(NT, P, 32).transpose(1, 0, 2).reshape(P, NT * 32)
    pair_head = 2 * np.arange(PAIRS)[None, :] + (p // DH)[:, None]
    parts = {
        "ident": np.eye(P),
        "causal": p[:, None] <= p[None, :],
        "neg_mask": np.where(p[None, :] <= p[:, None], 0.0, NEG),
        "before": p[:, None] < p[None, :],
        "cos": by_tile(np.cos(angle)),
        "sin": by_tile(np.sin(angle)),
        "v_decay": gamma[None, :] ** -(p[:, None] + 1.0),
        "q_decay": gamma[None, :] ** (p[:, None] + 1.0) * DH ** -0.5,
        "chunk_decay": gamma[pair_head] ** float(P),
        "lower": np.tile((np.arange(EPG)[None, :] < np.arange(EPG)[:, None]).reshape(1, -1), (P, 1)),
        "steps": np.tile(P * np.arange(1, NT)[None, :], (P, 1)),
    }
    return np.ascontiguousarray(np.concatenate([np.asarray(parts[n], np.float32) for n, _ in CONST_PARTS], axis=1))


_INS = ["x", "c", "w_ada", "b_ada", "w_in", "w_out", "lambda_q1", "lambda_k1", "lambda_q2", "lambda_k2", "diff_subln",
        "ln_mix_g", "ln_mix_b", "ln_ffn_g", "ln_ffn_b", "router_w", "router_b", "w_gate", "w_up", "w_down"]


def kernel(**inputs):
    import numpy as np
    import concourse.bacc as bacc
    from concourse.bass_utils import run_bass_kernel_spmd

    nc = bacc.Bacc("TRN2", target_bir_lowering=False, num_devices=1)
    arrays, args = {}, []
    tables = {"consts": table_of_constants(),
              "token_ids": np.ascontiguousarray(np.arange(S, dtype=np.int32).reshape(NT, P).T)}
    for name in _INS + ["consts", "token_ids"]:
        a = np.ascontiguousarray(inputs[name] if name in inputs else tables[name])
        arrays[f"in_{name}"] = a
        args.append(nc.dram_tensor(f"in_{name}", a.shape, mybir.dt.from_np(a.dtype), kind="ExternalInput").ap())
    out = nc.dram_tensor("out", (1, S, D), mybir.dt.float32, kind="ExternalOutput").ap()
    build(nc, *args, out)
    r = run_bass_kernel_spmd(nc, [arrays], core_ids=[0])
    return r.results[0]["out"]
```

```python
import math
from contextlib import ExitStack

import concourse.bass as bass
from concourse import mybir

P = 128
D = 1024
S = 1024
NT = S // P
KC = D // P
H = 512
RET_H, DH = 8, 64
PAIRS = RET_H // 2
DIFF_H = 4
NE, NG, EPG = 16, 4, 4
DE = 512
FK = DE // P
MAX_TILES = (2 * S + NE * (P - 1)) // P
IDX_TILES = MAX_TILES + 1
assert IDX_TILES == 1 << 5 and P == 1 << 7
ALPHA = 2.0 ** 0.25
YBUF = 4
EPS = 1e-5
NEG = -1e30
QUARTERS = 4
LAMBDA_INIT = 0.8 - 0.6 * math.exp(0.0)

CONST_PARTS = [("ident", P), ("causal", P), ("neg_mask", P), ("before", P), ("cos", NT * 32), ("sin", NT * 32),
               ("v_decay", RET_H), ("q_decay", RET_H), ("chunk_decay", PAIRS), ("lower", EPG * EPG), ("steps", NT - 1),
               ("slot_no", P), ("token_no", NT)]
CONST_AT = {}
_at = 0
for _n, _w in CONST_PARTS:
    CONST_AT[_n] = (_at, _at + _w)
    _at += _w
CONST_W = _at

RQ, RK, RV, RG, DQ, DK, DV = range(7)
BLOCKS = [("ada", 0), ("ada", 1), ("ada", 2), ("ada", 3), ("in", RQ), ("in", RK), ("ada", 6), ("in", RV), ("ada", 7),
          ("in", RG), ("ada", 8), ("in", DV), ("ada", 9), ("in", DQ), ("ada", 10), ("in", DK), ("ada", 11), ("ada", 4),
          ("ada", 5), ("out", 0), ("out", 1)]
PLACES = 5
PLACE = {("ada", 1): 1, ("ada", 2): 2, ("ada", 3): 3, ("in", RQ): 4, ("out", 0): 1, ("out", 1): 2}
ADA_ORDER = [b for k, b in BLOCKS if k == "ada"]
PROJ_ORDER = [b for k, b in BLOCKS if k == "in"]


def place_use(kind, b):
    place = PLACE.get((kind, b), 0)
    before = BLOCKS[:BLOCKS.index((kind, b)) + 1]
    return place, sum(PLACE.get(x, 0) == place for x in before)


def build(nc, x, c, w_ada, b_ada, w_in, w_out, lq1, lk1, lq2, lk2, subln, mix_g, mix_b, ffn_g, ffn_b, router_w,
          router_b, w_gate, w_up, w_down, consts, token_ids, out):
    f32, f32r, i32 = mybir.dt.float32, mybir.dt.float32r, mybir.dt.int32
    ALU, ACT, AX = mybir.AluOpType, mybir.ActivationFunctionType, mybir.AxisListType

    z_rows = nc.dram_tensor("z_rows", (S, D), f32)
    slot_ids = nc.dram_tensor("slot_ids", (IDX_TILES * P, 1), i32)
    x1_rows = nc.dram_tensor("x1_rows", (S, D), f32)
    y_rows = nc.dram_tensor("y_rows", (MAX_TILES * P, D), f32)

    w_ada_v = w_ada[0].rearrange("(p k) n -> p k n", k=KC)
    w_in_v = w_in[0].rearrange("(k p) n -> p k n", p=P)
    w_out_v = w_out[0].rearrange("(k p) n -> p k n", p=P)
    x_v = x[0].rearrange("(t p) d -> p t d", p=P)
    out_v = out[0].rearrange("(t p) d -> p t d", p=P)

    with ExitStack() as ctx:
        def sb(name, shape, dt=f32):
            return ctx.enter_context(nc.sbuf_tensor(name, shape, dt))

        def sem(name):
            return ctx.enter_context(nc.semaphore(name))

        start_of = {}

        def region(name, shape):
            t = sb(name, shape)
            start_of[name] = nc.sbuf_base - 4 * math.prod(shape[1:])
            return t

        rooms = [region(f"room{i}", [P, KC, H]) for i in range(3)]
        A = region("region_a", [P, 8192])
        B = region("region_b", [P, 8192])
        C = region("region_c", [P, 8192])
        M = region("region_m", [P, 8192])
        V = region("region_v", [P, 4096])

        def f32r_in(name, where, at, n):
            return nc.alloc_sbuf_tensor_at(name, [P, n], f32r, offset=start_of[where] + 4 * at)

        hT_hi = f32r_in("hT_hi", "region_a", 0, 8192)
        hT_lo = [f32r_in("hT_lo0", "region_m", 0, 4096), f32r_in("hT_lo1", "region_v", 0, 4096)]
        in_w = [f32r_in("in_hi", "room1", 0, 4096), f32r_in("in_lo", "room2", 0, 4096)]
        gate_w = [[f32r_in(f"gate{q}_{n}", w, at, 4096) for n, at in (("hi", a0), ("lo", a1))]
                  for q, (w, a0, a1) in enumerate((("region_b", 0, 4096), ("room1", 0, 4096)))]
        up_w = [f32r_in(f"up_{n}", "region_m", at, 4096) for n, at in (("hi", 0), ("lo", 4096))]
        down_w = [f32r_in(f"down_{n}", "region_a", at, 4096) for n, at in (("hi", 0), ("lo", 4096))]
        hg_parts = [f32r_in(f"hg_{n}", "region_c", at, D) for n, at in (("hi", 2048), ("lo", 3072))]
        heT_parts = [f32r_in(f"heT_{n}", "region_c", at, DE) for n, at in (("hi", 5120), ("lo", 5632))]
        raw = [rooms[0][:].rearrange("p k n -> p (k n)"), V[:]]
        cst = sb("cst", [P, CONST_W])
        ones = sb("ones", [P, P])
        g2b = sb("g2b", [P, D])
        rg_even = sb("rg_even", [P, H])
        b12 = sb("b12", [12, H])
        modcol = sb("modcol", [P, 4, KC])
        rw = sb("rw", [P, KC, NE])
        small = sb("small", [P, 224])
        ts_i = sb("ts_i", [1, NE + 1], i32)

        def const(name):
            a, b = CONST_AT[name]
            return cst[:, a:b]

        ident = const("ident")
        cos_t = const("cos").rearrange("p (t a) -> p t a", t=NT)
        sin_t = const("sin").rearrange("p (t a) -> p t a", t=NT)

        probs = A[:, 0:4096].rearrange("p (b c n) -> p b c n", b=2, c=2)
        aT = A[:, 4096:6144].rearrange("p (b n) -> p b n", b=2)
        x1 = A[:].rearrange("p (t d) -> p t d", t=NT)
        xn = B[:].rearrange("p (t d) -> p t d", t=NT)
        rqT = B[:, 0:4096].rearrange("p (c s) -> p c s", c=PAIRS)
        rkT = B[:, 4096:8192].rearrange("p (c s) -> p c s", c=PAIRS)
        dkT = rkT
        rk = C[:, 0:4096].rearrange("p (t n) -> p t n", t=NT)
        ret_out = rk
        hTf = C[:, 0:2048].rearrange("p (b n) -> p b n", b=2)
        vs = C[:, 4096:8192].rearrange("p (t n) -> p t n", t=NT)
        dv = vs
        g1b = A[:, 7168:8192]
        xr = C[:, 4096:6144].rearrange("p (b d) -> p b d", b=2)
        u = C[:, 6144:8192].rearrange("p (b d) -> p b d", b=2)
        z = M[:, 4096:6144].rearrange("p (b d) -> p b d", b=2)
        mixT = [a.rearrange("p (k n) -> p k n", k=KC) for a in (M[:, 6144:7168], V[:, 3072:4096])]
        places = [r[:] for r in rooms] + [C[:, at:at + 4096].rearrange("p (k n) -> p k n", k=KC) for at in (0, 4096)]
        xg = C[:, 0:1024]
        hgf = C[:, 1024:2048]
        sg = C[:, 4096:4608]
        he = C[:, 4608:5120]
        yb = C[:, 6144:7168]
        idx_all = C[:, 7168:7168 + IDX_TILES].bitcast(i32)
        idx_cur = C[:, 7232:7233].bitcast(i32)
        idx_first = C[:, 7236:7237].bitcast(i32)
        in_first = C[:, 1024:2048].rearrange("p (t n) -> p t n", t=NT)
        tok_i = C[:, 7240:7240 + NT].bitcast(i32)
        rt = C[:, 4736:7168]
        x1_end = B[:].rearrange("p (t d) -> p t d", t=NT)
        ygath = M[:].rearrange("p (b j d) -> p b j d", b=YBUF, j=2)
        fin = A[:, 0:4096].rearrange("p (b d) -> p b d", b=YBUF)
        dif_out = M[:, 0:4096].rearrange("p (t n) -> p t n", t=NT)
        dqT = [rqT, M[:, 4096:8192].rearrange("p (c s) -> p c s", c=DIFF_H)]
        t1 = M[:, 4096:4608]
        t2 = M[:, 4608:5120]
        qrot = M[:, 5120:6144].rearrange("p (b n) -> p b n", b=2)
        rgs = [rg_even[:], qrot[:, 1]]
        pm = M[:, 6144:7168].rearrange("p (r c n) -> p r c n", r=2, c=PAIRS)
        state = M[:, 7168:7680].rearrange("p (c e) -> p c e", c=PAIRS)
        state_new = M[:, 7936:8192].rearrange("p (c e) -> p c e", c=PAIRS)
        lamv = M[:, 7680:7936].rearrange("p (v n) -> p v n", v=4)
        ln_g, ln_b = V[:, 0:1024], V[:, 1024:2048]
        h2T = V[:, 2048:3072].rearrange("p (k n) -> p k n", k=KC)

        def cols(a, n):
            return small[:, a:a + n]

        eps_c = cols(0, 1)
        cond = cols(1, KC)
        craw = cols(9, KC)
        nlam = cols(17, 1)
        lam4 = cols(18, 4)
        stat = cols(22, 24).rearrange("p (b n) -> p b n", b=2)
        aggr = cols(46, 4).rearrange("p (b n) -> p b n", b=2)
        l_rstd, l_std, l_nb = cols(50, 2), cols(52, 2), cols(146, 2)
        z_stat = cols(150, 24).rearrange("p (b n) -> p b n", b=2)
        z_aggr = cols(174, 4).rearrange("p (b n) -> p b n", b=2)
        z_rstd, z_std, z_nb = cols(178, 2), cols(180, 2), cols(182, 2)
        hsum, hvar, hstd = cols(54, 8), cols(62, 8), cols(70, 8)
        negmax = cols(78, 4).rearrange("p (b n) -> p b n", b=2)
        zsum = cols(82, 4).rearrange("p (b n) -> p b n", b=2)
        zinv = cols(86, 4).rearrange("p (b n) -> p b n", b=2)
        r1 = cols(90, 8).rearrange("p (b n) -> p b n", b=2)
        ssq = cols(98, 32)
        r_spare = cols(206, 1)
        gates = cols(130, 2 * NT).rearrange("p (j t) -> p j t", j=2)
        router_bc = sb("router_bc", [P, NE])
        subg = sb("subg", [P, P])
        slot_i = sb("slot_i", [P, 2, NT], i32)
        id_at = sb("id_at", [P, 2, NT], i32)
        id_low = small[:, 190:190 + 2 * NT].bitcast(i32).rearrange("p (j t) -> p j t", j=2)

        psum = ctx.enter_context(nc.psum_tensor("psum", [P, 8, H], f32))

        def bank(i):
            return psum[:, i, :]

        def bank2(i):
            return psum[:, i:i + 2, :].rearrange("p b n -> p (b n)")

        sqt = V[:, 2048:2560]
        r_exp, r_prob = rt[:, 0:128], rt[:, 128:256]
        r_gt, r_eq = rt[:, 256:768], rt[:, 768:1280]
        r_rank, r_mask, r_tmp, r_tot = rt[:, 1280:1408], rt[:, 1408:1536], rt[:, 1536:1664], rt[:, 1664:1792]
        r_off = rt[:, 1792:1792 + (NT + 1) * NE]
        r_group, r_grank = rt[:, 1952:1984], rt[:, 1984:2016]
        r_row, r_lo, r_hi = rt[:, 2016:2024], rt[:, 2024:2032], rt[:, 2032:2040]
        r_pos = rt[:, 2040:2048]
        r_tiles, r_start = rt[:, 2048:2064], rt[:, 2064:2081]

        place_loaded = [sem(f"place_loaded{i}") for i in range(PLACES)]
        in_hi, in_lo, in_used = sem("in_hi"), sem("in_lo"), sem("in_used")
        hT_hi_ready, hT_stored, ret_stored = sem("hT_hi_ready"), sem("hT_stored"), sem("ret_stored")
        consts_in, small_in, cond_ready, ones_ready = (
            sem("consts_in"), sem("small_in"), sem("cond_ready"), sem("ones_ready"))
        c_in, b_in = sem("c_in"), sem("b_in")
        ada_summed, mod_done, mod_stored, var_ready = (
            sem("ada_summed"), sem("mod_done"), sem("mod_stored"), sem("var_ready"))
        std_ready, xn_ready, turned, hT_act = (
            sem("std_ready"), sem("xn_ready"), sem("turned"), sem("hT_act"))
        hT_dve, proj_done, rot_ready, rotT_done = (
            sem("hT_dve"), sem("proj_done"), sem("rot_ready"), sem("rotT_done"))
        rotT_stored, rs_done, rp_ready, ro_done = (
            sem("rotT_stored"), sem("rs_done"), sem("rp_ready"), sem("ro_done"))
        ro_free, kv_done, state_ready, rvar_ready = (
            sem("ro_free"), sem("kv_done"), sem("state_ready"), sem("rvar_ready"))
        rstd_ready, lam_sums, lam_exp, max_ready = (
            sem("rstd_ready"), sem("lam_sums"), sem("lam_exp"), sem("max_ready"))
        a_ready, aT_done, aT_stored, av_done = (
            sem("a_ready"), sem("aT_done"), sem("aT_stored"), sem("av_done"))
        ssq_ready, rms_std, ln_in, mix_ready = (
            sem("ssq_ready"), sem("rms_std"), sem("ln_in"), sem("mix_ready"))
        mixT_done, mixT_stored, o_done, o_free = (
            sem("mixT_done"), sem("mixT_stored"), sem("o_done"), sem("o_free"))
        ovar, ostd, orstd, un_ready = (
            sem("ovar"), sem("ostd"), sem("orstd"), sem("un_ready"))
        x1_ready, zvar, zstd, zrstd = (
            sem("x1_ready"), sem("zvar"), sem("zstd"), sem("zrstd"))
        z_ready, zT_done, h2_act, h2_dve = (
            sem("z_ready"), sem("zT_done"), sem("h2_act"), sem("h2_dve"))
        logits_done, lmax_ready, lexp_done, mask_ready = (
            sem("logits_done"), sem("lmax_ready"), sem("lexp_done"), sem("mask_ready"))
        count_done, ids_zeroed, slots_ready, ids_out = (
            sem("count_done"), sem("ids_zeroed"), sem("slots_ready"), sem("ids_out"))
        ids_in, idx_ready, tok_in, idx_zero = (
            sem("ids_in"), sem("idx_ready"), sem("tok_in"), sem("idx_zero"))
        starts_ready, gathered, xgT_done, hg_stored = (
            sem("starts_ready"), sem("gathered"), sem("xgT_done"), sem("hg_stored"))
        gate_done, up_done, silu_done, he_ready = (
            sem("gate_done"), sem("up_done"), sem("silu_done"), sem("he_ready"))
        heT_done, heT_stored, y_done, y_stored = (
            sem("heT_done"), sem("heT_stored"), sem("y_done"), sem("y_stored"))
        y_out, yg_free, fvar, fstd = (
            sem("y_out"), sem("yg_free"), sem("fvar"), sem("fstd"))
        frstd, fn_ready, ffn_in, dve_step = (
            sem("frstd"), sem("fn_ready"), sem("ffn_in"), sem("dve_step"))
        pool_step = (
            sem("pool_step"))
        av_free = sem("av_free")
        y_zeroed = sem("y_zeroed")
        in_first_ready, first_done, first_ready = sem("in_first_ready"), sem("first_done"), sem("first_ready")
        passed = sem("passed")
        dq_zeroed = sem("dq_zeroed")
        x_in = [sem(f"x_in{i}") for i in range(NT)]
        proj_free = [sem(f"proj_free{i}") for i in range(2)]
        s_done = [sem(f"s_done{i}") for i in range(2)]
        exp_done = [sem(f"exp_done{i}") for i in range(2)]
        xr_in = [sem(f"xr_in{i}") for i in range(2)]
        z_out = [sem(f"z_out{i}") for i in range(2)]
        raw_in = [[sem(f"raw_in{i}_{k}") for k in range(QUARTERS)] for i in range(2)]
        hi_ready, lo_ready = sem("hi_ready"), sem("lo_ready")
        hg_act, hg_dve, hg_hi_ready, heT_hi_ready = sem("hg_act"), sem("hg_dve"), sem("hg_hi_ready"), sem("heT_hi_ready")
        x1_out, x1_in = sem("x1_out"), sem("x1_in")
        y_in = [[sem(f"y_in{b}{j}") for j in range(2)] for b in range(YBUF)]
        out_done = [sem(f"out_done{i}") for i in range(YBUF)]
        xn_inv = sem("xn_inv")
        x1_scaled, y1_scaled, gained, biased = sem("x1_scaled"), sem("y1_scaled"), sem("gained"), sem("biased")

        block = ctx.enter_context(nc.Block())

        he_half = (slice(0, DE // 2), slice(DE // 2, DE))

        def quarter(k):
            return slice(k * 1024, (k + 1) * 1024)

        def block_no(i, q, j):
            return i * 6 + (3 * q + j)

        def split_count(i, q, j, quarters):
            return block_no(i, q, j) * QUARTERS + quarters

        def raw_count(i, q, j):
            n = 3 * q + j
            return n % 2, i * 48 + 16 * (n // 2 + 1)

        def bc(ap, shape, at):
            for d in at:
                ap = ap.unsqueeze(d)
            return ap.broadcast_to(shape)

        def wait_nonzero(engine, semaphore, count):
            if count > 0:
                engine.wait_ge(semaphore, count)

        def keys(qb):
            return (qb + 1) * P

        def mod_bank(b):
            return bank(7 if b in (4, 5) else 2)

        def place_free(kind, b):
            if kind == "out":
                return proj_done, NT * len(PROJ_ORDER)
            before = [x for x in BLOCKS[:BLOCKS.index((kind, b))] if PLACE.get(x, 0) == PLACE.get((kind, b), 0)]
            if not before:
                return None
            k0, b0 = before[-1]
            if k0 == "ada":
                return mod_done, ADA_ORDER.index(b0) + 1
            return in_lo, QUARTERS * (PROJ_ORDER.index(b0) + 1)

        @block.sync
        def _(sp):
            sp.dma_start(craw, c.rearrange("o (p k) -> (o p) k", k=KC)).then_inc(c_in, 16)
            sp.dma_start(cst[:], consts).then_inc(consts_in, 16)
            sp.dma_start(b12[:], b_ada[0].rearrange("(b n) -> b n", n=H)).then_inc(b_in, 16)
            for kind, b in BLOCKS:
                place, _ = place_use(kind, b)
                if place_free(kind, b):
                    sp.wait_ge(*place_free(kind, b))
                n = BLOCKS.index((kind, b))
                if 2 <= n < PLACES:
                    sp.wait_ge(place_loaded[n - 2], 16)
                src = {"ada": w_ada_v, "in": w_in_v, "out": w_out_v}[kind][:, :, b * H:(b + 1) * H]
                sp.dma_start(places[place], src).then_inc(place_loaded[place], 16)

            def load_raw(e, j, parity, after=None):
                src = (w_gate, w_up, w_down)[j][0][bass.ds(e, 1)].rearrange("o (k p) n -> p (o k) n", p=P)
                chunks = (FK if j == 2 else KC) // QUARTERS
                for k in range(QUARTERS):
                    if after:
                        sp.wait_ge(lo_ready, after(k))
                    dst = raw[parity][:, quarter(k)].rearrange("p (k n) -> p k n", k=chunks)
                    sp.dma_start(dst, src[:, k * chunks:(k + 1) * chunks]).then_inc(raw_in[parity][k], 16)

            sp.wait_ge(mod_done, len(ADA_ORDER))
            load_raw(0, 0, 0)
            sp.wait_ge(x1_out, 16 * NT)
            sp.wait_ge(x1_ready, NT)
            sp.wait_ge(o_done, NT)
            sp.wait_ge(logits_done, NT)
            load_raw(0, 1, 1)
            load_raw(0, 2, 0, after=lambda k: k + 1)

            def load_next(i, q):
                for j in range(3):
                    load_raw((i * 2 + (q + 1)).with_bounds(min_val=1, max_val=NE - 1), j, (3 * (q + 1) + j) % 2,
                             after=lambda k: split_count(i, q, 1 + j, k + 1))

            def store_y(g):
                sp.wait_ge(y_stored, g + 2)
                sp.dma_start(y_rows.ap()[bass.ds(g * P, P), :], yb).then_inc(y_out, 16)

            sp.wait_ge(starts_ready, 1)
            sp.sem_inc(y_out, 16)
            with sp.Fori(0, NE // 2) as i:
                for q in range(2):
                    first = sp.value_load(ts_i[0:1, bass.ds(i * 2 + q, 1)], min_val=0, max_val=MAX_TILES - 1)
                    end = sp.value_load(ts_i[0:1, bass.ds(i * 2 + (q + 1), 1)], min_val=1, max_val=MAX_TILES)
                    if q == 0:
                        load_next(i, q)
                    else:
                        with sp.If(i < NE // 2 - 1):
                            load_next(i, q)
                        with sp.If(i > NE // 2 - 2):
                            sp.wait_ge(y_done, first + 1)
                            sp.dma_start(x1_end, x1_rows.ap().rearrange("(t p) d -> p t d", p=P)).then_inc(x1_in, 16)
                    store_y(first)
                    with sp.If(first + 1 < end):
                        with sp.Fori(first + 1, end) as g:
                            store_y(g)
            for t in range(NT):
                sp.wait_ge(biased, t + 1)
                sp.dma_start(out_v[:, t], fin[:, t % YBUF]).then_inc(out_done[t % YBUF], 16)
            for b in range(YBUF):
                sp.wait_ge(out_done[b], 16 * NT // YBUF)

        @block.gpsimd
        def _(pool):
            for i, v in enumerate((lq1, lk1, lq2, lk2)):
                pool.dma_start(lamv[:, i, :], v[0].partition_broadcast(P)).then_inc(small_in, 16)
            pool.dma_start(subg[:], subln[0].partition_broadcast(P)).then_inc(small_in, 16)
            pool.dma_start(rw[:], router_w.rearrange("(k p) e -> p k e", p=P)).then_inc(small_in, 16)
            pool.dma_start(router_bc[:], router_b.partition_broadcast(P)).then_inc(small_in, 16)

            pool.memset(g2b[:], 0.0).then_inc(pool_step, 1)
            pool.wait_ge(pool_step, 1)
            pool.wait_ge(proj_done, 1)
            for g in range(NE, MAX_TILES):
                pool.dma_start(y_rows.ap()[g * P:(g + 1) * P, :], g2b[:]).then_inc(y_zeroed, 16)
            pool.wait_ge(rs_done, NT)
            pool.wait_ge(ro_done, NT)
            pool.memset(dqT[0][DH:P], 0.0).then_inc(dq_zeroed, 1)
            pool.wait_ge(ret_stored, NT)
            pool.memset(dqT[1][0:DH], 0.0).then_inc(dq_zeroed, 1)
            pool.wait_ge(proj_done, NT * len(PROJ_ORDER))
            pool.dma_start(ln_g, mix_g[0].partition_broadcast(P)).then_inc(ln_in, 16)
            pool.dma_start(ln_b, mix_b[0].partition_broadcast(P)).then_inc(ln_in, 16)
            pool.wait_ge(ln_in, 32)
            for t in range(NT):
                pool.wait_ge(un_ready, t + 1)
                pool.tensor_tensor(x1[:, t], u[:, t % 2], ln_g, ALU.mult).then_inc(pool_step, 1)
                pool.wait_ge(pool_step, t + 2)
                pool.tensor_tensor(x1[:, t], x1[:, t], ln_b, ALU.add).then_inc(x1_ready, 1)

            pool.wait_ge(x1_ready, NT)
            pool.memset(idx_all, 0).then_inc(idx_zero, 1)
            pool.wait_ge(idx_zero, 1)
            pool.dma_start(slot_ids.ap().rearrange("(p g) o -> p (g o)", p=P), idx_all).then_inc(ids_zeroed, 16)
            pool.dma_start(tok_i, token_ids).then_inc(tok_in, 16)
            pool.wait_ge(ids_zeroed, 16)
            pool.wait_ge(tok_in, 16)
            pool.wait_ge(z_out[0], 16 * NT // 2)
            pool.wait_ge(z_out[1], 16 * NT // 2)
            pool.wait_ge(first_ready, 1)
            pool.indirect_dma_start(xg, None, z_rows.ap(), bass.IndirectOffsetOnAxis(ap=idx_first, axis=0)
                                    ).then_inc(gathered, 16)
            pool.wait_ge(slots_ready, 1)
            for t in range(NT):
                for j in range(2):
                    pool.indirect_dma_start(slot_ids.ap(), bass.IndirectOffsetOnAxis(ap=id_at[:, j, t:t + 1], axis=0),
                                            tok_i[:, t:t + 1], None).then_inc(ids_out, 16)
            pool.wait_ge(ids_out, 16 * 2 * NT)
            pool.dma_start(idx_all, slot_ids.ap().rearrange("(p g) o -> p (g o)", p=P)).then_inc(ids_in, 16)
            pool.wait_ge(ids_in, 16)
            pool.wait_ge(starts_ready, 1)
            total = pool.value_load(ts_i[0:1, NE:NE + 1], min_val=NE, max_val=MAX_TILES)
            def gather(g):
                pool.wait_ge(xgT_done, g + 1)
                pool.tensor_copy(idx_cur, idx_all[:, bass.ds(g, 1)]).then_inc(idx_ready, 1)
                pool.wait_ge(idx_ready, g)
                pool.sem_inc(passed, 1)
                pool.indirect_dma_start(xg, None, z_rows.ap(),
                                        bass.IndirectOffsetOnAxis(ap=idx_cur, axis=0)).then_inc(gathered, 16)
                pool.wait_ge(gathered, g * 16 + 16)

            with pool.Fori(1, total + 1) as g:
                gather(g)

            pool.wait_ge(lo_ready, 3 * NE * QUARTERS)
            pool.dma_start(ln_g, ffn_g[0].partition_broadcast(P)).then_inc(ffn_in, 16)
            pool.dma_start(ln_b, ffn_b[0].partition_broadcast(P)).then_inc(ffn_in, 16)
            pool.wait_ge(y_out, total * 16 + 16)
            pool.sem_inc(passed, 1)

            def gain(t):
                pool.wait_ge(fn_ready, t + 1)
                pool.tensor_tensor(fin[:, t % YBUF], fin[:, t % YBUF], ln_g, ALU.mult).then_inc(gained, 1)

            for t in range(NT):
                if t >= YBUF:
                    pool.wait_ge(yg_free, t - YBUF + 1)
                for j in range(2):
                    pool.indirect_dma_start(ygath[:, t % YBUF, j], None, y_rows.ap(),
                                            bass.IndirectOffsetOnAxis(ap=slot_i[:, j, t:t + 1], axis=0)
                                            ).then_inc(y_in[t % YBUF][j], 16)
                if t == 0:
                    pool.wait_ge(ffn_in, 32)
                if t >= 3:
                    gain(t - 3)
            for t in range(NT - 3, NT):
                gain(t)

        @block.scalar
        def _(act):
            for t in range(NT):
                act.dma_start(xn[:, t], x_v[:, t]).then_inc(x_in[t], 16)
            act.wait_ge(c_in, 16)
            nc.scalar.activation(cond, craw, ACT.Silu).then_inc(cond_ready, 1)

            def normalise(t):
                b = t % 2
                act.wait_ge(var_ready, t + 1)
                nc.scalar.activation(l_std[:, b:b + 1], aggr[:, b, 1:2], ACT.Sqrt, bias=eps_c).then_inc(std_ready, 1)
                act.wait_ge(xn_inv, t + 1)
                nc.scalar.activation(xn[:, t], xn[:, t], ACT.Identity, scale=l_rstd[:, b:b + 1], bias=l_nb[:, b:b + 1]
                                     ).then_inc(xn_ready, 1)

            for t in range(4):
                normalise(t)
            def split_in(b):
                n = PROJ_ORDER.index(b)
                place, uses = place_use("in", b)
                src = places[place].rearrange("p k n -> p (k n)")
                act.wait_ge(place_loaded[place], 16 * uses)
                for k in range(QUARTERS):
                    if n >= 1 and k < QUARTERS - 1:
                        act.wait_ge(in_used, (QUARTERS - 1) * (n - 1) + k + 1)
                    elif n >= 1:
                        act.wait_ge(proj_done, NT * n)
                    nc.scalar.activation(in_w[0][:, quarter(k)], src[:, quarter(k)], ACT.Copy).then_inc(in_hi, 1)

            act.wait_ge(mod_done, 3)
            split_in(RQ)
            act.wait_ge(mod_stored, 4)

            def store_hT(t):
                act.wait_ge(turned, 2 * t + 1)
                if t >= 2:
                    act.wait_ge(hT_stored, t - 1)
                for k in range(4):
                    last = nc.scalar.activation(hTf[:, t % 2, k * P:(k + 1) * P], bank((5, 7)[t % 2])[:, k * P:(k + 1) * P],
                                                ACT.Identity, scale=modcol[:, 1, k:k + 1], bias=modcol[:, 0, k:k + 1])
                last.then_inc(hT_act, 1)
                act.wait_ge(hT_act, t + 1)
                act.wait_ge(hT_dve, t + 1)
                nc.scalar.activation(hT_hi[:].rearrange("p (k s) -> p k s", k=KC)[:, :, t * P:(t + 1) * P],
                                     hTf[:, t % 2].rearrange("p (k n) -> p k n", k=KC), ACT.Copy).then_inc(hT_hi_ready, 1)

            store_hT(0)
            store_hT(1)
            act.wait_ge(lam_sums, 1)
            nc.scalar.activation(lam4[:, 2:4], lam4[:, 0:2], ACT.Exp).then_inc(lam_exp, 1)
            for i in range(2 * NT):
                t = i % NT
                if i + 2 < NT:
                    store_hT(i + 2)
                if i + 4 < NT:
                    normalise(i + 4)
                if i == NT - 2:
                    split_in(RK)
                if i == 2 * NT - 2:
                    split_in(RV)
                act.wait_ge(rotT_done, i + 1)
                nc.scalar.activation((rqT, rkT)[i // NT][:, :, t * P:(t + 1) * P],
                                     bank(3 + i % 2).rearrange("p (c n) -> p c n", c=PAIRS), ACT.Copy
                                     ).then_inc(rotT_stored, 1)

            def from_projection(g, dst, func=ACT.Copy, scale=1.0):
                act.wait_ge(proj_done, g + 1)
                nc.scalar.activation(dst, bank(g % 2), func, scale=scale).then_inc(proj_free[g % 2], 1)

            split_in(RG)
            for n in range(NT):
                if n == NT - 1:
                    split_in(DV)
                if n >= 2:
                    act.wait_ge(ret_stored, n - 1)
                from_projection(3 * NT + n, rgs[n % 2], ACT.Silu)
                act.wait_ge(rvar_ready, n + 1)
                nc.scalar.activation(hstd, hvar, ACT.Sqrt, bias=eps_c, scale=1.0 / DH).then_inc(rstd_ready, 1)
            for t in range(NT):
                if t == NT - 1:
                    split_in(DQ)
                from_projection(4 * NT + t, dv[:, t])
            act.wait_ge(ret_stored, NT)
            for j in range(NT):
                if j == NT - 1:
                    split_in(DK)
                g = 5 * NT + j
                act.wait_ge(proj_done, g + 1)
                for q in range(2):
                    rows = slice(q * DH, (q + 1) * DH)
                    last = nc.scalar.activation(dqT[q][rows, j // 2, (j % 2) * H:(j % 2 + 1) * H], bank(g % 2)[rows, :],
                                                ACT.Copy, scale=DH ** -0.5)
                last.then_inc(proj_free[g % 2], 1)
            for j in range(NT):
                from_projection(6 * NT + j, dkT[:, j // 2, (j % 2) * H:(j % 2 + 1) * H])

            def exps(i, q):
                act.wait_ge(max_ready, 2 * i + q + 1)
                if i >= 2:
                    act.wait_ge(aT_done, i - 1)
                nc.scalar.activation(probs[:, i % 2, q, 0:keys(i // DIFF_H)], bank2(2 * q)[:, 0:keys(i // DIFF_H)],
                                     ACT.Exp, bias=negmax[:, i % 2, q:q + 1], accum_out=zsum[:, i % 2, q:q + 1]
                                     ).then_inc(exp_done[q], 1)

            def store_turned(i):
                act.wait_ge(aT_done, i + 1)
                if i >= 2:
                    act.wait_ge(av_done, i - 1)
                nc.scalar.activation(aT[:, i % 2, 0:keys(i // DIFF_H)], bank2(4)[:, 0:keys(i // DIFF_H)], ACT.Copy
                                     ).then_inc(aT_stored, 1)

            for i in range(NT * DIFF_H):
                exps(i, 0)
                if i >= 1:
                    store_turned(i - 1)
                exps(i, 1)
            ahead = (NT - 1) * DIFF_H
            act.wait_ge(ssq_ready, NT - 1)
            nc.scalar.activation(ssq[:, 0:ahead], ssq[:, 0:ahead], ACT.Sqrt, bias=eps_c, scale=1.0 / P).then_inc(rms_std, 1)
            store_turned(NT * DIFF_H - 1)
            act.wait_ge(ssq_ready, NT)
            nc.scalar.activation(ssq[:, ahead:], ssq[:, ahead:], ACT.Sqrt, bias=eps_c, scale=1.0 / P).then_inc(rms_std, 1)

            def store_mixT(t):
                act.wait_ge(mixT_done, t + 1)
                if t >= 2:
                    act.wait_ge(o_done, t - 1)
                nc.scalar.activation(mixT[t % 2], bank2(0).rearrange("p (k n) -> p k n", k=KC), ACT.Copy
                                     ).then_inc(mixT_stored, 1)

            def mixed(t):
                b = t % 2
                if t == 0:
                    act.wait_ge(av_done, NT * DIFF_H)
                    for n in range(2):
                        act.dma_start(xr[:, n], x_v[:, n]).then_inc(xr_in[n], 16)
                elif t + 1 < NT:
                    wait_nonzero(act, ovar, t)
                    act.dma_start(xr[:, (t + 1) % 2], x_v[:, t + 1]).then_inc(xr_in[(t + 1) % 2], 16)
                act.wait_ge(ovar, t + 1)
                nc.scalar.activation(l_std[:, b:b + 1], aggr[:, b, 1:2], ACT.Sqrt, bias=eps_c).then_inc(ostd, 1)
                act.wait_ge(orstd, t + 1)
                nc.scalar.activation(u[:, b], u[:, b], ACT.Identity, scale=l_rstd[:, b:b + 1], bias=l_nb[:, b:b + 1]
                                     ).then_inc(un_ready, 1)

            def renormed(t):
                b = t % 2
                act.wait_ge(zvar, t + 1)
                nc.scalar.activation(z_std[:, b:b + 1], z_aggr[:, b, 1:2], ACT.Sqrt, bias=eps_c).then_inc(zstd, 1)
                act.wait_ge(zrstd, t + 1)
                if t >= 2:
                    act.wait_ge(z_out[b], 16 * (t // 2))
                    act.wait_ge(zT_done, t - 1)
                nc.scalar.activation(z[:, b], x1[:, t], ACT.Identity, scale=z_rstd[:, b:b + 1], bias=z_nb[:, b:b + 1]
                                     ).then_inc(z_ready, 1)
                act.wait_ge(z_ready, t + 1)
                nc.scalar.activation(x1[:, t], x1[:, t], ACT.Copy, scale=ALPHA).then_inc(x1_scaled, 1)
                act.dma_start(z_rows.ap()[t * P:(t + 1) * P, :], z[:, b]).then_inc(z_out[b], 16)
                act.wait_ge(x1_scaled, t + 1)
                act.dma_start(x1_rows.ap()[t * P:(t + 1) * P, :], x1[:, t]).then_inc(x1_out, 16)

            def modulated(t):
                act.wait_ge(zT_done, t + 1)
                wait_nonzero(act, logits_done, t)
                for k in range(4):
                    last = nc.scalar.activation(h2T[:, k], bank(4)[:, k * P:(k + 1) * P], ACT.Identity,
                                                scale=modcol[:, 3, k:k + 1], bias=modcol[:, 2, k:k + 1])
                last.then_inc(h2_act, 1)

            def split_hi(dst, parity, loaded, quarters=range(QUARTERS)):
                for k in quarters:
                    act.wait_ge(raw_in[parity][k], loaded)
                    nc.scalar.activation(dst[:, quarter(k)], raw[parity][:, quarter(k)], ACT.Copy).then_inc(hi_ready, 1)

            store_mixT(0)
            for t in range(NT + 2):
                if 2 <= t < 2 + QUARTERS:
                    split_hi(gate_w[0][0], 0, 16, [t - 2])
                if t + 1 < NT:
                    store_mixT(t + 1)
                if t >= 2:
                    modulated(t - 2)
                if t < NT:
                    mixed(t)
                if 1 <= t <= NT:
                    renormed(t - 1)
            act.wait_ge(lmax_ready, 1)
            nc.scalar.activation(r_exp, r_exp, ACT.Exp).then_inc(lexp_done, 1)

            def modulate_gathered(g):
                for k in range(4):
                    last = nc.scalar.activation(hgf[:, k * P:(k + 1) * P], bank(2)[:, k * P:(k + 1) * P],
                                                ACT.Identity, scale=modcol[:, 3, k:k + 1], bias=modcol[:, 2, k:k + 1])
                last.then_inc(hg_act, 1)
                act.wait_ge(hg_act, g + 1)
                act.wait_ge(hg_dve, g + 1)
                nc.scalar.activation(hg_parts[0][:], hgf, ACT.Copy).then_inc(hg_hi_ready, 1)

            def expert_tile(g, first=None, i=None, q=None):
                if first is not None:
                    nc.scalar.activation(r_spare, eps_c, ACT.Silu)
                    act.wait_ge(up_done, first + 1)
                    split_hi(up_w[0], *raw_count(i, q, 1))
                act.wait_ge(gate_done, g + 1)
                act.wait_ge(he_ready, g * 2 + 2)
                nc.scalar.activation(sg, bank(0), ACT.Silu).then_inc(silu_done, 1)
                if first is not None:
                    act.wait_ge(y_done, first + 1)
                    split_hi(down_w[0], *raw_count(i, q, 2))
                act.wait_ge(y_done, g + 1)
                for r in range(2):
                    act.wait_ge(heT_done, g * 2 + (3 + r))
                    nc.scalar.activation(heT_parts[0][:, he_half[r]], bank((4, 7)[r])[:, 0:DE // 2], ACT.Copy
                                         ).then_inc(heT_hi_ready, 1)
                act.wait_ge(xgT_done, g + 3)
                act.wait_ge(hg_stored, g + 1)
                modulate_gathered(g + 1)
                if first is not None:
                    def split_next_gate():
                        split_hi(gate_w[1 - q][0], *raw_count(i, q, 3))
                    if q == 0:
                        split_next_gate()
                    else:
                        with act.If(i < NE // 2 - 1):
                            split_next_gate()
            act.wait_ge(starts_ready, 1)
            act.sem_inc(silu_done, 1)
            act.wait_ge(x1_out, 16 * NT)
            act.wait_ge(z_out[0], 16 * NT // 2)
            act.wait_ge(z_out[1], 16 * NT // 2)
            act.wait_ge(zT_done, NT)
            act.wait_ge(xgT_done, 2)
            modulate_gathered(0)
            with act.Fori(0, NE // 2) as i:
                for q in range(2):
                    first = act.value_load(ts_i[0:1, bass.ds(i * 2 + q, 1)], min_val=0, max_val=MAX_TILES - 1)
                    end = act.value_load(ts_i[0:1, bass.ds(i * 2 + (q + 1), 1)], min_val=1, max_val=MAX_TILES)
                    expert_tile(first, first, i, q)
                    with act.If(first + 1 < end):
                        with act.Fori(first + 1, end) as g:
                            expert_tile(g)

            def weigh(t):
                y1 = ygath[:, t % YBUF, 1]
                act.wait_ge(y_in[t % YBUF][1], 16 * (t // YBUF + 1))
                nc.scalar.activation(y1, y1, ACT.Copy, scale=gates[:, 1, t:t + 1]).then_inc(y1_scaled, 1)

            weigh(0)
            for t in range(NT):
                b = t % 2
                if t + 1 < NT:
                    weigh(t + 1)
                act.wait_ge(fvar, t + 1)
                nc.scalar.activation(l_std[:, b:b + 1], aggr[:, b, 1:2], ACT.Sqrt, bias=eps_c).then_inc(fstd, 1)
                act.wait_ge(frstd, t + 1)
                if t >= YBUF:
                    act.wait_ge(out_done[t % YBUF], 16 * (t // YBUF))
                nc.scalar.activation(fin[:, t % YBUF], x1_end[:, t], ACT.Identity, scale=l_rstd[:, b:b + 1],
                                     bias=l_nb[:, b:b + 1]).then_inc(fn_ready, 1)

        @block.vector
        def _(dve):
            steps = [0]

            def link(ins):
                steps[0] += 1
                ins.then_inc(dve_step, 1)
                dve.wait_ge(dve_step, steps[0])

            def mark(ins):
                steps[0] += 1
                ins.then_inc(dve_step, 1)

            def wait_marks():
                dve.wait_ge(dve_step, steps[0])

            def statistics(src, st, ag, ready):
                mark(nc.vector.bn_stats(st[:, 0:6], src[:, 0:H]))
                mark(nc.vector.bn_stats(st[:, 6:12], src[:, H:D]))
                wait_marks()
                nc.vector.bn_aggr(ag, st.rearrange("p (s n) -> p s n", s=2)).then_inc(ready, 1)

            def invert(sd, ag, rs, nb, ready):
                link(nc.vector.reciprocal(rs, sd))
                nc.vector.tensor_scalar(nb, ag[:, 0:1], rs, -1.0, ALU.mult, ALU.mult).then_inc(ready, 1)

            mark(nc.vector.memset(eps_c, EPS))
            mark(nc.vector.memset(state, 0.0))
            nc.vector.memset(ones[:], 1.0).then_inc(ones_ready, 1)
            wait_marks()
            dve.wait_ge(cond_ready, 1)

            def ada_sum(b):
                place, uses = place_use("ada", b)
                w = places[place]
                dve.wait_ge(place_loaded[place], 16 * uses)
                link(nc.vector.tensor_scalar(w[:, 0, :], w[:, 0, :], cond[:, 0:1], None, ALU.mult))
                for k in range(1, KC):
                    ins = nc.vector.scalar_tensor_tensor(out=w[:, 0, :], in0=w[:, k, :], scalar=cond[:, k:k + 1],
                                                         in1=w[:, 0, :], op0=ALU.mult, op1=ALU.add)
                    if k < KC - 1:
                        link(ins)
                ins.then_inc(ada_summed, 1)

            def mod_store(b):
                dve.wait_ge(mod_done, ADA_ORDER.index(b) + 1)
                vec, half = b // 2, b % 2
                if vec in (2, 5):
                    dst = (g1b if vec == 2 else g2b[:, :])[:, half * H:(half + 1) * H]
                    nc.vector.tensor_copy(dst, mod_bank(b)).then_inc(mod_stored, 1)
                else:
                    at, one = {0: (0, 0.0), 1: (1, 1.0), 3: (2, 0.0), 4: (3, 1.0)}[vec]
                    nc.vector.tensor_scalar(modcol[:, at, half * 4:half * 4 + 4], mod_bank(b)[:, 0:4], one, None,
                                            ALU.add).then_inc(mod_stored, 1)

            def x_statistics(t):
                dve.wait_ge(x_in[t], 16)
                if t >= 2:
                    dve.wait_ge(xn_ready, t - 1)
                statistics(xn[:, t], stat[:, t % 2], aggr[:, t % 2], var_ready)

            def x_invert(t):
                b = t % 2
                dve.wait_ge(std_ready, t + 1)
                invert(l_std[:, b:b + 1], aggr[:, b], l_rstd[:, b:b + 1], l_nb[:, b:b + 1], xn_inv)

            def split_in(b):
                n = PROJ_ORDER.index(b)
                src = places[place_use("in", b)[0]].rearrange("p k n -> p (k n)")
                for k in range(QUARTERS):
                    dve.wait_ge(in_hi, QUARTERS * n + k + 1)
                    nc.vector.tensor_tensor(in_w[1][:, quarter(k)], src[:, quarter(k)], in_w[0][:, quarter(k)].bitcast(f32),
                                            ALU.subtract).then_inc(in_lo, 1)

            for m in range(4):
                ada_sum(m)
                if m == 3:
                    split_in(RQ)
                for step in (x_statistics, x_invert):
                    for t in ((0, 1), (2,), (3,), ())[m]:
                        step(t)
                mod_store(m)
            dve.wait_ge(mod_stored, 4)

            def modulate_hT(t):
                dve.wait_ge(turned, 2 * t + 2)
                if t >= 2:
                    dve.wait_ge(hT_stored, t - 1)
                for k in range(4, KC):
                    last = nc.vector.tensor_scalar(hTf[:, t % 2, k * P:(k + 1) * P],
                                                   bank((6, 2)[t % 2])[:, (k - 4) * P:(k - 3) * P],
                                                   modcol[:, 1, k:k + 1], modcol[:, 0, k:k + 1], ALU.mult, ALU.add)
                last.then_inc(hT_dve, 1)

            def split_hT(t):
                dve.wait_ge(hT_hi_ready, t + 1)
                hi = hT_hi[:].rearrange("p (k s) -> p k s", k=KC)
                full = hTf[:, t % 2].rearrange("p (k n) -> p k n", k=KC)
                here = slice(t * P, (t + 1) * P)
                for r in range(2):
                    ks = slice(4 * r, 4 * r + 4)
                    ins = nc.vector.tensor_tensor(hT_lo[r][:].rearrange("p (k s) -> p k s", k=4)[:, :, here], full[:, ks],
                                                  hi[:, ks, here].bitcast(f32), ALU.subtract)
                    if r == 0:
                        mark(ins)
                ins.then_inc(hT_stored, 1)

            modulate_hT(0)
            split_hT(0)
            modulate_hT(1)
            split_hT(1)
            dve.wait_ge(small_in, 112)
            for i in range(2):
                link(nc.vector.tensor_tensor(lamv[:, 2 * i, :], lamv[:, 2 * i, :], lamv[:, 2 * i + 1, :], ALU.mult))
                ins = nc.vector.tensor_reduce(lam4[:, i:i + 1], lamv[:, 2 * i, :], AX.X, ALU.add)
                if i == 0:
                    mark(ins)
            ins.then_inc(lam_sums, 1)
            mark(nc.vector.tensor_scalar(subg[:], subg[:], 1.0 - LAMBDA_INIT, None, ALU.mult))
            dve.wait_ge(consts_in, 16)
            for i in range(2 * NT):
                t = i % NT
                if i + 2 < NT:
                    modulate_hT(i + 2)
                if i == NT - 1:
                    split_in(RK)
                if i == NT + 3:
                    ada_sum(6)
                if i == NT + 6:
                    mod_store(6)
                if i == 2 * NT - 1:
                    split_in(RV)
                dve.wait_ge(proj_done, i + 1)
                v = bank(i % 2).rearrange("p (h a d) -> p h a d", h=RET_H, a=2)
                ta = t1.rearrange("p (h a d) -> p h a d", h=RET_H, a=2)
                tb = t2.rearrange("p (h a d) -> p h a d", h=RET_H, a=2)
                sin_b = bc(sin_t[:, t], [P, RET_H, 32], (1,))
                wait_marks()
                wait_nonzero(dve, rot_ready, i)
                mark(nc.vector.tensor_tensor(ta, v, bc(cos_t[:, t], [P, RET_H, 2, 32], (1, 1)), ALU.mult))
                mark(nc.vector.tensor_tensor(tb[:, :, 0], v[:, :, 1], sin_b, ALU.mult))
                nc.vector.tensor_tensor(tb[:, :, 1], v[:, :, 0], sin_b, ALU.mult).then_inc(proj_free[i % 2], 1)
                wait_marks()
                dve.wait_ge(proj_free[i % 2], i // 2 + 1)
                if 2 <= i < NT:
                    dve.wait_ge(rotT_done, i - 1)
                dst = (qrot[:, t % 2] if i < NT else rk[:, t]).rearrange("p (h a d) -> p h a d", h=RET_H, a=2)
                mark(nc.vector.tensor_tensor(dst[:, :, 0], ta[:, :, 0], tb[:, :, 0], ALU.subtract))
                nc.vector.tensor_tensor(dst[:, :, 1], ta[:, :, 1], tb[:, :, 1], ALU.add).then_inc(rot_ready, 1)
                if i + 4 < NT:
                    x_statistics(i + 4)
                    x_invert(i + 4)
                if i + 2 < NT:
                    split_hT(i + 2)
            for t in range(NT):
                if t == 3:
                    ada_sum(7)
                if t == 6:
                    mod_store(7)
                if t == NT - 1:
                    split_in(RG)
                g = 2 * NT + t
                dve.wait_ge(proj_done, g + 1)
                nc.vector.tensor_tensor(vs[:, t].rearrange("p (h d) -> p h d", h=RET_H),
                                        bank(g % 2).rearrange("p (h d) -> p h d", h=RET_H),
                                        bc(const("v_decay"), [P, RET_H, DH], (2,)), ALU.mult
                                        ).then_inc(proj_free[g % 2], 1)

            dve.wait_ge(rot_ready, 2 * NT)
            for n in range(NT):
                dve.wait_ge(rs_done, n + 1)
                wait_nonzero(dve, ro_done, n)
                mark(nc.vector.tensor_tensor(pm[:, 0], bank(3).rearrange("p (c n) -> p c n", c=PAIRS),
                                             bc(const("causal"), [P, PAIRS, P], (1,)), ALU.mult))
                nc.vector.tensor_tensor(pm[:, 1], bank(4).rearrange("p (c n) -> p c n", c=PAIRS),
                                        bc(const("causal"), [P, PAIRS, P], (1,)), ALU.mult).then_inc(rp_ready, 1)
                if n == 3:
                    ada_sum(8)
                if n == 5:
                    mod_store(8)
                if n == NT - 1:
                    split_in(DV)
                dve.wait_ge(ro_done, n + 1)
                oh = t1.rearrange("p (h d) -> p h d", h=RET_H)
                xc = t2.rearrange("p (h d) -> p h d", h=RET_H)
                sq = qrot[:, 0].rearrange("p (h d) -> p h d", h=RET_H)
                wait_marks()
                nc.vector.tensor_tensor(oh, bank(5).rearrange("p (h d) -> p h d", h=RET_H),
                                        bc(const("q_decay"), [P, RET_H, DH], (2,)), ALU.mult).then_inc(ro_free, 1)
                if n < NT - 1:
                    dve.wait_ge(kv_done, n + 1)
                    kv = bank(7).rearrange("p (c n) -> p c n", c=PAIRS)
                    heads = [(slice(0, DH), slice(0, DH)), (slice(DH, P), slice(DH, P))]
                    for rows, at in heads:
                        mark(nc.vector.tensor_tensor(state_new[rows], kv[rows, :, at], state[rows, :, at], ALU.add))
                    wait_marks()
                    for rows, at in heads:
                        ins = nc.vector.tensor_tensor(state[rows, :, at], state_new[rows],
                                                      bc(const("chunk_decay")[rows], [DH, PAIRS, DH], (2,)), ALU.mult)
                        if rows.start == 0:
                            mark(ins)
                    ins.then_inc(state_ready, 1)
                    dve.wait_ge(state_ready, n + 1)
                wait_marks()
                dve.wait_ge(ro_free, n + 1)
                link(nc.vector.tensor_reduce(hsum, oh, AX.X, ALU.add))
                link(nc.vector.tensor_scalar(hsum, hsum, 1.0 / DH, None, ALU.mult))
                link(nc.vector.tensor_tensor(xc, oh, bc(hsum, [P, RET_H, DH], (2,)), ALU.subtract))
                link(nc.vector.tensor_tensor(sq, xc, xc, ALU.mult))
                nc.vector.tensor_reduce(hvar, sq, AX.X, ALU.add).then_inc(rvar_ready, 1)
                dve.wait_ge(rstd_ready, n + 1)
                link(nc.vector.reciprocal(hstd, hstd))
                link(nc.vector.tensor_tensor(xc, xc, bc(hstd, [P, RET_H, DH], (2,)), ALU.mult))
                dve.wait_ge(proj_free[n % 2], (3 * NT + n) // 2 + 1)
                mark(nc.vector.tensor_tensor(ret_out[:, n], t2, rgs[n % 2], ALU.mult))
                wait_marks()
                dve.sem_inc(ret_stored, 1)
            dve.wait_ge(lam_exp, 1)
            link(nc.vector.tensor_tensor(nlam, lam4[:, 3:4], lam4[:, 2:3], ALU.subtract))
            mark(nc.vector.tensor_scalar(nlam, nlam, -LAMBDA_INIT, None, ALU.add))
            for b, block in ((9, DQ), (10, DK), (11, None), (4, None)):
                ada_sum(b)
                if b == 10:
                    dve.wait_ge(y_zeroed, 16 * (MAX_TILES - NE))
                mod_store(b)
                if block is not None:
                    split_in(block)

            def maxima(i):
                for q in range(2):
                    dve.wait_ge(s_done[q], i + 1)
                    nc.vector.tensor_reduce(negmax[:, i % 2, q:q + 1], bank2(2 * q)[:, 0:keys(i // DIFF_H)], AX.X, ALU.max,
                                            negate=True).then_inc(max_ready, 1)

            def combine(i):
                b, qb, h = i % 2, i // DIFF_H, i % DIFF_H
                dve.wait_ge(exp_done[0], i + 1)
                dve.wait_ge(exp_done[1], i + 1)
                link(nc.vector.reciprocal(zinv[:, b], zsum[:, b]))
                mark(nc.vector.tensor_copy(r1[:, qb % 2, h:h + 1], zinv[:, b, 0:1]))
                link(nc.vector.scalar_tensor_tensor(out=zinv[:, b, 1:2], in0=zinv[:, b, 1:2], scalar=zsum[:, b, 0:1],
                                                    in1=nlam, op0=ALU.mult, op1=ALU.mult))
                nc.vector.scalar_tensor_tensor(out=probs[:, b, 0, 0:keys(qb)], in0=probs[:, b, 1, 0:keys(qb)],
                                               scalar=zinv[:, b, 1:2], in1=probs[:, b, 0, 0:keys(qb)],
                                               op0=ALU.mult, op1=ALU.add).then_inc(a_ready, 1)

            def heads_out(qb):
                dve.wait_ge(av_done, DIFF_H * (qb + 1))
                o = dif_out[:, qb].rearrange("p (h e) -> p h e", h=DIFF_H)
                nc.vector.tensor_tensor(o, bank(6).rearrange("p (h e) -> p h e", h=DIFF_H),
                                        bc(r1[:, qb % 2], [P, DIFF_H, P], (2,)), ALU.mult).then_inc(av_free, 1)
                dve.wait_ge(av_free, qb + 1)
                link(nc.vector.tensor_tensor(sqt.rearrange("p (h e) -> p h e", h=DIFF_H), o, o, ALU.mult))
                nc.vector.tensor_reduce(ssq[:, qb * DIFF_H:(qb + 1) * DIFF_H], sqt.rearrange("p (h e) -> p h e", h=DIFF_H),
                                        AX.X, ALU.add).then_inc(ssq_ready, 1)

            maxima(0)
            for i in range(NT * DIFF_H):
                if i % DIFF_H == 1 and i > 1:
                    heads_out(i // DIFF_H - 1)
                combine(i)
                if i + 1 < NT * DIFF_H:
                    maxima(i + 1)
                if i == 5:
                    ada_sum(5)
                if i == 7:
                    mod_store(5)
            def mix(t):
                o = dif_out[:, t].rearrange("p (h e) -> p h e", h=DIFF_H)
                link(nc.vector.tensor_tensor(o, o, bc(ssq[:, t * DIFF_H:(t + 1) * DIFF_H], [P, DIFF_H, P], (2,)), ALU.mult))
                nc.vector.tensor_tensor(o, o, bc(subg[:], [P, DIFF_H, P], (1,)), ALU.mult).then_inc(mix_ready, 1)

            def mixed(t):
                b = t % 2
                dve.wait_ge(o_done, t + 1)
                nc.vector.tensor_tensor(u[:, b], bank2(2), g1b, ALU.mult).then_inc(o_free, 1)
                dve.wait_ge(o_free, t + 1)
                dve.wait_ge(xr_in[b], 16 * (t // 2 + 1))
                link(nc.vector.scalar_tensor_tensor(out=u[:, b], in0=xr[:, b], scalar=ALPHA, in1=u[:, b],
                                                    op0=ALU.mult, op1=ALU.add))
                statistics(u[:, b], stat[:, b], aggr[:, b], ovar)
                dve.wait_ge(ostd, t + 1)
                invert(l_std[:, b:b + 1], aggr[:, b], l_rstd[:, b:b + 1], l_nb[:, b:b + 1], orstd)

            def renormed(t):
                b = t % 2
                dve.wait_ge(x1_ready, t + 1)
                statistics(x1[:, t], z_stat[:, b], z_aggr[:, b], zvar)
                dve.wait_ge(zstd, t + 1)
                invert(z_std[:, b:b + 1], z_aggr[:, b], z_rstd[:, b:b + 1], z_nb[:, b:b + 1], zrstd)

            def modulated(t):
                dve.wait_ge(zT_done, t + 1)
                wait_nonzero(dve, logits_done, t)
                for k in range(4, KC):
                    last = nc.vector.tensor_scalar(h2T[:, k], bank(5)[:, (k - 4) * P:(k - 3) * P],
                                                   modcol[:, 3, k:k + 1], modcol[:, 2, k:k + 1], ALU.mult, ALU.add)
                last.then_inc(h2_dve, 1)

            def split_lo(parts, parity, count):
                for k in range(QUARTERS) if callable(count) else [count]:
                    dve.wait_ge(hi_ready, count(k) if callable(count) else k + 1)
                    nc.vector.tensor_tensor(parts[1][:, quarter(k)], raw[parity][:, quarter(k)],
                                            parts[0][:, quarter(k)].bitcast(f32), ALU.subtract).then_inc(lo_ready, 1)

            ahead = (NT - 1) * DIFF_H
            dve.wait_ge(rms_std, 1)
            link(nc.vector.reciprocal(ssq[:, 0:ahead], ssq[:, 0:ahead]))
            mix(0)
            mix(1)
            heads_out(NT - 1)
            dve.wait_ge(rms_std, 2)
            link(nc.vector.reciprocal(ssq[:, ahead:], ssq[:, ahead:]))
            for t in range(NT + 2):
                if 2 <= t < 2 + QUARTERS:
                    split_lo(gate_w[0], 0, t - 2)
                if t + 2 < NT:
                    mix(t + 2)
                if t >= 2:
                    modulated(t - 2)
                if t < NT:
                    mixed(t)
                if 1 <= t <= NT:
                    renormed(t - 1)

            dve.wait_ge(logits_done, NT)
            te = lambda a: a.rearrange("p (t e) -> p t e", e=NE)
            link(nc.vector.tensor_tensor(te(r_exp), te(bank(7)[:, 0:NT * NE]), bc(router_bc[:], [P, NT, NE], (1,)), ALU.add))
            link(nc.vector.tensor_reduce(r_row, te(r_exp), AX.X, ALU.max))
            nc.vector.tensor_tensor(te(r_exp), te(r_exp), bc(r_row, [P, NT, NE], (2,)), ALU.subtract).then_inc(lmax_ready, 1)
            dve.wait_ge(lexp_done, 1)
            link(nc.vector.tensor_reduce(r_row, te(r_exp), AX.X, ALU.add))
            link(nc.vector.reciprocal(r_row, r_row))
            link(nc.vector.tensor_tensor(te(r_prob), te(r_exp), bc(r_row, [P, NT, NE], (2,)), ALU.mult))

            lower = const("lower").rearrange("p (e j) -> p e j", e=EPG)

            def ranks(values, n, gt, ge, rank):
                v = values.rearrange("p (g e) -> p g e", e=EPG)
                g4 = gt.rearrange("p (g e j) -> p g e j", e=EPG, j=EPG)
                q4 = ge.rearrange("p (g e j) -> p g e j", e=EPG, j=EPG)
                vj, ve = bc(v, [P, n, EPG, EPG], (2,)), bc(v, [P, n, EPG, EPG], (3,))
                mark(nc.vector.tensor_tensor(g4, vj, ve, ALU.is_gt))
                link(nc.vector.tensor_tensor(q4, vj, ve, ALU.is_equal))
                link(nc.vector.tensor_tensor(q4, q4, bc(lower, [P, n, EPG, EPG], (1,)), ALU.mult))
                link(nc.vector.tensor_tensor(g4, g4, q4, ALU.add))
                link(nc.vector.tensor_reduce(rank, g4, AX.X, ALU.add))

            ranks(r_prob, NT * NG, r_gt, r_eq, r_rank)
            link(nc.vector.tensor_scalar(r_mask, r_rank, 1.5, None, ALU.is_lt))
            link(nc.vector.tensor_tensor(r_tmp, r_prob, r_mask, ALU.mult))
            link(nc.vector.tensor_reduce(r_group, r_tmp.rearrange("p (g e) -> p g e", e=EPG), AX.X, ALU.add))
            ranks(r_group, NT, r_gt[:, 0:NT * 16], r_eq[:, 0:NT * 16], r_grank)
            link(nc.vector.tensor_scalar(r_grank, r_grank, 0.5, None, ALU.is_lt))
            gm = r_mask.rearrange("p (g e) -> p g e", e=EPG)
            nc.vector.tensor_tensor(gm, gm, bc(r_grank, [P, NT * NG, EPG], (2,)), ALU.mult).then_inc(mask_ready, 1)
            dve.wait_ge(mask_ready, 1)
            dve.wait_ge(count_done, 1)
            mark(nc.vector.memset(r_off[:, 0:NE], 0.0))
            link(nc.vector.tensor_copy(r_tot, bank(1)[:, 0:NT * NE]))
            for t in range(1, NT + 1):
                link(nc.vector.tensor_tensor(r_off[:, t * NE:(t + 1) * NE], r_off[:, (t - 1) * NE:t * NE],
                                             r_tot[:, (t - 1) * NE:t * NE], ALU.add))
            link(nc.vector.tensor_tensor(r_pos, te(bank(0)[:, 0:NT * NE])[:, :, 0], te(r_off[:, 0:NT * NE])[:, :, 0], ALU.add))
            link(nc.vector.scalar_tensor_tensor(out=r_pos, in0=r_pos, scalar=1.0, in1=te(r_mask)[:, :, 0],
                                                op0=ALU.add, op1=ALU.mult))
            nc.vector.tensor_tensor(in_first, bc(const("slot_no"), [P, NT, P], (1,)), bc(r_pos, [P, NT, P], (2,)),
                                    ALU.is_equal).then_inc(in_first_ready, 1)
            r7 = r_gt[:, 0:NE * (NT - 1)].rearrange("p (e m) -> p e m", m=NT - 1)
            link(nc.vector.tensor_tensor(r7, bc(r_off[:, NT * NE:], [P, NE, NT - 1], (2,)),
                                         bc(const("steps"), [P, NE, NT - 1], (1,)), ALU.is_gt))
            link(nc.vector.tensor_reduce(r_tiles, r7, AX.X, ALU.add))
            link(nc.vector.tensor_scalar(r_tiles, r_tiles, 1.0, None, ALU.add))
            mark(nc.vector.memset(r_start[:, 0:1], 0.0))
            link(nc.vector.tensor_tensor_scan(r_start[:, 1:NE + 1], ones[:, 0:NE], r_tiles, 0.0, ALU.mult, ALU.add))
            nc.vector.tensor_copy(ts_i[:], r_start[0:1, :]).then_inc(starts_ready, 1)
            link(nc.vector.tensor_scalar(r_tiles, r_start[:, 0:NE], float(P), None, ALU.mult))
            link(nc.vector.tensor_tensor(r_tmp, bank(0)[:, 0:NT * NE], r_off[:, 0:NT * NE], ALU.add))
            link(nc.vector.tensor_tensor(te(r_tmp), te(r_tmp), bc(r_tiles, [P, NT, NE], (1,)), ALU.add))
            link(nc.vector.tensor_tensor(r_tmp, r_tmp, r_mask, ALU.mult))
            dve.wait_ge(first_done, 1)
            nc.vector.tensor_copy(idx_first, bank(2)[:, 0:1]).then_inc(first_ready, 1)
            link(nc.vector.tensor_reduce(r_hi, te(r_tmp), AX.X, ALU.max))
            link(nc.vector.tensor_tensor(te(r_tot), te(r_tmp), bc(r_hi, [P, NT, NE], (2,)), ALU.is_equal))
            mark(nc.vector.tensor_copy(slot_i[:, 1], r_hi))
            link(nc.vector.tensor_tensor(r_exp, r_mask, r_tot, ALU.subtract))
            link(nc.vector.tensor_tensor(r_tmp, r_exp, r_tmp, ALU.mult))
            link(nc.vector.tensor_reduce(r_lo, te(r_tmp), AX.X, ALU.add))
            link(nc.vector.tensor_copy(slot_i[:, 0], r_lo))
            mark(nc.vector.tensor_single_scalar(id_at[:], slot_i[:], 7, ALU.logical_shift_right))
            link(nc.vector.tensor_scalar(id_low, slot_i[:], P - 1, 5, ALU.bitwise_and, ALU.logical_shift_left))
            nc.vector.tensor_tensor(id_at[:], id_at[:], id_low, ALU.bitwise_or).then_inc(slots_ready, 1)
            link(nc.vector.tensor_tensor(r_prob, r_prob, r_mask, ALU.mult))
            link(nc.vector.tensor_reduce(r_row, te(r_prob), AX.X, ALU.add))
            link(nc.vector.reciprocal(r_row, r_row))
            link(nc.vector.tensor_tensor(te(r_prob), te(r_prob), bc(r_row, [P, NT, NE], (2,)), ALU.mult))
            for j, which in ((1, r_tot), (0, r_exp)):
                link(nc.vector.tensor_tensor(which, which, r_prob, ALU.mult))
                link(nc.vector.tensor_reduce(gates[:, j], te(which), AX.X, ALU.add))

            def modulate_gathered(g):
                for k in range(4, KC):
                    last = nc.vector.tensor_scalar(hgf[:, k * P:(k + 1) * P], bank(3)[:, (k - 4) * P:(k - 3) * P],
                                                   modcol[:, 3, k:k + 1], modcol[:, 2, k:k + 1], ALU.mult, ALU.add)
                last.then_inc(hg_dve, 1)
                dve.wait_ge(hg_hi_ready, g + 1)
                nc.vector.tensor_tensor(hg_parts[1][:], hgf, hg_parts[0][:].bitcast(f32), ALU.subtract
                                        ).then_inc(hg_stored, 1)

            def expert_tile(g, first=None, i=None, q=None):
                if first is not None:
                    for j, parts in ((1, up_w), (2, down_w)):
                        split_lo(parts, raw_count(i, q, j)[0], lambda k: split_count(i, q, j, k + 1))
                dve.wait_ge(silu_done, g + 2)
                dve.wait_ge(up_done, g + 2)
                dve.wait_ge(heT_done, g * 2 + 2)
                for r in range(2):
                    nc.vector.tensor_tensor(he[:, he_half[r]], sg[:, he_half[r]], bank(1)[:, he_half[r]], ALU.mult
                                            ).then_inc(he_ready, 1)
                for r in range(2):
                    dve.wait_ge(heT_hi_ready, g * 2 + (1 + r))
                    nc.vector.tensor_tensor(heT_parts[1][:, he_half[r]], bank((4, 7)[r])[:, 0:DE // 2],
                                            heT_parts[0][:, he_half[r]].bitcast(f32), ALU.subtract
                                            ).then_inc(heT_stored, 1)
                dve.wait_ge(xgT_done, g + 3)
                dve.wait_ge(hg_stored, g + 1)
                modulate_gathered(g + 1)
                if first is not None:
                    def split_next_gate():
                        split_lo(gate_w[1 - q], raw_count(i, q, 3)[0], lambda k: split_count(i, q, 3, k + 1))
                    if q == 0:
                        split_next_gate()
                    else:
                        with dve.If(i < NE // 2 - 1):
                            split_next_gate()
                dve.wait_ge(y_done, g + 2)
                dve.wait_ge(y_out, g * 16 + 16)
                nc.vector.tensor_tensor(yb, bank2(5), g2b[:], ALU.mult).then_inc(y_stored, 1)

            dve.wait_ge(starts_ready, 1)
            for buffer_free, halves in ((he_ready, 2), (heT_stored, 2), (y_stored, 1)):
                dve.sem_inc(buffer_free, halves)
            dve.wait_ge(xgT_done, 2)
            modulate_gathered(0)
            with dve.Fori(0, NE // 2) as i:
                for q in range(2):
                    first = dve.value_load(ts_i[0:1, bass.ds(i * 2 + q, 1)], min_val=0, max_val=MAX_TILES - 1)
                    end = dve.value_load(ts_i[0:1, bass.ds(i * 2 + (q + 1), 1)], min_val=1, max_val=MAX_TILES)
                    expert_tile(first, first, i, q)
                    with dve.If(first + 1 < end):
                        with dve.Fori(first + 1, end) as g:
                            expert_tile(g)

            def last_norm(t):
                b = t % 2
                dve.wait_ge(fstd, t + 1)
                invert(l_std[:, b:b + 1], aggr[:, b], l_rstd[:, b:b + 1], l_nb[:, b:b + 1], frstd)

            def bias(t):
                dve.wait_ge(gained, t + 1)
                nc.vector.tensor_tensor(fin[:, t % YBUF], fin[:, t % YBUF], ln_b, ALU.add).then_inc(biased, 1)

            dve.wait_ge(x1_in, 16)
            for t in range(NT):
                b, yb_t = t % 2, t % YBUF
                dve.wait_ge(y_in[yb_t][0], 16 * (t // YBUF + 1))
                dve.wait_ge(y1_scaled, t + 1)
                link(nc.vector.scalar_tensor_tensor(out=ygath[:, yb_t, 1], in0=ygath[:, yb_t, 0],
                                                    scalar=gates[:, 0, t:t + 1], in1=ygath[:, yb_t, 1],
                                                    op0=ALU.mult, op1=ALU.add))
                nc.vector.tensor_tensor(x1_end[:, t], x1_end[:, t], ygath[:, yb_t, 1], ALU.add).then_inc(yg_free, 1)
                if t >= 1:
                    last_norm(t - 1)
                dve.wait_ge(yg_free, t + 1)
                statistics(x1_end[:, t], stat[:, b], aggr[:, b], fvar)
                if t >= 2:
                    bias(t - 2)
            last_norm(NT - 1)
            bias(NT - 2)
            bias(NT - 1)

        @block.tensor
        def _(pe):
            mm, tr = nc.tensor.matmul, nc.tensor.transpose

            def modulation(b):
                m = ADA_ORDER.index(b)
                vec = b // 2
                pe.wait_ge(ada_summed, m + 1)
                if m >= 1:
                    pe.wait_ge(mod_stored, m)
                w, out_b = places[place_use("ada", b)[0]], mod_bank(b)
                if vec in (2, 5):
                    mm(out_b, ones[:], w[:, 0, :], start=True, stop=False)
                    last = mm(out_b, ident[0:12, b:b + 1].broadcast_to([12, P]), b12[:, :], start=False, stop=True)
                else:
                    for q in range(4):
                        mm(out_b[:, q:q + 1], w[:, 0, q * P:(q + 1) * P], ones[:, 0:1], start=True, stop=False)
                        last = mm(out_b[:, q:q + 1], b12[:, q * P:(q + 1) * P], ident[0:12, b:b + 1],
                                  start=False, stop=True)
                last.then_inc(mod_done, 1)

            pe.wait_ge(ones_ready, 1)
            pe.wait_ge(consts_in, 16)
            pe.wait_ge(b_in, 16)
            for b in range(4):
                modulation(b)
            pe.wait_ge(mod_stored, 4)
            def turn_x(t):
                pe.wait_ge(xn_ready, t + 1)
                if t >= 2:
                    pe.wait_ge(hT_stored, t - 1)
                for k in range(KC):
                    last = tr(bank(((5, 6), (7, 2))[t % 2][k // 4])[:, (k % 4) * P:(k % 4 + 1) * P],
                              xn[:, t, k * P:(k + 1) * P], ident)
                    if k % 4 == 3:
                        last.then_inc(turned, 1)

            def hT_part(part, k, a, b):
                if part == 0:
                    return hT_hi[:, k * S + a:k * S + b]
                return hT_lo[k // 4][:, (k % 4) * S + a:(k % 4) * S + b]

            def project(b, j):
                n = PROJ_ORDER.index(b)
                g = NT * n + j
                if g >= 2:
                    pe.wait_ge(proj_free[g % 2], g // 2)
                if n == 0:
                    pe.wait_ge(hT_stored, j + 1)
                for k in range(KC):
                    if j == 0 and k % 2 == 0:
                        pe.wait_ge(in_lo, QUARTERS * n + k // 2 + 1)
                    for left, right in ((0, 0), (0, 1), (1, 0)):
                        if b in (DQ, DK):
                            at = k * H + (j // 2) * P
                            pair = in_w[left][:, at:at + P], hT_part(right, k, (j % 2) * H, (j % 2 + 1) * H)
                        else:
                            pair = hT_part(left, k, j * P, (j + 1) * P), in_w[right][:, k * H:(k + 1) * H]
                        last = mm(bank(g % 2), *pair, start=(k == left == right == 0), stop=(k == KC - 1 and left == 1))
                    if j == NT - 1 and k % 2 == 1 and k < KC - 1:
                        last.then_inc(in_used, 1)
                last.then_inc(proj_done, 1)

            def turn_rotated(i):
                pe.wait_ge(rot_ready, i + 1)
                if i >= 2:
                    pe.wait_ge(rotT_stored, i - 1)
                src = qrot[:, i % 2] if i < NT else rk[:, i - NT]
                for p in range(PAIRS):
                    last = tr(bank(3 + i % 2)[:, p * P:(p + 1) * P], src[:, p * P:(p + 1) * P], ident)
                last.then_inc(rotT_done, 1)

            turn_x(0)
            turn_x(1)
            for i in range(2 * NT):
                project((RQ, RK)[i // NT], i % NT)
                if i + 2 < NT:
                    turn_x(i + 2)
                if i >= 1:
                    turn_rotated(i - 1)
                if i == NT + 4:
                    modulation(6)
            for t in range(NT):
                project(RV, t)
                if t == 0:
                    turn_rotated(2 * NT - 1)
                if t == 4:
                    modulation(7)
            pe.wait_ge(rotT_stored, 2 * NT)
            for n in range(NT):
                wait_nonzero(pe, rp_ready, n)
                here = slice(n * P, (n + 1) * P)
                for p in range(PAIRS):
                    for r in range(2):
                        rows = slice(r * DH, (r + 1) * DH)
                        last = mm(bank(3 + r)[:, p * P:(p + 1) * P], rkT[rows, p, here], rqT[rows, p, here],
                                  start=True, stop=True)
                last.then_inc(rs_done, 1)
                project(RG, n)
                if n == 4:
                    modulation(8)
                if n >= 1:
                    pe.wait_ge(ro_free, n)
                    pe.wait_ge(state_ready, n)
                    for p in range(PAIRS):
                        mm(bank(5)[:, p * P:(p + 1) * P], rqT[:, p, here], state[:, p], start=(p == 0), stop=False)
                pe.wait_ge(rp_ready, n + 1)
                for p in range(PAIRS):
                    for r in range(2):
                        h = slice((2 * p + r) * DH, (2 * p + r + 1) * DH)
                        last = mm(bank(5)[:, h], pm[:, r, p], vs[:, n, h], start=(n == 0),
                                  stop=(n == 0 or 2 * p + r == RET_H - 1))
                last.then_inc(ro_done, 1)
                if n < NT - 1:
                    for p in range(PAIRS):
                        last = mm(bank(7)[:, p * P:(p + 1) * P], rk[:, n, p * P:(p + 1) * P], vs[:, n, p * P:(p + 1) * P],
                                  start=True, stop=True)
                    last.then_inc(kv_done, 1)
            for b, ada in ((DV, 9), (DQ, 10), (DK, 11)):
                for j in range(NT):
                    project(b, j)
                    if j == 4:
                        modulation(ada)
            modulation(4)
            pe.wait_ge(proj_free[0], 7 * NT // 2)
            pe.wait_ge(proj_free[1], 7 * NT // 2)

            pe.wait_ge(dq_zeroed, 2)

            def scores(i, q):
                qb, h = i // DIFF_H, i % DIFF_H
                wait_nonzero(pe, exp_done[q], i)
                for a in range(0, keys(qb), H):
                    n = min(H, keys(qb) - a)
                    diagonal = a + n == keys(qb)
                    mm(bank(2 * q + a // H)[:, 0:n], dqT[q][:, h, qb * P:(qb + 1) * P], dkT[:, h, a:a + n],
                       start=True, stop=not diagonal)
                mm(bank(2 * q + a // H)[:, n - P:n], ident, const("neg_mask"), start=False, stop=True
                   ).then_inc(s_done[q], 1)

            def turn_probs(i):
                qb = i // DIFF_H
                pe.wait_ge(a_ready, i + 1)
                wait_nonzero(pe, aT_stored, i)
                for kb in range(qb + 1):
                    last = tr(bank2(4)[:, kb * P:(kb + 1) * P], probs[:, i % 2, 0, kb * P:(kb + 1) * P], ident)
                last.then_inc(aT_done, 1)

            def times_v(i):
                qb, h = i // DIFF_H, i % DIFF_H
                pe.wait_ge(aT_stored, i + 1)
                if h == 0:
                    wait_nonzero(pe, av_free, qb)
                for kb in range(qb + 1):
                    last = mm(bank(6)[:, h * P:(h + 1) * P], aT[:, i % 2, kb * P:(kb + 1) * P],
                              dv[:, kb, h * P:(h + 1) * P], start=(kb == 0), stop=(kb == qb))
                last.then_inc(av_done, 1)

            for i in range(NT * DIFF_H + 2):
                if i >= 2:
                    turn_probs(i - 2)
                if i < NT * DIFF_H:
                    scores(i, 0)
                if i >= 2:
                    times_v(i - 2)
                if i < NT * DIFF_H:
                    scores(i, 1)
                if i == 7:
                    modulation(5)

            def turn_mixed(t):
                pe.wait_ge(mix_ready, t + 1)
                wait_nonzero(pe, mixT_stored, t)
                for k in range(KC):
                    src = ret_out if k < 4 else dif_out
                    last = tr(bank(k // 4)[:, (k % 4) * P:(k % 4 + 1) * P], src[:, t, (k % 4) * P:(k % 4 + 1) * P], ident)
                last.then_inc(mixT_done, 1)

            def project_out(t, half):
                place, uses = place_use("out", half)
                if t == 0:
                    pe.wait_ge(place_loaded[place], 16 * uses)
                if half == 0:
                    pe.wait_ge(mixT_stored, t + 1)
                    wait_nonzero(pe, o_free, t)
                for k in range(KC):
                    last = mm(bank(2 + half), mixT[t % 2][:, k], places[place][:, k, :], start=(k == 0), stop=(k == KC - 1))
                if half == 1:
                    last.then_inc(o_done, 1)

            def turn_z(t):
                pe.wait_ge(z_ready, t + 1)
                wait_nonzero(pe, h2_act, t)
                wait_nonzero(pe, h2_dve, t)
                for k in range(KC):
                    last = tr(bank(4 + k // 4)[:, (k % 4) * P:(k % 4 + 1) * P], z[:, t % 2, k * P:(k + 1) * P], ident)
                last.then_inc(zT_done, 1)

            def logits(t):
                pe.wait_ge(h2_act, t + 1)
                pe.wait_ge(h2_dve, t + 1)
                for k in range(KC):
                    last = mm(bank(7)[:, t * NE:(t + 1) * NE], h2T[:, k], rw[:, k], start=(k == 0), stop=(k == KC - 1))
                last.then_inc(logits_done, 1)

            pe.wait_ge(exp_done[0], NT * DIFF_H)
            pe.wait_ge(exp_done[1], NT * DIFF_H)
            pe.wait_ge(mod_stored, len(ADA_ORDER))
            turn_mixed(0)
            for t in range(NT + 2):
                if t < NT:
                    project_out(t, 0)
                if t + 1 < NT:
                    turn_mixed(t + 1)
                if t >= 2:
                    turn_z(t - 2)
                if t < NT:
                    project_out(t, 1)
                if t >= 2:
                    logits(t - 2)
            pe.wait_ge(mask_ready, 1)
            mm(bank(0)[:, 0:NT * NE], const("before"), r_mask, start=True, stop=True)
            mm(bank(1)[:, 0:NT * NE], ones[:], r_mask, start=True, stop=True).then_inc(count_done, 1)

            pe.wait_ge(in_first_ready, 1)
            for t in range(NT):
                last = mm(bank(2)[:, 0:1], in_first[:, t], const("token_no")[:, t:t + 1], start=(t == 0), stop=(t == NT - 1))
            last.then_inc(first_done, 1)

            def turn_gathered():
                for k in range(KC):
                    last = tr(bank2(2)[:, k * P:(k + 1) * P], xg[:, k * P:(k + 1) * P], ident)
                last.then_inc(xgT_done, 1)

            def rows_times(out_bank, right, before_step):
                for k in range(KC):
                    before_step(k)
                    here, cols_k = slice(k * P, (k + 1) * P), slice(k * H, (k + 1) * H)
                    mm(out_bank, hg_parts[0][:, here], right[0][:, cols_k], start=(k == 0), stop=False)
                    mm(out_bank, hg_parts[0][:, here], right[1][:, cols_k], start=False, stop=False)
                    last = mm(out_bank, hg_parts[1][:, here], right[0][:, cols_k], start=False, stop=(k == KC - 1))
                return last

            def expert_tile(g, q, first=None, i=None):
                def weights_split(j):
                    def wait(k):
                        if first is not None and k % 2 == 0:
                            pe.wait_ge(lo_ready, split_count(i, q, j, k // 2 + 1))
                    return wait

                pe.wait_ge(hg_stored, g + 1)
                pe.wait_ge(silu_done, g + 1)
                rows_times(bank(0), gate_w[q], weights_split(0)).then_inc(gate_done, 1)
                pe.wait_ge(he_ready, g * 2 + 2)
                rows_times(bank(1), up_w, weights_split(1)).then_inc(up_done, 1)
                pe.wait_ge(gathered, g * 16 + 32)
                turn_gathered()
                for r in range(2):
                    pe.wait_ge(he_ready, g * 2 + (3 + r))
                    pe.wait_ge(heT_stored, g * 2 + (1 + r))
                    for k in range(2):
                        last = tr(bank((4, 7)[r])[:, k * P:(k + 1) * P], he[:, (2 * r + k) * P:(2 * r + k + 1) * P], ident)
                    last.then_inc(heT_done, 1)
                if first is not None:
                    pe.wait_ge(lo_ready, split_count(i, q, 2, QUARTERS))
                pe.wait_ge(y_stored, g + 1)
                for r in range(2):
                    for left, rights in ((0, (0, 1)), (1, (0,))):
                        if left == 0:
                            pe.wait_ge(heT_hi_ready, g * 2 + (1 + r))
                        else:
                            pe.wait_ge(heT_stored, g * 2 + (3 + r))
                        for k in (2 * r, 2 * r + 1):
                            for half in range(2):
                                for right in rights:
                                    last = mm(bank(5 + half), heT_parts[left][:, k * P:(k + 1) * P],
                                              down_w[right][:, k * D + half * H:k * D + (half + 1) * H],
                                              start=(k == 0 and left == right == 0), stop=(k == FK - 1 and left == 1))
                last.then_inc(y_done, 1)

            pe.wait_ge(o_free, NT)
            pe.wait_ge(av_free, NT)
            for buffer_free in (xgT_done, up_done, y_done):
                pe.sem_inc(buffer_free, 1)
            pe.sem_inc(heT_done, 2)
            pe.wait_ge(gathered, 16)
            turn_gathered()
            pe.wait_ge(slots_ready, 1)
            with pe.Fori(0, NE // 2) as i:
                for q in range(2):
                    first = pe.value_load(ts_i[0:1, bass.ds(i * 2 + q, 1)], min_val=0, max_val=MAX_TILES - 1)
                    end = pe.value_load(ts_i[0:1, bass.ds(i * 2 + (q + 1), 1)], min_val=1, max_val=MAX_TILES)
                    expert_tile(first, q, first, i)
                    with pe.If(first + 1 < end):
                        with pe.Fori(first + 1, end) as g:
                            expert_tile(g, q)


def table_of_constants():
    import numpy as np

    p = np.arange(P)
    inv = (np.float32(1.0) / np.float32(10000.0) ** (np.arange(0, DH, 2, dtype=np.float32) / np.float32(DH))).astype(np.float32)
    angle = (np.arange(S, dtype=np.float32)[:, None] * inv[None, :]).astype(np.float32).astype(np.float64)
    gamma = 1.0 - 2.0 ** (-5.0 - np.arange(RET_H))
    by_tile = lambda a: a.reshape(NT, P, 32).transpose(1, 0, 2).reshape(P, NT * 32)
    pair_head = 2 * np.arange(PAIRS)[None, :] + (p // DH)[:, None]
    parts = {
        "ident": np.eye(P),
        "causal": p[:, None] <= p[None, :],
        "neg_mask": np.where(p[None, :] <= p[:, None], 0.0, NEG),
        "before": p[:, None] < p[None, :],
        "cos": by_tile(np.cos(angle)),
        "sin": by_tile(np.sin(angle)),
        "v_decay": gamma[None, :] ** -(p[:, None] + 1.0),
        "q_decay": gamma[None, :] ** (p[:, None] + 1.0) * DH ** -0.5,
        "chunk_decay": gamma[pair_head] ** float(P),
        "lower": np.tile((np.arange(EPG)[None, :] < np.arange(EPG)[:, None]).reshape(1, -1), (P, 1)),
        "slot_no": np.tile(np.arange(1, P + 1)[None, :], (P, 1)),
        "token_no": np.arange(S).reshape(NT, P).T,
        "steps": np.tile(P * np.arange(1, NT)[None, :], (P, 1)),
    }
    return np.ascontiguousarray(np.concatenate([np.asarray(parts[n], np.float32) for n, _ in CONST_PARTS], axis=1))


_INS = ["x", "c", "w_ada", "b_ada", "w_in", "w_out", "lambda_q1", "lambda_k1", "lambda_q2", "lambda_k2", "diff_subln",
        "ln_mix_g", "ln_mix_b", "ln_ffn_g", "ln_ffn_b", "router_w", "router_b", "w_gate", "w_up", "w_down"]


def kernel(**inputs):
    import numpy as np
    import concourse.bacc as bacc
    from concourse.bass_utils import run_bass_kernel_spmd

    nc = bacc.Bacc("TRN2", target_bir_lowering=False, num_devices=1)
    arrays, args = {}, []
    tables = {"consts": table_of_constants(),
              "token_ids": np.ascontiguousarray(np.arange(S, dtype=np.int32).reshape(NT, P).T)}
    for name in _INS + ["consts", "token_ids"]:
        a = np.ascontiguousarray(inputs[name] if name in inputs else tables[name])
        arrays[f"in_{name}"] = a
        args.append(nc.dram_tensor(f"in_{name}", a.shape, mybir.dt.from_np(a.dtype), kind="ExternalInput").ap())
    out = nc.dram_tensor("out", (1, S, D), mybir.dt.float32, kind="ExternalOutput").ap()
    build(nc, *args, out)
    r = run_bass_kernel_spmd(nc, [arrays], core_ids=[0])
    return r.results[0]["out"]
```
